# Optimizing a Trainium2 kernel written in Bass

```python
import math
import jax, jax.numpy as jnp
from jax import lax
import numpy as np
import jax
import jax.numpy as jnp

D_MODEL = 1024
BATCH = 1
SEQ = 512
DEPTH = 2

D_RNN = 1024
RNN_BLOCKS = 16
RNN_BLOCK = D_RNN // RNN_BLOCKS
CONV_WIDTH = 4
LRU_C = 8.0
N_HEADS = 16
QK_NOPE = 64
QK_ROPE = 32
V_HEAD = 64
Q_LORA = 384
KV_LORA = 256
ROPE_THETA = 10000.0
Q_BLOCK = 128
D_MIX = N_HEADS * V_HEAD
IN_WIDTH = 2 * D_RNN + Q_LORA + KV_LORA + QK_ROPE + 2 * D_MIX
D_FF = 3 * D_MODEL
FFN_CONV_WIDTH = 3
ALPHA = (2 * DEPTH) ** 0.25
BETA = (8 * DEPTH) ** -0.25
EPS = 1e-6
NEG_INF = -1e30


def _split_points():
    sizes = (D_RNN, D_RNN, Q_LORA, KV_LORA, QK_ROPE, D_MIX, D_MIX)
    pts, acc = [], 0
    for s in sizes[:-1]:
        acc += s
        pts.append(acc)
    return pts

def layer_norm(x, g, b):
    xf = x.astype(jnp.float32)
    mu = xf.mean(-1, keepdims=True)
    var = jnp.square(xf - mu).mean(-1, keepdims=True)
    y = (xf - mu) * lax.rsqrt(var + EPS) * g.astype(jnp.float32) + b.astype(jnp.float32)
    return y.astype(x.dtype)

def rms_norm(x, g):
    xf = x.astype(jnp.float32)
    y = xf * lax.rsqrt(jnp.mean(xf * xf, -1, keepdims=True) + EPS) * g.astype(jnp.float32)
    return y.astype(x.dtype)

def causal_dwconv(x, w, b):
    width, c = w.shape
    y = lax.conv_general_dilated(
        x, w[:, None, :].astype(x.dtype), window_strides=(1,), padding=[(width - 1, 0)],
        dimension_numbers=("NWC", "WIO", "NWC"), feature_group_count=c)
    return y + b.astype(x.dtype)

def rope_tables(positions, dtype):
    inv_freq = ROPE_THETA ** (-jnp.arange(0, QK_ROPE, 2, dtype=jnp.float32) / QK_ROPE)
    ang = positions.astype(jnp.float32)[..., None] * inv_freq
    return jnp.cos(ang)[:, :, None, :].astype(dtype), jnp.sin(ang)[:, :, None, :].astype(dtype)

def apply_rope(x, cos, sin):
    x1, x2 = jnp.split(x, 2, axis=-1)
    return jnp.concatenate([x1 * cos - x2 * sin, x2 * cos + x1 * sin], axis=-1)

def rg_lru(x, gx_w, gx_b, ga_w, ga_b, lru_lambda):
    B, S, _ = x.shape
    xb = x.reshape(B, S, RNN_BLOCKS, RNN_BLOCK)
    gate_x = jax.nn.sigmoid(jnp.einsum("bshi,hij->bshj", xb, gx_w).reshape(B, S, D_RNN) + gx_b)
    gate_a = jax.nn.sigmoid(jnp.einsum("bshi,hij->bshj", xb, ga_w).reshape(B, S, D_RNN) + ga_b)
    log_a = -LRU_C * gate_a.astype(jnp.float32) * jax.nn.softplus(-lru_lambda.astype(jnp.float32))
    a = jnp.exp(log_a)
    mult = jnp.sqrt(-jnp.expm1(2.0 * log_a))
    u = mult * (gate_x * x).astype(jnp.float32)

    def step(h, au):
        a_t, u_t = au
        h = a_t * h + u_t
        return h, h

    _, hs = lax.scan(step, jnp.zeros((B, D_RNN), jnp.float32),
                     (jnp.swapaxes(a, 0, 1), jnp.swapaxes(u, 0, 1)))
    return jnp.swapaxes(hs, 0, 1).astype(x.dtype)

def mla_attention(q_lat, kv_lat, k_rope_raw, cos, sin, q_norm_g, w_uq, kv_norm_g, w_ukv):
    B, S, _ = q_lat.shape
    q = (rms_norm(q_lat, q_norm_g) @ w_uq).reshape(B, S, N_HEADS, QK_NOPE + QK_ROPE)
    q_nope, q_pe = q[..., :QK_NOPE], apply_rope(q[..., QK_NOPE:], cos, sin)
    kv = (rms_norm(kv_lat, kv_norm_g) @ w_ukv).reshape(B, S, N_HEADS, QK_NOPE + V_HEAD)
    k_nope, v = kv[..., :QK_NOPE], kv[..., QK_NOPE:]
    k_pe = apply_rope(k_rope_raw[:, :, None, :], cos, sin)[:, :, 0, :]
    scale = (QK_NOPE + QK_ROPE) ** -0.5
    outs = []
    for start in range(0, S, Q_BLOCK):
        end = start + Q_BLOCK
        s = (jnp.einsum("bqhd,bkhd->bhqk", q_nope[:, start:end], k_nope[:, :end])
             + jnp.einsum("bqhd,bkd->bhqk", q_pe[:, start:end], k_pe[:, :end]))
        s = s.astype(jnp.float32) * scale
        causal = (start + jnp.arange(Q_BLOCK))[:, None] >= jnp.arange(end)[None, :]
        p = jax.nn.softmax(jnp.where(causal, s, NEG_INF), axis=-1).astype(v.dtype)
        outs.append(jnp.einsum("bhqk,bkhd->bqhd", p, v[:, :end]))
    return jnp.concatenate(outs, axis=1).reshape(B, S, D_MIX)

def mixer_sublayer(x, cos, sin, w_in, conv_w, conv_b, gx_w, gx_b, ga_w, ga_b, lru_lambda,
                   q_norm_g, w_uq, kv_norm_g, w_ukv, w_out):
    proj = x @ w_in
    x_rnn, g_rnn, q_lat, kv_lat, k_rope, gate_a, gate_b = jnp.split(proj, _split_points(), axis=-1)
    y_rnn = jax.nn.gelu(g_rnn) * rg_lru(causal_dwconv(x_rnn, conv_w, conv_b),
                                        gx_w, gx_b, ga_w, ga_b, lru_lambda)
    y_mla = mla_attention(q_lat, kv_lat, k_rope, cos, sin, q_norm_g, w_uq, kv_norm_g, w_ukv)
    merged = jax.nn.sigmoid(gate_a) * y_rnn + jax.nn.sigmoid(gate_b) * y_mla
    return merged @ w_out

def conv_ffn(x, w_up, ffn_conv_w, ffn_conv_b, w_down):
    h = causal_dwconv(x @ w_up, ffn_conv_w, ffn_conv_b)
    h_gate, h_val = jnp.split(h, 2, axis=-1)
    return (jax.nn.gelu(h_gate) * h_val) @ w_down

def first_inputs(seed: int = 0) -> dict:
    key = jax.random.key(seed)
    ks = jax.random.split(key, 24)
    f32 = jnp.float32

    def nrm(k, shape, scale):
        return jax.random.normal(k, shape, f32) * scale

    x = jax.random.normal(ks[0], (BATCH, SEQ, D_MODEL), f32)
    offsets = jax.random.randint(ks[1], (BATCH, 1), 0, 4096, dtype=jnp.int32)
    positions = (jnp.arange(SEQ, dtype=jnp.int32)[None, :] + offsets).astype(jnp.int32)
    u = jax.random.uniform(ks[2], (DEPTH, D_RNN), f32, 0.9, 0.999)
    a0 = u ** (1.0 / LRU_C)
    lru_lambda = jnp.log(a0) - jnp.log1p(-a0)
    return {
        "x": x,
        "positions": positions,
        "w_in": nrm(ks[3], (DEPTH, D_MODEL, IN_WIDTH), D_MODEL ** -0.5),
        "conv_w": nrm(ks[4], (DEPTH, CONV_WIDTH, D_RNN), CONV_WIDTH ** -0.5),
        "conv_b": nrm(ks[5], (DEPTH, D_RNN), 0.02),
        "gx_w": nrm(ks[6], (DEPTH, RNN_BLOCKS, RNN_BLOCK, RNN_BLOCK), RNN_BLOCK ** -0.5),
        "gx_b": nrm(ks[7], (DEPTH, D_RNN), 0.02),
        "ga_w": nrm(ks[8], (DEPTH, RNN_BLOCKS, RNN_BLOCK, RNN_BLOCK), RNN_BLOCK ** -0.5),
        "ga_b": nrm(ks[9], (DEPTH, D_RNN), 0.02),
        "lru_lambda": lru_lambda,
        "q_norm_g": 1.0 + nrm(ks[10], (DEPTH, Q_LORA), 0.02),
        "w_uq": nrm(ks[11], (DEPTH, Q_LORA, N_HEADS * (QK_NOPE + QK_ROPE)), Q_LORA ** -0.5),
        "kv_norm_g": 1.0 + nrm(ks[12], (DEPTH, KV_LORA), 0.02),
        "w_ukv": nrm(ks[13], (DEPTH, KV_LORA, N_HEADS * (QK_NOPE + V_HEAD)), KV_LORA ** -0.5),
        "w_out": nrm(ks[14], (DEPTH, D_MIX, D_MODEL), BETA * D_MIX ** -0.5),
        "ln1_g": 1.0 + nrm(ks[15], (DEPTH, D_MODEL), 0.02),
        "ln1_b": nrm(ks[16], (DEPTH, D_MODEL), 0.02),
        "w_up": nrm(ks[17], (DEPTH, D_MODEL, 2 * D_FF), D_MODEL ** -0.5),
        "ffn_conv_w": nrm(ks[18], (DEPTH, FFN_CONV_WIDTH, 2 * D_FF), FFN_CONV_WIDTH ** -0.5),
        "ffn_conv_b": nrm(ks[19], (DEPTH, 2 * D_FF), 0.02),
        "w_down": nrm(ks[20], (DEPTH, D_FF, D_MODEL), BETA * D_FF ** -0.5),
        "ln2_g": 1.0 + nrm(ks[21], (DEPTH, D_MODEL), 0.02),
        "ln2_b": nrm(ks[22], (DEPTH, D_MODEL), 0.02),
    }

def first_block(x, positions, w_in, conv_w, conv_b, gx_w, gx_b, ga_w, ga_b, lru_lambda,
              q_norm_g, w_uq, kv_norm_g, w_ukv, w_out, ln1_g, ln1_b,
              w_up, ffn_conv_w, ffn_conv_b, w_down, ln2_g, ln2_b):
    cos, sin = rope_tables(positions, x.dtype)
    for l in range(DEPTH):
        mix = mixer_sublayer(x, cos, sin, w_in[l], conv_w[l], conv_b[l], gx_w[l], gx_b[l],
                             ga_w[l], ga_b[l], lru_lambda[l], q_norm_g[l], w_uq[l],
                             kv_norm_g[l], w_ukv[l], w_out[l])
        x = layer_norm(ALPHA * x + mix, ln1_g[l], ln1_b[l])
        ffn = conv_ffn(x, w_up[l], ffn_conv_w[l], ffn_conv_b[l], w_down[l])
        x = layer_norm(ALPHA * x + ffn, ln2_g[l], ln2_b[l])
    return x


HY_WIDTH = D_MODEL // 4
HY_GROUPS = 4
ATT_WIDTH = D_MODEL // 2
ATT_HEADS = 4
ATT_HEAD_DIM = ATT_WIDTH // (2 * ATT_HEADS)
POOL_WINDOWS = (2, 4, 8, 16)
POOL_WIDTH = D_MODEL - HY_WIDTH - ATT_WIDTH
POOL_GROUP = POOL_WIDTH // len(POOL_WINDOWS)
IN_WIDTH_2 = 3 * HY_WIDTH + 3 * ATT_WIDTH + POOL_WIDTH
ROPE_THETA_2 = 500000.0
ROPE_DIM = ATT_HEAD_DIM // 4
HY_EMB = 33
HY_BANDS = (HY_EMB - 1) // 2
HY_FILTER_HIDDEN = 64
HY_DECAY_TARGET = 1e-2
HY_FAST_DECAY = 0.3
HY_SLOW_DECAY = 1.5
HY_SHIFT = 0.0
N_GROUPS = 4
EXPERTS_PER_GROUP = 4
N_EXPERTS = N_GROUPS * EXPERTS_PER_GROUP
TOP_K_IN_GROUP = 2
D_EXPERT = 256
PLE_DIM = 256
LN_EPS = 1e-5
RMS_EPS = 1e-5
DN_ALPHA = (2 * DEPTH) ** 0.25
DN_BETA = (8 * DEPTH) ** -0.25


def layer_norm_2(x, g, b):
    xf = x.astype(jnp.float32)
    mu = jnp.mean(xf, axis=-1, keepdims=True)
    var = jnp.mean(jnp.square(xf - mu), axis=-1, keepdims=True)
    y = (xf - mu) * lax.rsqrt(var + LN_EPS) * g.astype(jnp.float32) + b.astype(jnp.float32)
    return y.astype(x.dtype)

def rms_norm_2(x, g):
    xf = x.astype(jnp.float32)
    y = xf * lax.rsqrt(jnp.mean(jnp.square(xf), axis=-1, keepdims=True) + RMS_EPS) * g.astype(jnp.float32)
    return y.astype(x.dtype)

def rope_tables_2(seq_len):
    pos = jnp.arange(seq_len, dtype=jnp.float32)
    inv_freq = jnp.power(ROPE_THETA_2, -jnp.arange(0, ROPE_DIM, 2, dtype=jnp.float32) / ROPE_DIM)
    ang = pos[:, None] * inv_freq[None, :]
    ang = jnp.concatenate([ang, ang], axis=-1)
    return jnp.cos(ang), jnp.sin(ang)

def apply_partial_rope(x, cos, sin):
    xf = x.astype(jnp.float32)
    xr, xp = xf[..., :ROPE_DIM], xf[..., ROPE_DIM:]
    half = ROPE_DIM // 2
    rot = jnp.concatenate([-xr[..., half:], xr[..., :half]], axis=-1)
    c = cos[None, :, None, None, :]
    s = sin[None, :, None, None, :]
    return jnp.concatenate([xr * c + rot * s, xp], axis=-1).astype(x.dtype)

def short_conv_centred(u, w, b):
    up = jnp.pad(u, ((0, 0), (1, 1), (0, 0)))
    return up[:, :-2] * w[0] + up[:, 1:-1] * w[1] + up[:, 2:] * w[2] + b

def hyena_filters(seq_len, fw1, fb1, freq1, fw2, fb2, freq2, fw3):
    f32 = jnp.float32
    t = jnp.linspace(0.0, 1.0, seq_len, dtype=f32)[:, None]
    wpos = 2.0 * math.pi * jnp.arange(seq_len, dtype=f32)[:, None] / seq_len
    bands = jnp.linspace(1e-4, HY_BANDS - 1, HY_BANDS, dtype=f32)[None, :]
    z = jnp.concatenate([t, jnp.cos(wpos * bands), -jnp.sin(wpos * bands)], axis=-1)
    hdn = jnp.sin(freq1.astype(f32) * (z @ fw1.astype(f32) + fb1.astype(f32)))
    hdn = jnp.sin(freq2.astype(f32) * (hdn @ fw2.astype(f32) + fb2.astype(f32)))
    filt = hdn @ fw3.astype(f32)
    max_decay = math.log(HY_DECAY_TARGET) / HY_FAST_DECAY
    min_decay = math.log(HY_DECAY_TARGET) / HY_SLOW_DECAY
    deltas = jnp.linspace(min_decay, max_decay, HY_WIDTH, dtype=f32)[None, :]
    window = jnp.exp(-t * jnp.abs(deltas)) + HY_SHIFT
    h_fwd = filt[:, :HY_WIDTH] * window
    h_bwd = filt[:, HY_WIDTH:] * window
    k = jnp.concatenate([h_fwd, jnp.zeros((1, HY_WIDTH), f32), h_bwd[:0:-1]], axis=0)
    return k * lax.rsqrt(jnp.sum(jnp.square(k), axis=0, keepdims=True) + 1e-6)

def hyena_mixer(u, conv_w, conv_b, fw1, fb1, freq1, fw2, fb2, freq2, fw3, bias_d):
    B, L, _ = u.shape
    uc = short_conv_centred(u, conv_w, conv_b)
    x0, x1, v = jnp.split(uc, 3, axis=-1)
    v = (v * x1).astype(jnp.float32)
    k = hyena_filters(L, fw1, fb1, freq1, fw2, fb2, freq2, fw3)
    vf = jnp.fft.rfft(v, n=2 * L, axis=1)
    kf = jnp.fft.rfft(k, axis=0)
    y = jnp.fft.irfft(vf * kf[None], n=2 * L, axis=1)[:, :L]
    y = y + v * bias_d.astype(jnp.float32)
    return (y * x0.astype(jnp.float32)).astype(u.dtype)

def diff_attention(q, k, v, lq1, lk1, lq2, lk2, subln_g, lam_init, cos, sin):
    B, S, _ = q.shape
    q = q.reshape(B, S, ATT_HEADS, 2, ATT_HEAD_DIM)
    k = k.reshape(B, S, ATT_HEADS, 2, ATT_HEAD_DIM)
    v = v.reshape(B, S, ATT_HEADS, 2 * ATT_HEAD_DIM)
    q = apply_partial_rope(q, cos, sin) * (ATT_HEAD_DIM ** -0.5)
    k = apply_partial_rope(k, cos, sin)
    f32 = jnp.float32
    lam = (jnp.exp(jnp.sum(lq1.astype(f32) * lk1.astype(f32)))
           - jnp.exp(jnp.sum(lq2.astype(f32) * lk2.astype(f32))) + lam_init)
    nb = S // Q_BLOCK
    qb = q.reshape(B, nb, Q_BLOCK, ATT_HEADS, 2, ATT_HEAD_DIM).transpose(1, 0, 2, 3, 4, 5)

    def one_block(qblk):
        s = jnp.einsum('bqhcd,bkhcd->bhcqk', qblk, k, preferred_element_type=f32)
        pr = jax.nn.softmax(s, axis=-1)
        a = pr[:, :, 0] - lam * pr[:, :, 1]
        return jnp.einsum('bhqk,bkhe->bqhe', a.astype(v.dtype), v)

    o = lax.map(one_block, qb)
    o = o.transpose(1, 0, 2, 3, 4).reshape(B, S, ATT_HEADS, 2 * ATT_HEAD_DIM)
    o = rms_norm_2(o, subln_g) * (1.0 - lam_init)
    return o.reshape(B, S, ATT_HEADS * 2 * ATT_HEAD_DIM)

def pool_mixer(u, w, b, scale):
    B, S, _ = u.shape
    G = len(POOL_WINDOWS)
    f32 = jnp.float32
    uf = u.astype(f32).reshape(B, S, G, POOL_GROUP)
    csum = jnp.concatenate([jnp.zeros((B, 1, G, POOL_GROUP), f32), jnp.cumsum(uf, axis=1)], axis=1)
    pos = jnp.arange(S)
    pooled = []
    for g, win in enumerate(POOL_WINDOWS):
        lo = jnp.clip(pos - win // 2, 0, S - 1)
        hi = jnp.clip(pos + win // 2 - 1, 0, S - 1)
        cg = csum[:, :, g]
        cnt = (hi - lo + 1).astype(f32)[None, :, None]
        pooled.append((cg[:, hi + 1] - cg[:, lo]) / cnt)
    y = jnp.stack(pooled, axis=2) - uf
    y = jnp.einsum('bsgc,gcd->bsgd', y, w.astype(f32)) + b.astype(f32)
    return (y.reshape(B, S, POOL_WIDTH) * scale.astype(f32)).astype(u.dtype)

def hier_moe(h, wgc, bgc, wgf, bgf, w1, w3, w2):
    B, S, D = h.shape
    f32 = jnp.float32
    t = h.reshape(B * S, D)
    T = t.shape[0]
    pg = jax.nn.softmax(jnp.dot(t, wgc, preferred_element_type=f32) + bgc.astype(f32), axis=-1)
    gw, gi = lax.top_k(pg, 1)
    fl = (jnp.dot(t, wgf, preferred_element_type=f32) + bgf.astype(f32)).reshape(T, N_GROUPS, EXPERTS_PER_GROUP)
    idx = jnp.broadcast_to(gi[:, :, None], (T, 1, EXPERTS_PER_GROUP))
    fs = jnp.take_along_axis(fl, idx, axis=1)[:, 0]
    tv, ti = lax.top_k(jax.nn.softmax(fs, axis=-1), TOP_K_IN_GROUP)
    tv = tv / jnp.sum(tv, axis=-1, keepdims=True)
    eid = gi * EXPERTS_PER_GROUP + ti
    wts = gw * tv
    gates = jnp.sum(jax.nn.one_hot(eid, N_EXPERTS, dtype=f32) * wts[..., None], axis=1)
    a = jnp.einsum('td,edf->tef', t, w1)
    c = jnp.einsum('td,edf->tef', t, w3)
    act = jax.nn.silu(a) * c * gates[:, :, None].astype(t.dtype)
    y = jnp.einsum('tef,efd->td', act, w2)
    return y.reshape(B, S, D)

def second_inputs(seed: int = 0) -> dict:
    key = jax.random.key(seed)
    ks = iter(jax.random.split(key, 48))
    f32 = jnp.float32

    def nrm(shape, scale):
        return scale * jax.random.normal(next(ks), shape, f32)

    def gain(shape):
        return 1.0 + 0.05 * jax.random.normal(next(ks), shape, f32)

    L = DEPTH
    return {
        'x': nrm((BATCH, SEQ, D_MODEL), 1.0),
        'p': nrm((DEPTH, BATCH, SEQ, PLE_DIM), 1.0),
        'ln0_g': gain((D_MODEL,)),
        'ln0_b': nrm((D_MODEL,), 0.02),
        'w_in': nrm((L, D_MODEL, IN_WIDTH_2), D_MODEL ** -0.5),
        'hy_conv_w': nrm((L, 3, 3 * HY_WIDTH), 3 ** -0.5),
        'hy_conv_b': nrm((L, 3 * HY_WIDTH), 0.02),
        'hy_fw1': nrm((L, HY_EMB, HY_FILTER_HIDDEN), HY_EMB ** -0.5),
        'hy_fb1': nrm((L, HY_FILTER_HIDDEN), 0.02),
        'hy_freq1': gain((L, HY_FILTER_HIDDEN)),
        'hy_fw2': nrm((L, HY_FILTER_HIDDEN, HY_FILTER_HIDDEN), HY_FILTER_HIDDEN ** -0.5),
        'hy_fb2': nrm((L, HY_FILTER_HIDDEN), 0.02),
        'hy_freq2': gain((L, HY_FILTER_HIDDEN)),
        'hy_fw3': nrm((L, HY_FILTER_HIDDEN, 2 * HY_WIDTH), HY_FILTER_HIDDEN ** -0.5),
        'hy_bias': nrm((L, HY_WIDTH), 1.0),
        'att_lq1': nrm((L, ATT_HEAD_DIM), 0.1),
        'att_lk1': nrm((L, ATT_HEAD_DIM), 0.1),
        'att_lq2': nrm((L, ATT_HEAD_DIM), 0.1),
        'att_lk2': nrm((L, ATT_HEAD_DIM), 0.1),
        'att_subln_g': gain((L, 2 * ATT_HEAD_DIM)),
        'pool_w': nrm((L, len(POOL_WINDOWS), POOL_GROUP, POOL_GROUP), POOL_GROUP ** -0.5),
        'pool_b': nrm((L, len(POOL_WINDOWS), POOL_GROUP), 0.02),
        'pool_scale': gain((L, POOL_WIDTH)),
        'w_out': nrm((L, D_MODEL, D_MODEL), DN_BETA * D_MODEL ** -0.5),
        'ln1_g': gain((L, D_MODEL)),
        'ln1_b': nrm((L, D_MODEL), 0.02),
        'moe_wgc': nrm((L, D_MODEL, N_GROUPS), D_MODEL ** -0.5),
        'moe_bgc': nrm((L, N_GROUPS), 0.01),
        'moe_wgf': nrm((L, D_MODEL, N_EXPERTS), D_MODEL ** -0.5),
        'moe_bgf': nrm((L, N_EXPERTS), 0.01),
        'moe_w1': nrm((L, N_EXPERTS, D_MODEL, D_EXPERT), D_MODEL ** -0.5),
        'moe_w3': nrm((L, N_EXPERTS, D_MODEL, D_EXPERT), D_MODEL ** -0.5),
        'moe_w2': nrm((L, N_EXPERTS, D_EXPERT, D_MODEL), DN_BETA * D_EXPERT ** -0.5),
        'ple_wg': nrm((L, D_MODEL, D_MODEL), D_MODEL ** -0.5),
        'ple_bg': nrm((L, D_MODEL), 0.02),
        'ple_wp': nrm((L, PLE_DIM, D_MODEL), DN_BETA * PLE_DIM ** -0.5),
        'ln2_g': gain((L, D_MODEL)),
        'ln2_b': nrm((L, D_MODEL), 0.02),
    }

def second_block(x, p, ln0_g, ln0_b, w_in, hy_conv_w, hy_conv_b, hy_fw1, hy_fb1, hy_freq1,
              hy_fw2, hy_fb2, hy_freq2, hy_fw3, hy_bias, att_lq1, att_lk1, att_lq2, att_lk2,
              att_subln_g, pool_w, pool_b, pool_scale, w_out, ln1_g, ln1_b, moe_wgc, moe_bgc,
              moe_wgf, moe_bgf, moe_w1, moe_w3, moe_w2, ple_wg, ple_bg, ple_wp, ln2_g, ln2_b):
    S = x.shape[1]
    h = layer_norm_2(x, ln0_g, ln0_b)
    cos, sin = rope_tables_2(S)
    o_q = 3 * HY_WIDTH
    o_k = o_q + ATT_WIDTH
    o_v = o_k + ATT_WIDTH
    o_p = o_v + ATT_WIDTH
    for i in range(DEPTH):
        lam_init = 0.8 - 0.6 * math.exp(-0.3 * i)
        u = h @ w_in[i]
        y_hy = hyena_mixer(u[..., :o_q], hy_conv_w[i], hy_conv_b[i], hy_fw1[i], hy_fb1[i],
                           hy_freq1[i], hy_fw2[i], hy_fb2[i], hy_freq2[i], hy_fw3[i], hy_bias[i])
        y_att = diff_attention(u[..., o_q:o_k], u[..., o_k:o_v], u[..., o_v:o_p],
                               att_lq1[i], att_lk1[i], att_lq2[i], att_lk2[i], att_subln_g[i],
                               lam_init, cos, sin)
        y_pool = pool_mixer(u[..., o_p:], pool_w[i], pool_b[i], pool_scale[i])
        mix = jnp.concatenate([y_hy, y_att, y_pool], axis=-1) @ w_out[i]
        h = layer_norm_2(DN_ALPHA * h + mix, ln1_g[i], ln1_b[i])
        y_moe = hier_moe(h, moe_wgc[i], moe_bgc[i], moe_wgf[i], moe_bgf[i],
                         moe_w1[i], moe_w3[i], moe_w2[i])
        y_ple = jax.nn.sigmoid(h @ ple_wg[i] + ple_bg[i]) * (p[i] @ ple_wp[i])
        h = layer_norm_2(DN_ALPHA * h + y_moe + y_ple, ln2_g[i], ln2_b[i])
    return h


def setup_inputs(seed=0):
    out = dict(first_inputs(seed))
    for name, value in second_inputs(seed + 1).items():
        if name != "x":
            out[name + "_2"] = value
    return out


def reference(
    x, positions, w_in, conv_w, conv_b, gx_w, gx_b, ga_w, ga_b, lru_lambda, q_norm_g, w_uq,
    kv_norm_g, w_ukv, w_out, ln1_g, ln1_b, w_up, ffn_conv_w, ffn_conv_b, w_down, ln2_g, ln2_b,
    p_2, ln0_g_2, ln0_b_2, w_in_2, hy_conv_w_2, hy_conv_b_2, hy_fw1_2, hy_fb1_2, hy_freq1_2,
    hy_fw2_2, hy_fb2_2, hy_freq2_2, hy_fw3_2, hy_bias_2, att_lq1_2, att_lk1_2, att_lq2_2,
    att_lk2_2, att_subln_g_2, pool_w_2, pool_b_2, pool_scale_2, w_out_2, ln1_g_2, ln1_b_2,
    moe_wgc_2, moe_bgc_2, moe_wgf_2, moe_bgf_2, moe_w1_2, moe_w3_2, moe_w2_2, ple_wg_2,
    ple_bg_2, ple_wp_2, ln2_g_2, ln2_b_2,
):
    x = first_block(
        x, positions, w_in, conv_w, conv_b, gx_w, gx_b, ga_w, ga_b, lru_lambda, q_norm_g, w_uq,
        kv_norm_g, w_ukv, w_out, ln1_g, ln1_b, w_up, ffn_conv_w, ffn_conv_b, w_down, ln2_g,
        ln2_b,
    )
    return second_block(
        x, p_2, ln0_g_2, ln0_b_2, w_in_2, hy_conv_w_2, hy_conv_b_2, hy_fw1_2, hy_fb1_2,
        hy_freq1_2, hy_fw2_2, hy_fb2_2, hy_freq2_2, hy_fw3_2, hy_bias_2, att_lq1_2, att_lk1_2,
        att_lq2_2, att_lk2_2, att_subln_g_2, pool_w_2, pool_b_2, pool_scale_2, w_out_2, ln1_g_2,
        ln1_b_2, moe_wgc_2, moe_bgc_2, moe_wgf_2, moe_bgf_2, moe_w1_2, moe_w3_2, moe_w2_2,
        ple_wg_2, ple_bg_2, ple_wp_2, ln2_g_2, ln2_b_2,
    )


_drawn_inputs = setup_inputs


def setup_inputs(seed=0):
    import zlib

    import numpy as np

    out = dict(_drawn_inputs(seed))
    spreads = {}
    factors = {'gx_b': 8.0,
     'ga_b': 27.099,
     'q_norm_g': 8.0,
     'kv_norm_g': 8.0,
     'ffn_conv_b': 3.672,
     'hy_conv_b_2': 3.948,
     'hy_fb1_2': 6.194,
     'hy_freq1_2': 5.392,
     'hy_fb2_2': 4.656,
     'hy_freq2_2': 5.101,
     'att_lq1_2': 7.924,
     'att_lk1_2': 5.522,
     'att_lk2_2': 11.13,
     'att_subln_g_2': 3.466,
     'pool_b_2': 7.706,
     'pool_scale_2': 4.454,
     'moe_bgc_2': 7.952,
     'moe_bgf_2': 25.298,
     'ple_bg_2': 26.165,
     'att_lq2_2': 4.401}
    for name, (base, spread) in spreads.items():
        noise = np.random.default_rng([zlib.crc32(name.encode()), seed]).standard_normal(out[name].shape)
        drawn = base * np.exp(spread * noise) if base else spread * noise
        out[name] = jnp.asarray(drawn.astype(out[name].dtype))
    for name, factor in factors.items():
        out[name] = (out[name] * factor).astype(out[name].dtype)
    return out
```

```python
from contextlib import ExitStack

import numpy as np

import concourse.bass as bass
from concourse import mybir

F32 = mybir.dt.float32
I32 = mybir.dt.int32
ALU = mybir.AluOpType
ACT = mybir.ActivationFunctionType
AXX = mybir.AxisListType.X
ds = bass.ds

P = 128
S = 512
D = 1024
DEPTH = 2
HEAD = 1
C8 = D // P
ALPHA = float((2 * DEPTH) ** 0.25)

HEADS = 16
NOPE, ROPE, VH = 64, 32, 64
QC, KVC = 3, 2
FF = 3 * D
FC = FF // P
SCALE1 = float((NOPE + ROPE) ** -0.5)
EPS1 = 1e-6
PAIRS = HEADS // 2
R1 = 8
PROJ_UNITS = KVC + 1 + QC + 4 * C8
OUT_UNITS = C8
UP_UNITS = 2 * FC
DOWN_PER = FC // 8
U_OUT = PROJ_UNITS
U_UP = U_OUT + OUT_UNITS
U_DOWN = U_UP + UP_UNITS
U1 = U_DOWN + DOWN_PER * C8

TWO_PI = 6.283185307179586
PI2_A = 6.28125
PI2_B = 0.0019350051879882812
PI2_C = TWO_PI - PI2_A - PI2_B
MAGIC = 12582912.0
PI_DOWN = 3.1415925


def columns(spec):
    at, out = 0, {}
    for name, n in spec:
        out[name] = (at, n)
        at += n
    return out, at


PAR1, NPAR1 = columns([("conv_w", 4 * C8), ("conv_b", C8), ("gx_b", C8), ("ga_b", C8), ("lam", C8),
                       ("q_g", QC), ("kv_g", KVC), ("ln1_g", C8), ("ln1_b", C8), ("ln2_g", C8),
                       ("ln2_b", C8), ("ffw", 3 * 2 * FC), ("ffb", 2 * FC)])
CST, NCST = columns([("ident", P), ("mask", P), ("invf", 1), ("sign", 1)])


class Count:

    def __init__(self, sem):
        self.sem, self.n, self.off = sem, 0, 0

    def inc(self, ins):
        ins.then_inc(self.sem, 1)
        self.n += 1

    def now(self):
        return self.off + self.n

    def step(self, eng, ins):
        self.inc(ins)
        eng.wait_ge(self.sem, self.now())

    def enter(self, i, per):
        self.base, self.off, self.per = self.n, i * per, per

    def leave(self, times):
        assert self.n == self.base + self.per, (self.n, self.base, self.per)
        self.off, self.n = 0, self.base + self.per * times


def sems(nc, ctx, names):
    handles = {n: ctx.enter_context(nc.semaphore(n)) for n in names}
    nums = sorted(h.num for h in handles.values())
    assert nums == list(range(nums[0], nums[0] + len(nums)))
    return handles, range(nums[0], nums[-1] + 1)


def layer_norm_engines(rounds_before, sem, x, sq, ps_mean, ps_var, ones_d, eps, par, g0, b0, stat):
    r = rounds_before

    def tensor(pe, nc):
        for k in range(C8):
            pe.wait_ge(sem["z_ready"], r * C8 + k + 1)
            mm = nc.tensor.matmul(ps_mean, ones_d, x[:, k, :], start=(k == 0), stop=(k == C8 - 1))
        mm.then_inc(sem["mean_mm"], 1)
        for k in range(C8):
            pe.wait_ge(sem["sq_ready"], r * C8 + k + 1)
            mm = nc.tensor.matmul(ps_var, ones_d, sq[:, k, :], start=(k == 0), stop=(k == C8 - 1))
        mm.then_inc(sem["var_mm"], 1)

    def vector(dve, nc):
        dve.wait_ge(sem["mean_mm"], r + 1)
        for k in range(C8):
            nc.vector.tensor_tensor(x[:, k, :], x[:, k, :], ps_mean, ALU.subtract).then_inc(sem["xc_ready"], 1)
        dve.wait_ge(sem["std_ready"], r + 1)
        nc.vector.reciprocal(stat[:, 0, :], stat[:, 1, :]).then_inc(sem["rstd_ready"], 1)
        dve.wait_ge(sem["rstd_ready"], r + 1)
        dve.wait_ge(sem["xc_ready"], r * C8 + C8)
        for k in range(C8):
            nc.vector.tensor_tensor(x[:, k, :], x[:, k, :], stat[:, 0, :], ALU.mult).then_inc(sem["xn_ready"], 1)

    def scalar(act, nc):
        for k in range(C8):
            act.wait_ge(sem["xc_ready"], r * C8 + k + 1)
            nc.scalar.activation(sq[:, k, :], x[:, k, :], ACT.Square).then_inc(sem["sq_ready"], 1)
        act.wait_ge(sem["var_mm"], r + 1)
        nc.scalar.activation(stat[:, 1, :], ps_var, ACT.Sqrt, bias=eps).then_inc(sem["std_ready"], 1)
        for k in range(C8):
            act.wait_ge(sem["xn_ready"], r * C8 + k + 1)
            nc.scalar.activation(x[:, k, :], x[:, k, :], ACT.Identity, scale=par[:, g0 + k:g0 + k + 1],
                                 bias=par[:, b0 + k:b0 + k + 1]).then_inc(sem["x_ready"], 1)

    return tensor, vector, scalar


def reduce_angle(dve, nc, step, r, ang, n):
    step.step(dve, nc.vector.tensor_scalar(n, ang, 1.0 / TWO_PI, MAGIC, ALU.mult, ALU.add))
    step.step(dve, nc.vector.tensor_scalar(n, n, -MAGIC, None, ALU.add))
    step.step(dve, nc.vector.scalar_tensor_tensor(r, n, -PI2_A, ang, ALU.mult, ALU.add))
    step.step(dve, nc.vector.scalar_tensor_tensor(r, n, -PI2_B, r, ALU.mult, ALU.add))
    step.step(dve, nc.vector.scalar_tensor_tensor(r, n, -PI2_C, r, ALU.mult, ALU.add))
    step.step(dve, nc.vector.tensor_scalar(r, r, PI_DOWN, -PI_DOWN, ALU.min, ALU.max))


def first_block(nc, x, ps, d_x, d_pos, d_cst, d_w, d_aw, d_par):
    with ExitStack() as ctx:
        def sb(name, shape, dt=F32):
            return ctx.enter_context(nc.sbuf_tensor(name, shape, dt))

        ring = sb("ring", [P, R1, 8, P])
        aw = sb("aw", [P, 2, 12, P])
        par = sb("par", [P, NPAR1])
        cst = sb("cst", [P, NCST])
        rope = sb("rope", [P, S])
        ones = sb("ones", [P, P])
        ones_d = sb("ones_d", [P, P])
        eps = sb("eps", [P, 1])
        wide = sb("wide", [P, FC, S])
        gate_r, gate_b, rnn_in = wide[:, 0:C8, :], wide[:, C8:2 * C8, :], wide[:, 2 * C8:3 * C8, :]
        lat = sb("lat", [P, KVC + 1 + QC, S])
        kvn, krope, qn = lat[:, 0:KVC, :], lat[:, KVC, :], lat[:, KVC + 1:, :]
        qt = sb("qt", [P, 2, S])
        kt = sb("kt", [P, 2, S])
        rt = sb("rt", [P, 2, S])
        vb = sb("vb", [P, 2, 4, P])
        pb = sb("pb", [P, 4, S])
        pt = sb("pt", [P, 4, S])
        osb = sb("osb", [P, 2, 4, P])
        small = sb("small", [P, 4, 16])
        stat = sb("stat", [P, 2, S])
        sx, sa, th, av, m2 = (sb(n, [P, S]) for n in ("sx", "sa", "th", "av", "m2"))
        lru = sb("lru", [P, 6, C8])
        taps = sb("taps", [P, 2, 2, S])

        names = ([f"w_in{j}" for j in range(R1)] + ["aw_in0", "aw_in1", "par_in", "cst_in", "x_in",
                 "unit_done", "proj_evac", "proj_tap", "lat_sq", "lat_mm", "lat_std", "lat_rstd", "lat_ready",
                 "kpe_ready", "dve_step", "ang_ready", "sin_ready", "abs_ready", "expl_ready", "lru_ready",
                 "q_mm", "k_mm", "v_mm", "qn_ready", "qr_ready", "k_ready", "v_ready", "s_mm", "nmax_ready",
                 "p_ready", "t_mm", "pt_ready", "o_mm", "o_ready", "y_mm", "merged", "conv_ready", "gate_mm",
                 "gate_sig", "a_ready", "m2_ready", "mu_ready", "rnn_done", "gated_r",
                 "z_ready", "mean_mm", "xc_ready", "sq_ready", "var_mm", "std_ready", "rstd_ready", "xn_ready",
                 "x_ready", "ff_tap", "ff_conv", "ff_gelu", "ff_done"])
        sem, sem_range = sems(nc, ctx, names)

        def chunk(t, k):
            return t[:, k, :] if isinstance(k, int) else t[:, ds(k, 1), :]

        def one(t, k):
            return t[:, k:k + 1] if isinstance(k, int) else t[:, ds(k, 1)]

        def col(name, k=0):
            return one(par, k + PAR1[name][0])

        ident = cst[:, CST["ident"][0]:CST["ident"][0] + P]
        mask = cst[:, CST["mask"][0]:CST["mask"][0] + P]

        ln1 = layer_norm_engines(0, sem, x, wide[:, 0:C8, :], ps[:, 4, :], ps[:, 5, :], ones_d[:, :], eps[:, 0:1],
                                 par, PAR1["ln1_g"][0], PAR1["ln1_b"][0], stat)
        ln2 = layer_norm_engines(1, sem, x, wide[:, 0:C8, :], ps[:, 4, :], ps[:, 5, :], ones_d[:, :], eps[:, 0:1],
                                 par, PAR1["ln2_g"][0], PAR1["ln2_b"][0], stat)

        with nc.sbuf_tensor("pos", [P, S], I32) as pos, nc.Block() as block:
            @block.sync
            def _(sp):
                sp.dma_start(pos[:, :], d_pos).then_inc(sem["par_in"], 16)
                sp.dma_start(cst[:, :], d_cst).then_inc(sem["cst_in"], 16)
                sp.dma_start(x[:, :, :], d_x).then_inc(sem["x_in"], 16)
                sp.wait_ge(sem["x_in"], 16)

            @block.gpsimd
            def _(pool):
                nc.gpsimd.memset(ones[:, :], 1.0)
                nc.gpsimd.memset(ones_d[:, :], 1.0 / D)
                nc.gpsimd.memset(eps[:, :], EPS1)

            @block.vector
            def _(dve):
                step = Count(sem["dve_step"])
                fr, sg = CST["invf"][0], CST["sign"][0]
                dve.wait_ge(sem["par_in"], 16)
                dve.wait_ge(sem["cst_in"], 16)
                hi = slice(64, P)
                ang, n, r = pb[hi, 0, :], pb[hi, 1, :], pb[hi, 2, :]
                step.step(dve, nc.vector.tensor_copy(ang, pos[hi, :]))
                step.step(dve, nc.vector.tensor_scalar(ang, ang, cst[hi, fr:fr + 1], None, ALU.mult))
                reduce_angle(dve, nc, step, r, ang, n)
                c = pb[64:96, 2, :]
                step.step(dve, nc.vector.tensor_scalar(pb[64:96, 3, :], c, -1.0, None, ALU.mult))
                step.step(dve, nc.vector.tensor_tensor(c, c, pb[64:96, 3, :], ALU.max))
                nc.vector.tensor_scalar(c, c, -1.0, TWO_PI / 4, ALU.mult, ALU.add).then_inc(sem["ang_ready"], 1)
                dve.wait_ge(sem["sin_ready"], 1)
                nc.vector.tensor_scalar(rope[hi, :], rope[hi, :], cst[hi, sg:sg + 1], None, ALU.mult)

            @block.scalar
            def _(act):
                act.wait_ge(sem["ang_ready"], 1)
                nc.scalar.activation(rope[64:P, :], pb[64:P, 2, :], ACT.Sin).then_inc(sem["sin_ready"], 1)

        nc.all_engine_barrier(sems_to_clear=sem_range)

        with nc.Fori(0, DEPTH) as layer:
            with nc.Block() as block:
                @block.sync
                def _(sp):
                    sp.dma_start(par[:, :], d_par[ds(layer, 1)].rearrange("a p n -> p (a n)")).then_inc(sem["par_in"], 16)

                    def load(slot, unit):
                        sp.dma_start(ring[:, slot], d_w[ds(layer * U1 + unit, 1)].rearrange("a p (k m) -> p (a k) m", m=P)
                                     ).then_inc(sem[f"w_in{slot}"], 16)

                    def load_pair(slot, pair):
                        sp.dma_start(aw[:, slot], d_aw[ds(layer * PAIRS + pair, 1)].rearrange("a p (k m) -> p (a k) m", m=P)
                                     ).then_inc(sem[f"aw_in{slot}"], 16)

                    for j in range(R1):
                        load(j, j)
                    for j in range(2):
                        load_pair(j, j)
                    with sp.Fori(0, PROJ_UNITS // R1) as i:
                        for j in range(R1):
                            sp.wait_ge(sem["unit_done"], i * R1 + j + 1)
                            load(j, i * R1 + j + R1)
                    at = PROJ_UNITS // R1 * R1
                    for u in range(at, PROJ_UNITS):
                        sp.wait_ge(sem["unit_done"], u + 1)
                        load(u % R1, u + R1)
                    with sp.Fori(0, PAIRS // 2 - 1) as i:
                        for j in range(2):
                            sp.wait_ge(sem["q_mm"], i * 4 + 2 * j + 2)
                            sp.wait_ge(sem["k_mm"], i * 4 + 2 * j + 2)
                            sp.wait_ge(sem["v_mm"], i * 2 + j + 1)
                            sp.wait_ge(sem["gate_mm"], i * 4 + 2 * j + 2)
                            load_pair(j, i * 2 + j + 2)
                    at = PROJ_UNITS
                    turns = (U1 - R1 - at) // R1
                    with sp.Fori(0, turns) as i:
                        for j in range(R1):
                            sp.wait_ge(sem["unit_done"], i * R1 + (at + j + 1))
                            load((at + j) % R1, i * R1 + (at + j + R1))
                    for u in range(at + turns * R1, U1 - R1):
                        sp.wait_ge(sem["unit_done"], u + 1)
                        load(u % R1, u + R1)

                @block.tensor
                def _(pe):
                    def unit(rhs, bank, u0, i=0, first=True, last=True):
                        slot = u0 % R1
                        pe.wait_ge(sem[f"w_in{slot}"], i * 16 + (u0 // R1 + 1) * 16)
                        for k in range(8):
                            mm = nc.tensor.matmul(bank, ring[:, slot, k, :], rhs[:, k, :],
                                                  start=(first and k == 0), stop=(last and k == 7))
                        mm.then_inc(sem["unit_done"], 1)

                    for n in ("t_mm", "o_mm"):
                        pe.sem_inc(sem[n], HEAD)
                    head = KVC + 1 + QC
                    for u in range(head):
                        pe.wait_ge(sem["proj_evac"], u + 1)
                        unit(x, ps[:, u % 4, :], u)
                    with pe.Fori(0, 3) as i:
                        for j in range(R1):
                            pe.wait_ge(sem["proj_evac"], i * R1 + (head + j + 1))
                            unit(x, ps[:, (head + j) % 4, :], head + j, i)
                    pe.wait_ge(sem["lat_sq"], KVC + QC)
                    for k in range(KVC):
                        mm = nc.tensor.matmul(ps[:, 4, :], ones[:, :], pb[:, k, :], start=(k == 0), stop=(k == KVC - 1))
                    mm.then_inc(sem["lat_mm"], 1)
                    for k in range(QC):
                        mm = nc.tensor.matmul(ps[:, 5, :], ones[:, :], pt[:, k, :], start=(k == 0), stop=(k == QC - 1))
                    mm.then_inc(sem["lat_mm"], 1)
                    for u in range(head + 3 * R1, PROJ_UNITS):
                        pe.wait_ge(sem["proj_evac"], u + 1)
                        unit(x, ps[:, u % 4, :], u)

                    def project_qk(slot, half):
                        for c in range(QC):
                            mm = nc.tensor.matmul(ps[:, 0, :], aw[:, slot, half * 3 + c, :], qn[:, c, :],
                                                  start=(c == 0), stop=(c == QC - 1))
                        mm.then_inc(sem["q_mm"], 1)
                        for c in range(KVC):
                            mm = nc.tensor.matmul(ps[0:64, 1, :], aw[:, slot, 6 + half, c * 64:c * 64 + 64], kvn[:, c, :],
                                                  start=(c == 0), stop=(c == KVC - 1))
                        mm.then_inc(sem["k_mm"], 1)

                    def project_v(slot):
                        for t in range(4):
                            for c in range(KVC):
                                mm = nc.tensor.matmul(ps[:, 7, t * P:t * P + P], kvn[:, c, t * P:t * P + P],
                                                      aw[:, slot, 8 + c, :], start=(c == 0), stop=(c == KVC - 1))
                        mm.then_inc(sem["v_mm"], 1)

                    def scores(hb, b):
                        n = (b + 1) * P
                        nc.tensor.matmul(ps[:, 2 + b % 2, 0:n], qt[0:96, hb, b * P:b * P + P], kt[0:96, hb, 0:n],
                                         start=True, stop=True).then_inc(sem["s_mm"], 1)

                    def turn(b):
                        for j in range(b + 1):
                            mm = nc.tensor.transpose(ps[:, 4 + b % 2, j * P:j * P + P], pb[:, b, j * P:j * P + P], ident)
                        mm.then_inc(sem["t_mm"], 1)

                    def weigh(pp, hb, b):
                        for j in range(b + 1):
                            mm = nc.tensor.matmul(ps[:, 6, b * 64:b * 64 + 64],
                                                  pt[:, b, j * P:j * P + P], vb[:, pp, j, hb * 64:hb * 64 + 64],
                                                  start=(j == 0), stop=(j == b))
                        mm.then_inc(sem["o_mm"], 1)

                    def turn_out(pp):
                        for b in range(4):
                            mm = nc.tensor.transpose(ps[:, 7, b * P:b * P + P], osb[:, pp, b, :], ident)
                        mm.then_inc(sem["y_mm"], 1)

                    pe.wait_ge(sem["lat_ready"], KVC + QC)
                    pe.wait_ge(sem["proj_evac"], PROJ_UNITS + 4)
                    pe.wait_ge(sem["aw_in0"], 16)
                    project_qk(0, 0)
                    project_v(0)
                    pe.wait_ge(sem["kpe_ready"], 2)

                    def four_heads(i, last):
                        for hh in range(4):
                            pp, hb = hh // 2, hh % 2
                            h4, h, p = i * 16 + hh * 4, i * 4 + hh, i * 2 + pp
                            nxt = 1 - pp if hb else pp
                            pe.wait_ge(sem["qn_ready"], h + 1)
                            pe.wait_ge(sem["qr_ready"], h + 1)
                            pe.wait_ge(sem["k_ready"], h + 1)
                            pe.wait_ge(sem["p_ready"], HEAD + h4)
                            scores(hb, 0)
                            scores(hb, 1)
                            if not (last and hh == 3):
                                pe.wait_ge(sem["gate_sig"], HEAD + p * 2 + 2 * hb)
                                if hb == 1:
                                    pe.wait_ge(sem[f"aw_in{1 - pp}"], i * 16 + pp * 16 + 16)
                                project_qk(nxt, 1 - hb)
                                if hb == 1:
                                    pe.wait_ge(sem["merged"], HEAD + p)
                                    project_v(nxt)
                            pe.wait_ge(sem["pt_ready"], HEAD + h4)
                            pe.wait_ge(sem["p_ready"], HEAD + h4 + 1)
                            turn(0)
                            scores(hb, 2)
                            pe.wait_ge(sem["p_ready"], HEAD + h4 + 2)
                            turn(1)
                            scores(hb, 3)
                            pe.wait_ge(sem["v_ready"], p + 1)
                            pe.wait_ge(sem["o_ready"], HEAD + h)
                            pe.wait_ge(sem["pt_ready"], HEAD + h4 + 1)
                            weigh(pp, hb, 0)
                            pe.wait_ge(sem["pt_ready"], HEAD + h4 + 2)
                            weigh(pp, hb, 1)
                            if hb == 0:
                                pe.wait_ge(sem["qn_ready"], h + 2)
                                pe.wait_ge(sem["qr_ready"], h + 2)
                                pe.wait_ge(sem["k_ready"], h + 2)
                                for g in range(2):
                                    nc.tensor.matmul(ps[:, g, :], aw[:, pp, 10 + g, :], chunk(rnn_in, p),
                                                     start=True, stop=True).then_inc(sem["gate_mm"], 1)
                            pe.wait_ge(sem["p_ready"], HEAD + h4 + 3)
                            turn(2)
                            pe.wait_ge(sem["p_ready"], HEAD + h4 + 4)
                            turn(3)
                            pe.wait_ge(sem["pt_ready"], HEAD + h4 + 3)
                            weigh(pp, hb, 2)
                            pe.wait_ge(sem["pt_ready"], HEAD + h4 + 4)
                            weigh(pp, hb, 3)
                            if hb == 1:
                                if not (last and hh == 3):
                                    pe.wait_ge(sem["v_ready"], p + 2)
                                else:
                                    pe.wait_ge(sem["merged"], HEAD + p)
                                pe.wait_ge(sem["o_ready"], HEAD + h + 1)
                                turn_out(pp)

                    with pe.Fori(0, PAIRS // 2 - 1) as i:
                        four_heads(i, False)
                    four_heads(PAIRS // 2 - 1, True)

                    pe.wait_ge(sem["merged"], HEAD + PAIRS)
                    for m in range(C8):
                        if m >= 4:
                            pe.wait_ge(sem["z_ready"], m - 3)
                        unit(gate_b, ps[:, m % 4, :], U_OUT + m)
                    ln1[0](pe, nc)

                    pe.wait_ge(sem["x_ready"], C8)
                    with pe.Fori(0, FC // 4) as i:
                        for j in range(4):
                            pe.wait_ge(sem["ff_conv"], i * 4 + j + 1)
                            for half in range(2):
                                unit(x, ps[:, 2 * j + half, :], U_UP + 2 * j + half, i)
                    pe.wait_ge(sem["ff_done"], HEAD + FC)
                    for m in range(C8):
                        if m >= 4:
                            pe.wait_ge(sem["z_ready"], C8 + m - 3)
                        for q in range(DOWN_PER):
                            unit(wide[:, q * 8:q * 8 + 8, :], ps[:, m % 4, :], U_DOWN + m * DOWN_PER + q, 0,
                                 q == 0, q == DOWN_PER - 1)
                    ln2[0](pe, nc)

                @block.scalar
                def _(act):
                    for n in ("p_ready", "pt_ready", "gate_sig"):
                        act.sem_inc(sem[n], HEAD)
                    act.sem_inc(sem["proj_evac"], 4)
                    for u in range(KVC + 1 + QC):
                        act.wait_ge(sem["unit_done"], u + 1)
                        nc.scalar.activation(lat[:, u, :], ps[:, u % 4, :], ACT.Copy).then_inc(sem["proj_evac"], 1)
                    act.wait_ge(sem["proj_evac"], 4 + KVC + 1 + QC)
                    for k in range(KVC):
                        nc.scalar.activation(pb[:, k, :], kvn[:, k, :], ACT.Square).then_inc(sem["lat_sq"], 1)
                    for k in range(QC):
                        nc.scalar.activation(pt[:, k, :], qn[:, k, :], ACT.Square).then_inc(sem["lat_sq"], 1)
                    act.wait_ge(sem["par_in"], 16)
                    u0 = KVC + 1 + QC
                    with act.Fori(0, 2) as i:
                        for j in range(4):
                            act.wait_ge(sem["unit_done"], i * 4 + (u0 + j + 1))
                            nc.scalar.activation(chunk(rnn_in, i * 4 + j), ps[:, (u0 + j) % 4, :], ACT.Identity,
                                                 scale=col("conv_w", i * 4 + (3 * C8 + j)), bias=col("conv_b", i * 4 + j)
                                                 ).then_inc(sem["proj_tap"], 1)
                            act.wait_ge(sem["conv_ready"], i * 4 + j + 1)
                            act.sem_inc(sem["proj_evac"], 1)
                    u0 += C8
                    with act.Fori(0, 2) as i:
                        for j in range(4):
                            act.wait_ge(sem["unit_done"], i * 4 + (u0 + j + 1))
                            nc.scalar.activation(chunk(gate_r, i * 4 + j), ps[:, (u0 + j) % 4, :],
                                                 ACT.Gelu_apprx_tanh).then_inc(sem["proj_evac"], 1)
                    u0 += C8
                    act.wait_ge(sem["abs_ready"], 1)
                    nc.scalar.activation(lru[:, 1, :], lru[:, 0, :], ACT.Exp, scale=-1.0).then_inc(sem["expl_ready"], 1)
                    with act.Fori(0, 4) as i:
                        for j in range(2):
                            act.wait_ge(sem["unit_done"], i * 2 + (u0 + j + 1))
                            if j == 0:
                                act.wait_ge(sem["gated_r"], HEAD + i * 2)
                            bank = ps[:, ds((i * 2 + (u0 + j)) % 4, 1), :]
                            nc.scalar.activation(taps[:, 0, j:j + 1, :], bank, ACT.Sigmoid).then_inc(sem["proj_evac"], 1)
                    u0 += C8
                    for m in range(C8):
                        if m == 4:
                            for n, (bank, width) in enumerate(((4, KVC * P), (5, QC * P))):
                                act.wait_ge(sem["lat_mm"], n + 1)
                                nc.scalar.activation(stat[:, n, :], ps[:, bank, :], ACT.Sqrt, scale=1.0 / width,
                                                     bias=eps[:, 0:1]).then_inc(sem["lat_std"], 1)
                        act.wait_ge(sem["unit_done"], u0 + m + 1)
                        nc.scalar.activation(gate_b[:, m, :], ps[:, (u0 + m) % 4, :], ACT.Sigmoid
                                             ).then_inc(sem["proj_evac"], 1)

                    def evac_qk(h, buf):
                        act.wait_ge(sem["q_mm"], h + 1)
                        nc.scalar.activation(qt[0:64, buf, :], ps[0:64, 0, :], ACT.Copy).then_inc(sem["qn_ready"], 1)
                        act.wait_ge(sem["k_mm"], h + 1)
                        nc.scalar.activation(kt[0:64, buf, :], ps[0:64, 1, :], ACT.Copy).then_inc(sem["k_ready"], 1)

                    def evac_v(p, pp):
                        act.wait_ge(sem["v_mm"], p + 1)
                        nc.scalar.activation(vb[:, pp, :, :], ps[:, 7, :].rearrange("p (a b) -> p a b", b=P), ACT.Copy
                                             ).then_inc(sem["v_ready"], 1)

                    def expo(hh, h4, b):
                        act.wait_ge(sem["nmax_ready"], h4 + b + 1)
                        c = hh * 4 + b
                        nc.scalar.activation(pb[:, b, 0:(b + 1) * P], ps[:, 2 + b % 2, 0:(b + 1) * P], ACT.Exp,
                                             scale=SCALE1, bias=small[:, 1, c:c + 1], accum_out=small[:, 2, c:c + 1]
                                             ).then_inc(sem["p_ready"], 1)

                    def evac_pt(h4, b):
                        act.wait_ge(sem["t_mm"], HEAD + h4 + b + 1)
                        nc.scalar.activation(pt[:, b, 0:(b + 1) * P], ps[:, 4 + b % 2, 0:(b + 1) * P], ACT.Copy
                                             ).then_inc(sem["pt_ready"], 1)

                    evac_qk(0, 0)
                    evac_v(0, 0)

                    def four_heads(i, last):
                        for hh in range(4):
                            pp, hb = hh // 2, hh % 2
                            h4, h, p = i * 16 + hh * 4, i * 4 + hh, i * 2 + pp
                            act.wait_ge(sem["t_mm"], HEAD + h4)
                            expo(hh, h4, 0)
                            expo(hh, h4, 1)
                            if not (last and hh == 3):
                                evac_qk(h + 1, 1 - hb)
                                if hb == 1:
                                    evac_v(p + 1, 1 - pp)
                            if hb == 1:
                                act.wait_ge(sem["m2_ready"], p + 1)
                                nc.scalar.activation(m2[:, :], m2[:, :], ACT.Sqrt, scale=2.0).then_inc(sem["mu_ready"], 1)
                            act.wait_ge(sem["o_mm"], HEAD + h4)
                            evac_pt(h4, 0)
                            evac_pt(h4, 1)
                            expo(hh, h4, 2)
                            expo(hh, h4, 3)
                            if hb == 0:
                                act.wait_ge(sem["rnn_done"], HEAD + p)
                                for g, (name, out) in enumerate((("gx_b", sx), ("ga_b", sa))):
                                    act.wait_ge(sem["gate_mm"], p * 2 + g + 1)
                                    nc.scalar.activation(out[:, :], ps[:, g, :], ACT.Sigmoid, bias=col(name, p)
                                                         ).then_inc(sem["gate_sig"], 1)
                                act.wait_ge(sem["gate_sig"], HEAD + p * 2 + 2)
                                act.wait_ge(sem["lru_ready"], 1)
                                nc.scalar.activation(th[:, :], sa[:, :], ACT.Tanh, scale=one(lru[:, 4, :], p)
                                                     ).then_inc(sem["a_ready"], 1)
                                nc.scalar.activation(av[:, :], sa[:, :], ACT.Exp, scale=one(lru[:, 5, :], p)
                                                     ).then_inc(sem["a_ready"], 1)
                            evac_pt(h4, 2)
                            evac_pt(h4, 3)

                    with act.Fori(0, PAIRS // 2 - 1) as i:
                        four_heads(i, False)
                    four_heads(PAIRS // 2 - 1, True)

                    ln1[2](act, nc)
                    with act.Fori(0, FC // 4) as i:
                        for j in range(4):
                            f = i * 4 + j
                            act.wait_ge(sem["ff_done"], HEAD + (f - 1 if j else f))
                            for half in range(2):
                                act.wait_ge(sem["unit_done"], f * 2 + (U_UP + half + 1))
                                nc.scalar.activation(taps[:, j % 2, half, :], ps[:, 2 * j + half, :], ACT.Identity,
                                                     scale=col("ffw", f + (2 * 2 * FC + half * FC)),
                                                     bias=col("ffb", f + half * FC)).then_inc(sem["ff_tap"], 1)
                            act.wait_ge(sem["ff_conv"], f + 5)
                            nc.scalar.activation(taps[:, j % 2, 0, :], taps[:, j % 2, 0, :], ACT.Gelu_apprx_tanh
                                                 ).then_inc(sem["ff_gelu"], 1)
                    ln2[2](act, nc)

                @block.vector
                def _(dve):
                    step = Count(sem["dve_step"])
                    V = nc.vector
                    dve.sem_inc(sem["ff_conv"], 4)
                    for n in ("merged", "o_ready", "gated_r", "rnn_done", "ff_done"):
                        dve.sem_inc(sem[n], HEAD)
                    dve.wait_ge(sem["proj_evac"], 4 + KVC + 1)
                    step.step(dve, V.tensor_tensor(rt[64:96, 0, :], krope[96:P, :], rope[96:P, :], ALU.mult))
                    step.step(dve, V.tensor_tensor(rt[64:96, 1, :], krope[64:96, :], rope[64:96, :], ALU.mult))
                    for n in range(2):
                        V.tensor_tensor(kt[64:96, n, :], rt[64:96, 0, :], rt[64:96, 1, :], ALU.add
                                        ).then_inc(sem["kpe_ready"], 1)
                    dve.wait_ge(sem["par_in"], 16)
                    lam = par[:, PAR1["lam"][0]:PAR1["lam"][0] + C8]
                    L = [lru[:, n, :] for n in range(6)]
                    step.step(dve, V.tensor_scalar(L[2], lam, -1.0, None, ALU.mult))
                    V.tensor_tensor(L[0], L[2], lam, ALU.max).then_inc(sem["abs_ready"], 1)

                    u0 = KVC + 1 + QC
                    with dve.Fori(0, 2) as i:
                        step.enter(i, 8)
                        for j in range(4):
                            m, bank = i * 4 + j, ps[:, (u0 + j) % 4, :]
                            dve.wait_ge(sem["proj_tap"], i * 4 + j + 1)
                            for s in (1, 2, 3):
                                out = rnn_in[:, ds(m, 1), s:]
                                ins = V.scalar_tensor_tensor(out, bank[:, 0:S - s], col("conv_w", i * 4 + (j + (3 - s) * C8)),
                                                             out, ALU.mult, ALU.add)
                                if s < 3:
                                    step.step(dve, ins)
                                else:
                                    ins.then_inc(sem["conv_ready"], 1)
                        step.leave(2)

                    dve.wait_ge(sem["expl_ready"], 1)
                    z, t, s2 = L[1], L[3], L[0]
                    step.step(dve, V.tensor_scalar(t, z, 2.0, None, ALU.add))
                    step.step(dve, V.reciprocal(t, t))
                    step.step(dve, V.tensor_tensor(t, z, t, ALU.mult))
                    step.step(dve, V.tensor_tensor(s2, t, t, ALU.mult))
                    acc = L[4]
                    step.step(dve, V.tensor_scalar(acc, s2, 1.0 / 15, None, ALU.mult))
                    for n in (13, 11, 9, 7, 5, 3):
                        step.step(dve, V.scalar_tensor_tensor(acc, acc, 1.0 / n, s2, ALU.add, ALU.mult))
                    step.step(dve, V.scalar_tensor_tensor(acc, acc, 1.0, t, ALU.add, ALU.mult))
                    step.step(dve, V.tensor_scalar(L[2], L[2], 0.0, None, ALU.max))
                    step.step(dve, V.scalar_tensor_tensor(acc, acc, 2.0, L[2], ALU.mult, ALU.add))
                    step.step(dve, V.tensor_scalar(L[5], acc, -8.0, None, ALU.mult))
                    V.tensor_scalar(acc, acc, 8.0, None, ALU.mult).then_inc(sem["lru_ready"], 1)

                    u0 += 2 * C8
                    with dve.Fori(0, 4) as i:
                        for j in range(2):
                            dve.wait_ge(sem["proj_evac"], i * 2 + (u0 + j + 5))
                            g = chunk(gate_r, i * 2 + j)
                            V.tensor_tensor(g, g, taps[:, 0, j:j + 1, :], ALU.mult).then_inc(sem["gated_r"], 1)

                    for n, (t, name, width) in enumerate(((kvn, "kv_g", KVC), (qn, "q_g", QC))):
                        dve.wait_ge(sem["lat_std"], n + 1)
                        V.reciprocal(stat[:, n, :], stat[:, n, :]).then_inc(sem["lat_rstd"], 1)
                        dve.wait_ge(sem["lat_rstd"], n + 1)
                        for k in range(width):
                            V.scalar_tensor_tensor(t[:, k, :], t[:, k, :], col(name, k), stat[:, n, :], ALU.mult, ALU.mult
                                                   ).then_inc(sem["lat_ready"], 1)

                    def rotate_q(h, buf):
                        dve.wait_ge(sem["q_mm"], h + 1)
                        step.step(dve, V.tensor_tensor(rt[64:96, buf, :], ps[96:P, 0, :], rope[96:P, :], ALU.mult))
                        step.step(dve, V.tensor_tensor(qt[64:96, buf, :], ps[64:96, 0, :], rope[64:96, :], ALU.mult))
                        V.tensor_tensor(qt[64:96, buf, :], qt[64:96, buf, :], rt[64:96, buf, :], ALU.add
                                        ).then_inc(sem["qr_ready"], 1)

                    def row_max(hh, h4, b):
                        dve.wait_ge(sem["s_mm"], h4 + b + 1)
                        bank, c = ps[:, 2 + b % 2, :], hh * 4 + b
                        own = bank[:, b * P:b * P + P]
                        step.step(dve, V.tensor_tensor(own, own, mask, ALU.add))
                        step.step(dve, V.reduce_max(small[:, 0, c:c + 1], bank[:, 0:(b + 1) * P], AXX))
                        V.tensor_scalar(small[:, 1, c:c + 1], small[:, 0, c:c + 1], -SCALE1, None, ALU.mult
                                        ).then_inc(sem["nmax_ready"], 1)

                    def normalise_out(hh, h):
                        pp, hb, c = hh // 2, hh % 2, hh * 4
                        dve.wait_ge(sem["o_mm"], HEAD + h * 4 + 4)
                        step.step(dve, V.reciprocal(small[:, 3, c:c + 4], small[:, 2, c:c + 4]))
                        V.tensor_tensor(osb[:, pp, :, hb * 64:hb * 64 + 64],
                                        ps[:, 6, 0:256].rearrange("p (b e) -> p b e", b=4),
                                        small[:, 3, c:c + 4].unsqueeze(2).to_broadcast([P, 4, 64]), ALU.mult
                                        ).then_inc(sem["o_ready"], 1)

                    rotate_q(0, 0)

                    def four_heads(i, last):
                        for hh in range(4):
                            pp, hb = hh // 2, hh % 2
                            h4, h, p = i * 16 + hh * 4, i * 4 + hh, i * 2 + pp
                            row_max(hh, h4, 0)
                            row_max(hh, h4, 1)
                            if not (last and hh == 3):
                                rotate_q(h + 1, 1 - hb)
                            row_max(hh, h4, 2)
                            row_max(hh, h4, 3)
                            normalise_out(hh, h)
                            if hb == 0:
                                dve.wait_ge(sem["a_ready"], p * 2 + 1)
                                step.step(dve, V.tensor_scalar(m2[:, :], th[:, :], 1.0, None, ALU.add))
                                step.step(dve, V.reciprocal(m2[:, :], m2[:, :]))
                                V.tensor_tensor(m2[:, :], th[:, :], m2[:, :], ALU.mult).then_inc(sem["m2_ready"], 1)
                            else:
                                dve.wait_ge(sem["mu_ready"], p + 1)
                                step.step(dve, V.tensor_tensor(sx[:, :], sx[:, :], chunk(rnn_in, p)[:, 0, :]
                                                               if not isinstance(p, int) else rnn_in[:, p, :], ALU.mult))
                                step.step(dve, V.tensor_tensor(sx[:, :], sx[:, :], m2[:, :], ALU.mult))
                                dve.wait_ge(sem["a_ready"], p * 2 + 2)
                                step.step(dve, V.tensor_tensor_scan(sa[:, :], av[:, :], sx[:, :], 0.0, ALU.mult, ALU.add))
                                g = chunk(gate_r, p)
                                V.tensor_tensor(g, g, sa[:, :], ALU.mult).then_inc(sem["rnn_done"], 1)
                                dve.wait_ge(sem["y_mm"], p + 1)
                                dve.wait_ge(sem["rnn_done"], HEAD + p + 1)
                                g2 = chunk(gate_b, p)
                                step.step(dve, V.tensor_tensor(g2, g2, ps[:, 7, :], ALU.mult))
                                V.tensor_tensor(g2, g2, g, ALU.add).then_inc(sem["merged"], 1)

                    per = 4 * (2 + 8 + 1) + 2 * 2 + 2 * 4
                    with dve.Fori(0, PAIRS // 2 - 1) as i:
                        step.enter(i, per)
                        four_heads(i, False)
                        step.leave(PAIRS // 2 - 1)
                    four_heads(PAIRS // 2 - 1, True)

                    def residual(u0, z0, per_tile):
                        for m in range(C8):
                            dve.wait_ge(sem["unit_done"], u0 + (m + 1) * per_tile)
                            V.scalar_tensor_tensor(x[:, m, :], x[:, m, :], ALPHA, ps[:, m % 4, :], ALU.mult, ALU.add
                                                   ).then_inc(sem["z_ready"], 1)

                    residual(U_OUT, 0, 1)
                    dve.wait_ge(sem["z_ready"], C8)
                    ln1[1](dve, nc)
                    with dve.Fori(0, FC // 4) as i:
                        step.enter(i, 4 * 3)
                        for j in range(4):
                            f = i * 4 + j
                            for half in range(2):
                                dve.wait_ge(sem["ff_tap"], f * 2 + half + 1)
                                for s in (1, 2):
                                    out = taps[:, j % 2, half, s:]
                                    ins = V.scalar_tensor_tensor(
                                        out, ps[:, 2 * j + half, 0:S - s], col("ffw", f + ((2 - s) * 2 * FC + half * FC)),
                                        out, ALU.mult, ALU.add)
                                    if half == 1 and s == 2:
                                        ins.then_inc(sem["ff_conv"], 1)
                                    else:
                                        step.step(dve, ins)
                            dve.wait_ge(sem["ff_gelu"], f + 1)
                            dve.wait_ge(sem["ff_conv"], f + 5)
                            V.tensor_tensor(chunk(wide, f), taps[:, j % 2, 0:1, :], taps[:, j % 2, 1:2, :], ALU.mult
                                            ).then_inc(sem["ff_done"], 1)
                        step.leave(FC // 4)
                    residual(U_DOWN, C8, DOWN_PER)
                    dve.wait_ge(sem["z_ready"], 2 * C8)
                    ln2[1](dve, nc)

            nc.all_engine_barrier(sems_to_clear=sem_range)


HW, AW, PW = D // 4, D // 2, D // 4
AHEADS = 4
HYC, AC, PC = HW // P, AW // P, PW // P
LN_EPS = 1e-5
FH = 64
FEMB = 33
EXPERTS, GROUPS, DE = 16, 4, 256
EC = DE // P
PLE = 256
R2 = 8
NF = S // P
V_HY = 0
V_QK = V_HY + 3 * HYC
V_V = V_QK + 2 * AC
V_POOL = V_V + AC
V_DFT = V_POOL + PC
V_IDFT = V_DFT + NF
V_OUT = V_IDFT + NF
V_PLEG = V_OUT + C8
V_PLEP = V_PLEG + C8
V_EXP = V_PLEP + 2
V_DOWN = V_EXP + 2 * EC * EXPERTS
U2 = V_DOWN + C8 * (EXPERTS * EC // 8)

PAR2, NPAR2 = columns([("hw", 9 * HYC), ("hb", 3 * HYC), ("fb1", 1), ("fr1", 1), ("fb2", 1), ("fr2", 1),
                       ("bias", HYC), ("lq1", 1), ("lq2", 1), ("lk1", 1), ("lk2", 1), ("lam0", 1), ("lam1", 1),
                       ("sub_g", 1), ("pool_b", PC), ("pool_s", PC), ("ln1_g", C8), ("ln1_b", C8), ("ln2_g", C8),
                       ("ln2_b", C8), ("ple_b", C8), ("rbias", 20), ("fw1", FH), ("fw2", FH), ("fw3", 2 * HW),
                       ("poolw", PC * P), ("router", C8 * 20)])
CST2, NCST2 = columns([("ident", P), ("perm", P), ("z", S), ("cos", S), ("sin", S), ("win", 4 * HW),
                       ("icnt", PC * S), ("ln0_g", C8), ("ln0_b", C8)])
PADW = 8


def second_block(nc, x, ps, d_cst, d_w, d_par, d_p):
    with ExitStack() as ctx:
        def sb(name, shape, dt=F32):
            return ctx.enter_context(nc.sbuf_tensor(name, shape, dt))

        ring = sb("ring2", [P, R2, 8, P])
        par = sb("par2", [P, NPAR2])
        cst = sb("cst2", [P, NCST2])
        ones = sb("ones2", [P, P])
        ones_d = sb("ones_d2", [P, P])
        eps = sb("eps2", [P, 2])
        wide = sb("wide2", [P, EXPERTS * EC, S])
        hy = wide[:, 0:6, :]
        qk = wide[:, 6:14, :]
        v4 = wide[:, 14:18, :]
        mix = wide[:, 18:26, :]
        rhs3 = wide[:, 26:32, :].rearrange("p a b -> p (a b)").rearrange("p (t c) -> p t c", c=3 * HW)
        flat3 = wide[:, 26:32, :].rearrange("p a b -> p (a b)")
        spec = sb("spec", [P, 8, S])
        ys = flat3[:, 0:8 * HW].rearrange("p (f c) -> p f c", c=HW)
        ytmp = flat3[:, 8 * HW:12 * HW].rearrange("p (f c) -> p f c", c=HW)
        pexp = sb("pexp", [P, 2, 2, S])
        filt = pexp[:, :, :, :].rearrange("p a b c -> p (a b c)").rearrange("p (t w c) -> p t w c", w=2, c=HW)
        at = sb("at", [P, 2, S])
        osb = sb("osb2", [P, 2, 4, P])
        small = sb("small2", [P, 2, 12])
        headv = sb("headv", [P, 2, 12])
        stat = sb("stat2", [P, 2, S])
        hid = sb("hid", [P, 2, S])
        tmp = sb("tmp2", [P, 2, S])
        pool = sb("pool", [P, 2, S + 2 * PADW])
        pacc = sb("pacc", [P, 2, S + 2 * PADW])
        pw = sb("pw", [P, 2, S + 2 * PADW])
        lamt = sb("lamt", [P, 8])
        rtr = sb("rtr", [P, 12, 4, 20])
        gT = sb("gT", [EXPERTS, S])
        gm = sb("gm", [EXPERTS, 2, S])
        pT = sb("pT", [P, 2, S])

        names = ([f"v_in{j}" for j in range(R2)] + ["par_in2", "cst_in2", "p_in", "unit_done2", "proj_evac2", "hy_tap",
                 "hy_ready", "hy_v", "f1_mm", "ang1", "sin1", "f2_mm", "ang2", "sin2", "filt_mm", "kf_done", "sqk", "norm_mm",
                 "nstd", "nrs", "rot_mm", "qk_ready", "v_ready2", "pool_in", "pool_zero", "pool_step", "pool_y", "poolm_mm",
                 "pool_done", "vt_mm", "vt_ready", "dft_mm", "spec_evac", "ys_ready", "idft_mm", "hy_done", "lam_prod",
                 "lam_mm", "lam_exp", "lam_ready", "s_mm2", "nmax2", "p_ready2", "a_ready2", "t_mm2", "at_ready", "o_mm2",
                 "o_sc", "o_sq", "o_std", "o_nrm", "ot_mm", "att_done", "dve_step2", "act_step2",
                 "route_mm", "r_a", "r_ea", "r_b", "r_eb", "r_c", "r_ec", "gates", "gt_mm", "gt_ready", "gm_ready",
                 "g_mm", "silu", "ex_done", "pg_sig", "pp_done",
                 "z_ready", "mean_mm", "xc_ready", "sq_ready", "var_mm", "std_ready", "rstd_ready", "xn_ready",
                 "x_ready"])
        sem, sem_range = sems(nc, ctx, names)

        def chunk(t, k):
            return t[:, k, :] if isinstance(k, int) else t[:, ds(k, 1), :]

        def col(name, k=0, n=1, rows=P):
            at_ = PAR2[name][0] + k
            return par[0:rows, at_:at_ + n]

        def con(name, k=0, n=None):
            at_, w = CST2[name]
            return cst[:, at_ + k:at_ + k + (w if n is None else n)]

        ident = con("ident")
        args = (sem, x, wide[:, 0:C8, :], ps[:, 4, :], ps[:, 5, :], ones_d[:, :], eps[:, 0:1])
        ln0 = layer_norm_engines(0, *args, cst, CST2["ln0_g"][0], CST2["ln0_b"][0], stat)
        ln1 = layer_norm_engines(0, *args, par, PAR2["ln1_g"][0], PAR2["ln1_b"][0], stat)
        ln2 = layer_norm_engines(1, *args, par, PAR2["ln2_g"][0], PAR2["ln2_b"][0], stat)

        with nc.Block() as block:
            @block.sync
            def _(sp):
                sp.dma_start(cst[:, :], d_cst).then_inc(sem["cst_in2"], 16)
                sp.wait_ge(sem["cst_in2"], 16)

            @block.gpsimd
            def _(g):
                nc.gpsimd.memset(ones[:, :], 1.0)
                nc.gpsimd.memset(eps[:, 0:1], LN_EPS)
                nc.gpsimd.memset(eps[:, 1:2], 1e-6)
                nc.gpsimd.memset(pool[:, :, :], 0.0)
                nc.gpsimd.memset(ones_d[:, :], 1.0 / D)

        nc.all_engine_barrier(sems_to_clear=sem_range)
        with nc.Block() as block:
            @block.tensor
            def _(pe):
                ln0[0](pe, nc)

            @block.scalar
            def _(act):
                ln0[2](act, nc)

            @block.vector
            def _(dve):
                dve.sem_inc(sem["z_ready"], C8)
                ln0[1](dve, nc)

        nc.all_engine_barrier(sems_to_clear=sem_range)

        with nc.Fori(0, DEPTH) as layer:
            with nc.Block() as block:
                @block.sync
                def _(sp):
                    sp.dma_start(par[:, :], d_par[ds(layer, 1)].rearrange("a p n -> p (a n)")).then_inc(sem["par_in2"], 16)

                    def load(slot, unit):
                        sp.dma_start(ring[:, slot], d_w[ds(layer * U2 + unit, 1)].rearrange("a p (k m) -> p (a k) m", m=P)
                                     ).then_inc(sem[f"v_in{slot}"], 16)

                    for j in range(R2):
                        load(j, j)
                    sp.dma_start(pT[:, :, :], d_p[ds(layer, 1)].rearrange("a p k t -> p (a k) t")).then_inc(sem["p_in"], 16)
                    turns = (U2 - R2) // R2
                    with sp.Fori(0, turns) as i:
                        for j in range(R2):
                            sp.wait_ge(sem["unit_done2"], i * R2 + (j + 1))
                            load(j, i * R2 + (j + R2))
                    for u in range(turns * R2, U2 - R2):
                        sp.wait_ge(sem["unit_done2"], u + 1)
                        load(u % R2, u + R2)

                @block.tensor
                def _(pe):
                    T = nc.tensor

                    def loaded(u0, i=0):
                        pe.wait_ge(sem[f"v_in{u0 % R2}"], i * 16 + (u0 // R2 + 1) * 16)

                    def unit(rhs, bank, u0, i=0, first=True, last=True):
                        loaded(u0, i)
                        for k in range(8):
                            mm = T.matmul(bank, ring[:, u0 % R2, k, :], rhs[:, k, :],
                                          start=(first and k == 0), stop=(last and k == 7))
                        mm.then_inc(sem["unit_done2"], 1)

                    pe.sem_inc(sem["g_mm"], HEAD)
                    pe.wait_ge(sem["par_in2"], 16)
                    T.matmul(ps[0:FH, 6, :], col("fw1", 0, FH, FEMB), cst[0:FEMB, CST2["z"][0]:CST2["z"][0] + S],
                             start=True, stop=True).then_inc(sem["f1_mm"], 1)
                    pe.wait_ge(sem["lam_prod"], 1)
                    T.matmul(ps[:, 7, 0:2], ones[:, :], lamt[:, 0:2], start=True, stop=True).then_inc(sem["lam_mm"], 1)
                    for u in range(V_QK):
                        pe.wait_ge(sem["proj_evac2"], u + 1)
                        unit(x, ps[:, u % 4, :], u)
                    pe.wait_ge(sem["sin1"], 1)
                    pe.wait_ge(sem["lam_exp"], 1)
                    T.matmul(ps[0:FH, 7, :], col("fw2", 0, FH, FH), hid[0:FH, 0, :], start=True, stop=True
                             ).then_inc(sem["f2_mm"], 1)

                    def rotate(n):
                        pe.wait_ge(sem["proj_evac2"], 4 + V_QK + n + 1)
                        if n >= 2:
                            pe.wait_ge(sem["qk_ready"], n - 1)
                        T.matmul(ps[:, 4 + n % 2, :], con("perm"), qk[:, n, :], start=True, stop=True
                                 ).then_inc(sem["rot_mm"], 1)

                    for n in range(2 * AC):
                        u = V_QK + n
                        pe.wait_ge(sem["proj_evac2"], u + 1)
                        unit(x, ps[:, u % 4, :], u)
                        if n:
                            rotate(n - 1)
                    pe.wait_ge(sem["proj_evac2"], 4 + V_V)
                    for q in range(AC):
                        loaded(V_V + q)
                        for kk in range(2):
                            k = 2 * q + kk
                            w = ring[:, (V_V + q) % R2, kk * 4:kk * 4 + 4, :].rearrange("p a b -> p (a b)")
                            for t in range(4):
                                mm = T.matmul(ps[:, t, :], x[:, k, t * P:t * P + P], w, start=(k == 0), stop=(k == 7),
                                              skip_group_check=True)
                        mm.then_inc(sem["unit_done2"], 1)
                        if q == 0:
                            rotate(2 * AC - 1)
                    pe.wait_ge(sem["sin2"], 1)
                    pe.wait_ge(sem["qk_ready"], 2 * AC)
                    for t in range(4):
                        T.matmul(ps[:, 4 + t, :], hid[0:FH, 1, t * P:t * P + P], col("fw3", 0, 2 * HW, FH),
                                 start=True, stop=True).then_inc(sem["filt_mm"], 1)
                    pe.wait_ge(sem["kf_done"], 4)
                    for n in range(PC):
                        unit(x, ps[:, 4 + n, :], V_POOL + n)
                    pe.wait_ge(sem["hy_v"], HYC)
                    for c in range(HYC):
                        for t in range(4):
                            mm = T.transpose(ps[:, 6 + c, t * P:t * P + P], hy[:, 4 + c, t * P:t * P + P], ident)
                        mm.then_inc(sem["vt_mm"], 1)
                    pe.wait_ge(sem["v_ready2"], 4)
                    pe.wait_ge(sem["vt_ready"], HYC)
                    for n in range(2 * NF):
                        if n % 2 == 0:
                            loaded(V_DFT + n // 2)
                        if n >= 4:
                            pe.wait_ge(sem["spec_evac"], n - 3)
                        for t in range(4):
                            mm = T.matmul(ps[:, n % 4, :], ring[:, (V_DFT + n // 2) % R2, (n % 2) * 4 + t, :],
                                          rhs3[:, t, 0:2 * HW] if n < NF else rhs3[:, t, HW:3 * HW],
                                          start=(t == 0), stop=(t == 3))
                        mm.then_inc(sem["dft_mm" if n % 2 == 0 else "unit_done2"], 1)
                    pe.wait_ge(sem["sqk"], 1)
                    for c in range(HYC):
                        for t in range(4):
                            for w in range(2):
                                mm = T.matmul(ps[:, 6, c:c + 1], filt[:, t, w, c * P:c * P + P], ones[:, 0:1],
                                              start=(t + w == 0), stop=(t == 3 and w == 1), skip_group_check=True)
                    mm.then_inc(sem["norm_mm"], 1)
                    pe.wait_ge(sem["pool_y"], PC)
                    pe.wait_ge(sem["pool_in"], PC)
                    for n in range(PC):
                        T.matmul(ps[:, 4 + n, :], col("poolw", n * P, P), pacc[:, n, 0:S], start=True, stop=True
                                 ).then_inc(sem["poolm_mm"], 1)

                    pe.wait_ge(sem["spec_evac"], 2 * NF)
                    pe.wait_ge(sem["pool_done"], PC)
                    pe.wait_ge(sem["nstd"], 1)

                    def scores(n):
                        h, b = n // 4, n % 4
                        if n >= 2:
                            pe.wait_ge(sem["p_ready2"], 2 * (n - 1))
                        for c in range(2):
                            lo = slice(64 * c, 64 * c + 64)
                            T.matmul(ps[:, 2 * (n % 2) + c, :], qk[lo, h, b * P:b * P + P], qk[lo, AC + h, :],
                                     start=True, stop=True).then_inc(sem["s_mm2"], 1)

                    def turn(n):
                        pe.wait_ge(sem["a_ready2"], n + 1)
                        if n >= 2:
                            pe.wait_ge(sem["at_ready"], n - 1)
                        for j in range(4):
                            mm = T.transpose(ps[:, 4 + n % 2, j * P:j * P + P], pexp[:, n % 2, 0, j * P:j * P + P], ident)
                        mm.then_inc(sem["t_mm2"], 1)

                    def weigh(n):
                        h = n // 4
                        pe.wait_ge(sem["at_ready"], n + 1)
                        pe.wait_ge(sem["o_sc"], n)
                        for j in range(4):
                            mm = T.matmul(ps[:, 6, 0:P], at[:, n % 2, j * P:j * P + P], v4[:, j, h * P:h * P + P],
                                          start=(j == 0), stop=(j == 3))
                        mm.then_inc(sem["o_mm2"], 1)

                    def turn_out(h):
                        pe.wait_ge(sem["o_nrm"], h + 1)
                        pe.wait_ge(sem["att_done"], h)
                        for b in range(4):
                            mm = T.transpose(ps[:, 7, b * P:b * P + P], osb[:, h % 2, b, :], ident)
                        mm.then_inc(sem["ot_mm"], 1)

                    scores(0)
                    for n in range(4 * AHEADS):
                        if n + 1 < 4 * AHEADS:
                            scores(n + 1)
                        turn(n)
                        if n:
                            weigh(n - 1)
                        if n >= 6 and n % 4 == 2:
                            turn_out((n - 6) // 4)
                    weigh(4 * AHEADS - 1)
                    pe.wait_ge(sem["ys_ready"], 1)
                    pe.wait_ge(sem["p_ready2"], 8 * AHEADS)
                    for q in range(NF):
                        loaded(V_IDFT + q)
                        for kk in range(2):
                            f = 2 * q + kk
                            w = ring[:, (V_IDFT + q) % R2, kk * 4:kk * 4 + 4, :].rearrange("p a b -> p (a b)")
                            for c in range(HYC):
                                mm = T.matmul(ps[:, c, :], ys[:, f, c * P:c * P + P], w, start=(f == 0), stop=(f == 7),
                                              skip_group_check=True)
                        mm.then_inc(sem["unit_done2"], 1)
                    turn_out(AHEADS - 1)

                    pe.wait_ge(sem["hy_done"], HYC)
                    pe.wait_ge(sem["pool_done"], PC)
                    pe.wait_ge(sem["att_done"], AHEADS)
                    for m in range(C8):
                        if m >= 4:
                            pe.wait_ge(sem["z_ready"], m - 3)
                        unit(mix, ps[:, m % 4, :], V_OUT + m)
                    ln1[0](pe, nc)

                    pe.wait_ge(sem["x_ready"], C8)
                    for t in range(4):
                        for k in range(C8):
                            mm = T.matmul(ps[:, 6, t * 20:t * 20 + 20], x[:, k, t * P:t * P + P], col("router", k * 20, 20),
                                          start=(k == 0), stop=(k == C8 - 1))
                    mm.then_inc(sem["route_mm"], 1)
                    for m in range(C8):
                        if m >= 4:
                            pe.wait_ge(sem["pg_sig"], m - 3)
                        unit(x, ps[:, m % 4, :], V_PLEG + m)
                    pe.wait_ge(sem["p_in"], 16)
                    for m in range(C8):
                        if m % 4 == 0:
                            loaded(V_PLEP + m // 4)
                        if m < 4:
                            pe.wait_ge(sem["pg_sig"], C8)
                        else:
                            pe.wait_ge(sem["pp_done"], m - 3)
                        for k in range(2):
                            mm = T.matmul(ps[:, m % 4, :], ring[:, (V_PLEP + m // 4) % R2, (m % 4) * 2 + k, :], pT[:, k, :],
                                          start=(k == 0), stop=(k == 1))
                        mm.then_inc(sem["unit_done2" if m % 4 == 3 else "dft_mm"], 1)
                    pe.wait_ge(sem["gates"], 1)
                    for t in range(4):
                        mm = T.transpose(ps[0:EXPERTS, 7, t * P:t * P + P], rtr[:, 11, t, 0:16], ident)
                    mm.then_inc(sem["gt_mm"], 1)
                    pe.wait_ge(sem["pp_done"], C8)
                    with pe.Fori(0, EXPERTS // 2) as i:
                        for e in range(2):
                            for f in range(EC):
                                pe.wait_ge(sem["ex_done"], i * 4 + 2 * e + f + 1)
                                for half in range(2):
                                    unit(x, ps[:, 2 * f + half, :], V_EXP + 4 * e + 2 * f + half, i)
                                if f == 0:
                                    pe.wait_ge(sem["gm_ready"], i * 2 + e + 1)
                                    T.matmul(ps[:, 4 + e, :], ones[0:EXPERTS, :], gm[:, e, :], start=True, stop=True
                                             ).then_inc(sem["g_mm"], 1)
                    pe.wait_ge(sem["ex_done"], 2 * EXPERTS + 2)
                    per = EXPERTS * EC // 8
                    with pe.Fori(0, C8 // 2) as i:
                        for m in range(2):
                            pe.wait_ge(sem["z_ready"], i * 2 + (C8 + m - 1 if m else C8))
                            for q in range(per):
                                unit(wide[:, q * 8:q * 8 + 8, :], ps[:, m, :], V_DOWN + m * per + q, i, q == 0, q == per - 1)
                    ln2[0](pe, nc)

                @block.scalar
                def _(act):
                    A = nc.scalar.activation
                    act.sem_inc(sem["proj_evac2"], 4)
                    act.wait_ge(sem["par_in2"], 16)

                    def hy_tile(u):
                        act.wait_ge(sem["unit_done2"], u + 1)
                        A(hy[:, u, :], ps[:, u % 4, :], ACT.Identity, scale=col("hw", 3 * HYC + u), bias=col("hb", u)
                          ).then_inc(sem["hy_tap"], 1)
                        act.wait_ge(sem["hy_ready"], u + 1)
                        act.sem_inc(sem["proj_evac2"], 1)

                    def filter_sin(n):
                        act.wait_ge(sem[f"ang{n + 1}"], 1)
                        A(hid[0:FH, n, :], hid[0:FH, n, :], ACT.Sin).then_inc(sem[f"sin{n + 1}"], 1)

                    hy_tile(0)
                    hy_tile(1)
                    filter_sin(0)
                    for u in range(2, V_QK):
                        hy_tile(u)
                    act.wait_ge(sem["lam_mm"], 1)
                    A(lamt[:, 2:4], ps[:, 7, 0:2], ACT.Exp).then_inc(sem["lam_exp"], 1)
                    for n in range(2 * AC):
                        u = V_QK + n
                        act.wait_ge(sem["unit_done2"], u + 1)
                        A(qk[:, n, :], ps[:, u % 4, :], ACT.Copy).then_inc(sem["proj_evac2"], 1)
                        if n == 4:
                            filter_sin(1)
                    act.wait_ge(sem["unit_done2"], V_POOL)
                    for t in range(4):
                        A(v4[:, t, :], ps[:, t, :], ACT.Copy).then_inc(sem["v_ready2"], 1)
                    for n in range(PC):
                        act.wait_ge(sem["unit_done2"], V_POOL + n + 1)
                        A(pool[:, n, PADW:PADW + S], ps[:, 4 + n, :], ACT.Copy).then_inc(sem["pool_in"], 1)
                    act.wait_ge(sem["kf_done"], 8)
                    A(pexp[:, :, :, :], pexp[:, :, :, :], ACT.Square).then_inc(sem["sqk"], 1)
                    for n in range(2 * NF):
                        if n % 2:
                            act.wait_ge(sem["unit_done2"], V_DFT + n // 2 + 1)
                        else:
                            act.wait_ge(sem["dft_mm"], n // 2 + 1)
                        A(spec[:, n, :], ps[:, n % 4, :], ACT.Copy).then_inc(sem["spec_evac"], 1)
                    act.wait_ge(sem["norm_mm"], 1)
                    A(lamt[:, 6:8], ps[:, 6, 0:2], ACT.Sqrt, bias=eps[:, 1:2]).then_inc(sem["nstd"], 1)

                    def expo(n):
                        for c in range(2):
                            act.wait_ge(sem["nmax2"], 2 * n + c + 1)
                            if n >= 2:
                                act.wait_ge(sem["t_mm2"], n - 1)
                            A(pexp[:, n % 2, c, :], ps[:, 2 * (n % 2) + c, :], ACT.Exp, scale=0.125,
                              bias=small[:, n % 2, 2 + c:3 + c], accum_out=small[:, n % 2, 4 + c:5 + c]
                              ).then_inc(sem["p_ready2"], 1)

                    def evac_at(n):
                        act.wait_ge(sem["t_mm2"], n + 1)
                        if n >= 2:
                            act.wait_ge(sem["o_mm2"], n - 1)
                        A(at[:, n % 2, :], ps[:, 4 + n % 2, :], ACT.Copy).then_inc(sem["at_ready"], 1)

                    def squares(n):
                        h, b = n // 4, n % 4
                        act.wait_ge(sem["o_sc"], n + 1)
                        A(tmp[:, 0, 0:P], osb[:, h % 2, b, :], ACT.Square, accum_out=headv[:, h % 2, b:b + 1]
                          ).then_inc(sem["o_sq"], 1)
                        act.wait_ge(sem["o_sq"], n + 1)
                        if b == 3:
                            A(headv[:, h % 2, 4:8], headv[:, h % 2, 0:4], ACT.Sqrt, scale=1.0 / P, bias=eps[:, 0:1]
                              ).then_inc(sem["o_std"], 1)

                    expo(0)
                    for n in range(4 * AHEADS):
                        if n + 1 < 4 * AHEADS:
                            expo(n + 1)
                        evac_at(n)
                        if n >= 2:
                            squares(n - 2)
                    squares(4 * AHEADS - 2)
                    squares(4 * AHEADS - 1)
                    ln1[2](act, nc)

                    for m in range(C8):
                        act.wait_ge(sem["unit_done2"], V_PLEG + m + 1)
                        A(spec[:, m, :], ps[:, m % 4, :], ACT.Sigmoid, bias=col("ple_b", m)).then_inc(sem["pg_sig"], 1)
                        if m == 3:
                            act.wait_ge(sem["r_a"], 1)
                            A(rtr[:, 1, :, 0:4], rtr[:, 1, :, 0:4], ACT.Exp).then_inc(sem["r_ea"], 1)
                            act.wait_ge(sem["r_b"], 1)
                            A(rtr[:, 6, :, 0:1], rtr[:, 6, :, 0:1], ACT.Exp).then_inc(sem["r_eb"], 1)
                    act.wait_ge(sem["gt_mm"], 1)
                    A(gT[:, :], ps[0:EXPERTS, 7, :], ACT.Copy).then_inc(sem["gt_ready"], 1)
                    with act.Fori(0, EXPERTS // 2) as i:
                        for n in range(4):
                            f = n % 2
                            act.wait_ge(sem["ex_done"], i * 4 + n + 1)
                            act.wait_ge(sem["unit_done2"], i * 8 + (V_EXP + 2 * n + 1))
                            A(hid[:, f, :], ps[:, 2 * f, :], ACT.Silu).then_inc(sem["silu"], 1)
                    ln2[2](act, nc)

                @block.gpsimd
                def _(g):
                    G = nc.gpsimd
                    step = Count(sem["pool_step"])
                    for n in range(PC):
                        g.wait_ge(sem["pool_in"], n + 1)
                        src = pool[:, n, :]
                        n0 = S + 2 * PADW
                        cur, width, have = src, n0, 1
                        dst = [pw[:, 0, :], pw[:, 1, :]]
                        k = 0
                        for half in range(2):
                            win = 2 ** (2 * n + half + 1)
                            while have < win:
                                out_, width = dst[k % 2], width - have
                                step.step(g, G.tensor_tensor(out_[:, 0:width], cur[:, 0:width], cur[:, have:have + width],
                                                             ALU.add))
                                cur, have, k = out_, 2 * have, k + 1
                            lo = PADW - win // 2
                            rows = slice(64 * half, 64 * half + 64)
                            step.step(g, G.tensor_tensor(pacc[rows, n, 0:S], cur[rows, lo:lo + S],
                                                         cst[rows, CST2["icnt"][0] + n * S:CST2["icnt"][0] + (n + 1) * S],
                                                         ALU.mult))
                        G.tensor_tensor(pacc[:, n, 0:S], pacc[:, n, 0:S], src[:, PADW:PADW + S], ALU.subtract
                                        ).then_inc(sem["pool_y"], 1)

                @block.vector
                def _(dve):
                    V = nc.vector
                    step = Count(sem["dve_step2"])

                    def do(ins):
                        step.step(dve, ins)

                    dve.sem_inc(sem["ex_done"], 2)
                    dve.wait_ge(sem["par_in2"], 16)
                    V.tensor_tensor(lamt[:, 0:2], col("lq1", 0, 2), col("lk1", 0, 2), ALU.mult).then_inc(sem["lam_prod"], 1)

                    def angles(n, bank):
                        dve.wait_ge(sem[f"f{n + 1}_mm"], 1)
                        r, a, k = hid[0:FH, n, :], tmp[0:FH, 0, :], tmp[0:FH, 1, :]
                        do(V.tensor_scalar(a, ps[0:FH, bank, :], col(f"fb{n + 1}", 0, 1, FH), col(f"fr{n + 1}", 0, 1, FH),
                                           ALU.add, ALU.mult))
                        reduce_angle(dve, nc, step, r, a, k)
                        dve.sem_inc(sem[f"ang{n + 1}"], 1)

                    def hy_taps(u):
                        dve.wait_ge(sem["hy_tap"], u + 1)
                        bank = ps[:, u % 4, :]
                        do(V.scalar_tensor_tensor(hy[:, u, 1:], bank[:, 0:S - 1], col("hw", u), hy[:, u, 1:], ALU.mult, ALU.add))
                        V.scalar_tensor_tensor(hy[:, u, 0:S - 1], bank[:, 1:], col("hw", 6 * HYC + u), hy[:, u, 0:S - 1],
                                               ALU.mult, ALU.add).then_inc(sem["hy_ready"], 1)

                    angles(0, 6)
                    for u in range(V_QK):
                        hy_taps(u)
                    dve.wait_ge(sem["hy_ready"], V_QK)
                    for c in range(HYC):
                        V.tensor_tensor(hy[:, 4 + c, :], hy[:, 4 + c, :], hy[:, 2 + c, :], ALU.mult).then_inc(sem["hy_v"], 1)
                    dve.wait_ge(sem["lam_exp"], 1)
                    do(V.tensor_tensor(lamt[:, 4:5], lamt[:, 3:4], lamt[:, 2:3], ALU.subtract))
                    do(V.tensor_scalar(lamt[:, 4:5], lamt[:, 4:5], col("lam0"), None, ALU.subtract))
                    do(V.tensor_scalar(lamt[:, 5:6], col("sub_g"), col("lam1"), None, ALU.mult))
                    angles(1, 7)
                    for n in range(2 * AC):
                        dve.wait_ge(sem["rot_mm"], n + 1)
                        do(V.tensor_tensor(tmp[:, n % 2, :], ps[:, 4 + n % 2, :], con("sin"), ALU.mult))
                        do(V.tensor_tensor(qk[:, n, :], qk[:, n, :], con("cos"), ALU.mult))
                        V.tensor_tensor(qk[:, n, :], qk[:, n, :], tmp[:, n % 2, :], ALU.add).then_inc(sem["qk_ready"], 1)
                    for t in range(4):
                        dve.wait_ge(sem["filt_mm"], t + 1)
                        win = con("win", t * HW, HW)
                        V.tensor_tensor(filt[:, t, 0, :], ps[:, 4 + t, 0:HW], win, ALU.mult).then_inc(sem["dve_step2"], 1)
                        V.tensor_tensor(filt[:, t, 1, :], ps[:, 4 + t, HW:2 * HW], win, ALU.mult).then_inc(sem["kf_done"], 1)
                        step.n += 1
                    dve.wait_ge(sem["kf_done"], 4)
                    dve.wait_ge(sem["dve_step2"], step.now())
                    do(V.memset(filt[0:1, 0, 1, :], 0.0))
                    for t in range(4):
                        do(V.tensor_tensor(rhs3[:, t, 0:HW], filt[:, t, 0, :], filt[:, t, 1, :], ALU.add))
                        V.tensor_tensor(rhs3[:, t, 2 * HW:], filt[:, t, 0, :], filt[:, t, 1, :], ALU.subtract
                                        ).then_inc(sem["kf_done"], 1)
                    for c in range(HYC):
                        dve.wait_ge(sem["vt_mm"], c + 1)
                        V.tensor_copy(rhs3[:, :, HW + c * P:HW + c * P + P], ps[:, 6 + c, :].rearrange("p (t e) -> p t e", e=P)
                                      ).then_inc(sem["vt_ready"], 1)

                    def spectrum():
                        dve.wait_ge(sem["spec_evac"], 2 * NF)
                        kr, vr = spec[:, 0:NF, 0:HW], spec[:, 0:NF, HW:2 * HW]
                        vs, ks = spec[:, NF:2 * NF, 0:HW], spec[:, NF:2 * NF, HW:2 * HW]
                        do(V.tensor_tensor(ys[:, 0:NF, :], vr, kr, ALU.mult))
                        do(V.tensor_tensor(ytmp, vs, ks, ALU.mult))
                        do(V.tensor_tensor(ys[:, 0:NF, :], ys[:, 0:NF, :], ytmp, ALU.subtract))
                        do(V.tensor_tensor(ys[:, NF:2 * NF, :], vr, ks, ALU.mult))
                        do(V.tensor_tensor(ytmp, vs, kr, ALU.mult))
                        V.tensor_tensor(ys[:, NF:2 * NF, :], ys[:, NF:2 * NF, :], ytmp, ALU.add).then_inc(sem["ys_ready"], 1)
                        dve.wait_ge(sem["nstd"], 1)
                        do(V.reciprocal(lamt[:, 6:8], lamt[:, 6:8]))

                    for n in range(PC):
                        dve.wait_ge(sem["poolm_mm"], n + 1)
                        V.tensor_scalar(mix[:, 6 + n, :], ps[:, 4 + n, :], col("pool_b", n), col("pool_s", n), ALU.add, ALU.mult
                                        ).then_inc(sem["pool_done"], 1)

                    def row_max(n):
                        for c in range(2):
                            dve.wait_ge(sem["s_mm2"], 2 * n + c + 1)
                            sm = small[:, n % 2, :]
                            do(V.reduce_max(sm[:, c:c + 1], ps[:, 2 * (n % 2) + c, :], AXX))
                            V.tensor_scalar(sm[:, 2 + c:3 + c], sm[:, c:c + 1], -0.125, None, ALU.mult).then_inc(sem["nmax2"], 1)

                    def difference(n):
                        dve.wait_ge(sem["p_ready2"], 2 * n + 2)
                        sm = small[:, n % 2, :]
                        do(V.reciprocal(sm[:, 6:8], sm[:, 4:6]))
                        do(V.tensor_scalar(sm[:, 8:9], sm[:, 7:8], sm[:, 4:5], lamt[:, 4:5], ALU.mult, ALU.mult))
                        do(V.tensor_copy(headv[:, n // 4 % 2, 8 + n % 4:9 + n % 4], sm[:, 6:7]))
                        V.scalar_tensor_tensor(pexp[:, n % 2, 0, :], pexp[:, n % 2, 1, :], sm[:, 8:9], pexp[:, n % 2, 0, :],
                                               ALU.mult, ALU.add).then_inc(sem["a_ready2"], 1)

                    def scale_out(n):
                        h, b = n // 4, n % 4
                        dve.wait_ge(sem["o_mm2"], n + 1)
                        V.tensor_scalar(osb[:, h % 2, b, :], ps[:, 6, 0:P], headv[:, h % 2, 8 + b:9 + b], None, ALU.mult
                                        ).then_inc(sem["o_sc"], 1)

                    def norm_out(h):
                        dve.wait_ge(sem["o_std"], h + 1)
                        do(V.reciprocal(headv[:, h % 2, 4:8], headv[:, h % 2, 4:8]))
                        V.tensor_tensor(osb[:, h % 2, :, :], osb[:, h % 2, :, :],
                                        headv[:, h % 2, 4:8].unsqueeze(2).to_broadcast([P, 4, P]), ALU.mult
                                        ).then_inc(sem["o_nrm"], 1)

                    def att_out(h):
                        dve.wait_ge(sem["ot_mm"], h + 1)
                        V.tensor_scalar(mix[:, HYC + h, :], ps[:, 7, :], lamt[:, 5:6], None, ALU.mult).then_inc(sem["att_done"], 1)

                    row_max(0)
                    for n in range(4 * AHEADS):
                        if n + 1 < 4 * AHEADS:
                            row_max(n + 1)
                        difference(n)
                        if n >= 2:
                            scale_out(n - 2)
                        if n >= 5 and n % 4 == 1:
                            norm_out((n - 5) // 4 )
                        if n >= 7 and n % 4 == 3:
                            att_out((n - 7) // 4)
                        if n == 2:
                            spectrum()
                    scale_out(4 * AHEADS - 2)
                    scale_out(4 * AHEADS - 1)
                    norm_out(AHEADS - 1)
                    dve.wait_ge(sem["unit_done2"], V_OUT)
                    for c in range(HYC):
                        do(V.tensor_scalar(tmp[:, c, :], hy[:, 4 + c, :], col("bias", c), None, ALU.mult))
                        do(V.scalar_tensor_tensor(tmp[:, c, :], ps[:, c, :], lamt[:, 6 + c:7 + c], tmp[:, c, :], ALU.mult, ALU.add))
                        V.tensor_tensor(mix[:, c, :], tmp[:, c, :], hy[:, c, :], ALU.mult).then_inc(sem["hy_done"], 1)
                    att_out(AHEADS - 1)

                    for m in range(C8):
                        dve.wait_ge(sem["unit_done2"], V_OUT + m + 1)
                        V.scalar_tensor_tensor(x[:, m, :], x[:, m, :], ALPHA, ps[:, m % 4, :], ALU.mult, ALU.add
                                               ).then_inc(sem["z_ready"], 1)
                    dve.wait_ge(sem["z_ready"], C8)
                    ln1[1](dve, nc)

                    R = [rtr[:, n, :, :] for n in range(12)]

                    def bc(a, n):
                        return a.to_broadcast([P, 4, n])

                    def first_max(src, n, mx, oh):
                        do(V.reduce_max(mx, src, AXX))
                        do(V.tensor_tensor(oh, src, bc(mx, n), ALU.is_equal))
                        for j in range(n):
                            if j:
                                do(V.tensor_tensor(oh[:, :, j:j + 1], oh[:, :, j:j + 1], R[10][:, :, 4:5], ALU.is_gt))
                                do(V.tensor_tensor(R[10][:, :, 4:5], R[10][:, :, 4:5], oh[:, :, j:j + 1], ALU.add))
                            else:
                                do(V.tensor_copy(R[10][:, :, 4:5], oh[:, :, 0:1]))

                    dve.wait_ge(sem["route_mm"], 1)
                    rb = col("rbias", 0, 20).unsqueeze(1).to_broadcast([P, 4, 20])
                    do(V.tensor_tensor(R[0], ps[:, 6, 0:80].rearrange("p (t n) -> p t n", n=20), rb, ALU.add))
                    gl, fl = R[0][:, :, 0:4], R[0][:, :, 4:20]
                    ohg = R[2][:, :, 0:4]
                    first_max(gl, 4, R[2][:, :, 4:5], ohg)
                    V.tensor_tensor(R[1][:, :, 0:4], gl, bc(R[2][:, :, 4:5], 4), ALU.subtract).then_inc(sem["r_a"], 1)
                    for gidx in range(GROUPS):
                        do(V.tensor_tensor(R[3][:, :, 4 * gidx:4 * gidx + 4], fl[:, :, 4 * gidx:4 * gidx + 4],
                                           bc(ohg[:, :, gidx:gidx + 1], 4), ALU.mult))
                    fs = R[4][:, :, 0:4]
                    do(V.tensor_tensor(fs, R[3][:, :, 0:4], R[3][:, :, 4:8], ALU.add))
                    do(V.tensor_tensor(fs, fs, R[3][:, :, 8:12], ALU.add))
                    do(V.tensor_tensor(fs, fs, R[3][:, :, 12:16], ALU.add))
                    m1, oh1 = R[4][:, :, 8:9], R[5][:, :, 0:4]
                    first_max(fs, 4, m1, oh1)
                    fs2 = R[5][:, :, 4:8]
                    do(V.scalar_tensor_tensor(fs2, oh1, -1e30, fs, ALU.mult, ALU.add))
                    m2_, oh2 = R[5][:, :, 12:13], R[5][:, :, 8:12]
                    first_max(fs2, 4, m2_, oh2)
                    V.tensor_tensor(R[6][:, :, 0:1], m2_, m1, ALU.subtract).then_inc(sem["r_b"], 1)
                    dve.wait_ge(sem["r_ea"], 1)
                    do(V.reduce_sum(R[7][:, :, 0:1], R[1][:, :, 0:4], AXX))
                    dve.wait_ge(sem["r_eb"], 1)
                    do(V.tensor_scalar(R[7][:, :, 1:2], R[6][:, :, 0:1], 1.0, None, ALU.add))
                    do(V.tensor_tensor(R[7][:, :, 2:3], R[7][:, :, 1:2], R[7][:, :, 0:1], ALU.mult))
                    do(V.reciprocal(R[7][:, :, 3:4], R[7][:, :, 2:3]))
                    do(V.tensor_tensor(R[7][:, :, 4:5], R[7][:, :, 3:4], R[6][:, :, 0:1], ALU.mult))
                    do(V.tensor_tensor(oh1, oh1, bc(R[7][:, :, 3:4], 4), ALU.mult))
                    do(V.tensor_tensor(oh2, oh2, bc(R[7][:, :, 4:5], 4), ALU.mult))
                    do(V.tensor_tensor(oh1, oh1, oh2, ALU.add))
                    for gidx in range(GROUPS):
                        ins = V.tensor_tensor(R[11][:, :, 4 * gidx:4 * gidx + 4], oh1, bc(ohg[:, :, gidx:gidx + 1], 4), ALU.mult)
                        if gidx < GROUPS - 1:
                            do(ins)
                        else:
                            ins.then_inc(sem["gates"], 1)
                    for m in range(C8):
                        if m % 4 == 3:
                            dve.wait_ge(sem["unit_done2"], V_PLEP + m // 4 + 1)
                        else:
                            dve.wait_ge(sem["dft_mm"], NF + m // 4 * 3 + m % 4 + 1)
                        V.tensor_tensor(spec[:, m, :], spec[:, m, :], ps[:, m % 4, :], ALU.mult).then_inc(sem["pp_done"], 1)
                    dve.wait_ge(sem["gt_ready"], 1)

                    def mask_gate(e, slot):
                        one = cst[0:EXPERTS, e:e + 1] if isinstance(e, int) else cst[0:EXPERTS, ds(e, 1)]
                        V.tensor_scalar(gm[:, slot, :], gT[:, :], one, None, ALU.mult).then_inc(sem["gm_ready"], 1)

                    with dve.Fori(0, EXPERTS // 2) as i:
                        step.enter(i, 4)
                        for e in range(2):
                            if e == 0:
                                dve.wait_ge(sem["g_mm"], HEAD + i * 2)
                                mask_gate(i * 2, 0)
                                mask_gate(i * 2 + 1, 1)
                            for f in range(EC):
                                n = 2 * e + f
                                dve.wait_ge(sem["silu"], i * 4 + n + 1)
                                dve.wait_ge(sem["unit_done2"], i * 8 + (V_EXP + 2 * n + 2))
                                do(V.tensor_tensor(hid[:, f, :], hid[:, f, :], ps[:, 2 * f + 1, :], ALU.mult))
                                dve.wait_ge(sem["g_mm"], HEAD + i * 2 + e + 1)
                                V.tensor_tensor(chunk(wide, i * 4 + n), hid[:, f:f + 1, :], ps[:, 4 + e:5 + e, :], ALU.mult
                                                ).then_inc(sem["ex_done"], 1)
                        step.leave(EXPERTS // 2)
                    per = EXPERTS * EC // 8
                    with dve.Fori(0, C8 // 2) as i:
                        step.enter(i, 2)
                        for m in range(2):
                            dve.wait_ge(sem["unit_done2"], i * 8 + (V_DOWN + per * (m + 1)))
                            xm, sm_ = chunk(x, i * 2 + m), chunk(spec, i * 2 + m)
                            do(V.scalar_tensor_tensor(xm, xm, ALPHA, ps[:, m:m + 1, :], ALU.mult, ALU.add))
                            V.tensor_tensor(xm, xm, sm_, ALU.add).then_inc(sem["z_ready"], 1)
                        step.leave(C8 // 2)
                    dve.wait_ge(sem["z_ready"], 2 * C8)
                    ln2[1](dve, nc)

            nc.all_engine_barrier(sems_to_clear=sem_range)


def build(nc, d, out, only=0):
    with ExitStack() as ctx:
        x = ctx.enter_context(nc.sbuf_tensor("x", [P, C8, S], F32))
        ps = ctx.enter_context(nc.psum_tensor("ps", [P, 8, S], F32))
        stored = ctx.enter_context(nc.semaphore("stored"))
        if only != 2:
            first_block(nc, x, ps, d["x"], d["pos"], d["cst"], d["w1"], d["aw"], d["par1"])
        else:
            with nc.Block() as block:
                @block.sync
                def _(sp):
                    sp.dma_start(x[:, :, :], d["x"]).then_inc(stored, 16)
                    sp.wait_ge(stored, 16)
            nc.all_engine_barrier(sems_to_clear=range(stored.num, stored.num + 1))
        if only != 1:
            second_block(nc, x, ps, d["cst2"], d["w2"], d["par2"], d["p"])
        with nc.Block() as block:
            @block.sync
            def _(sp):
                sp.dma_start(out, x[:, :, :]).then_inc(stored, 16)
                sp.wait_ge(stored, 16)


def _blocks(w):
    k, m = w.shape
    return w.reshape(k // P, P, m // P, P).transpose(2, 1, 0, 3)


def _units(w):
    b = _blocks(w)
    m, p, k, n = b.shape
    return b.reshape(m, p, k // 8, 8 * n).transpose(0, 2, 1, 3).reshape(m * (k // 8), p, 8 * n)


def _cols(v):
    return np.asarray(v).reshape(-1, P).T


def _swap(w):
    h = w.shape[-1] // 2
    return np.concatenate([w[..., h:], w[..., :h]], -1)


def _first_layout(a):
    out = {}
    w1, aw, par = [], [], []
    for l in range(DEPTH):
        w_in = a["w_in"][l]
        q0 = 2 * D
        kv0 = q0 + QC * P
        r0 = kv0 + KVC * P
        ga0 = r0 + ROPE
        gb0 = ga0 + D
        wr = w_in[:, r0:ga0]
        tile = np.concatenate([np.zeros((D, 64), np.float32), wr, _swap(wr)], 1)
        order = [w_in[:, kv0:r0], tile, w_in[:, q0:kv0], w_in[:, 0:D], w_in[:, D:2 * D], w_in[:, ga0:gb0], w_in[:, gb0:]]
        w1 += [_units(np.concatenate(order, 1)), _units(a["w_out"][l])]
        up = _units(a["w_up"][l]).reshape(2, FC, P, 1024).transpose(1, 0, 2, 3).reshape(2 * FC, P, 1024)
        w1 += [up, _units(a["w_down"][l])]
        uq = a["w_uq"][l].reshape(QC, P, HEADS, NOPE + ROPE)
        uq = np.concatenate([uq, _swap(uq[..., NOPE:])], -1)
        ukv = a["w_ukv"][l].reshape(KVC, P, HEADS, NOPE + VH)
        pad = np.zeros((P, P), np.float32)
        for p in range(PAIRS):
            bl = [uq[c, :, 2 * p + h] for h in range(2) for c in range(QC)]
            bl += [np.concatenate([ukv[c, :, 2 * p + h, :NOPE] for c in range(KVC)], -1) for h in range(2)]
            bl += [ukv[c, :, 2 * p:2 * p + 2, NOPE:].reshape(P, P) for c in range(KVC)]
            for g in ("gx_w", "ga_w"):
                d = pad.copy()
                d[:64, :64], d[64:, 64:] = a[g][l][2 * p], a[g][l][2 * p + 1]
                bl.append(d)
            aw.append(np.concatenate(bl, 1))
        par.append(np.concatenate([_cols(a[n][l]) for n in (
            "conv_w", "conv_b", "gx_b", "ga_b", "lru_lambda", "q_norm_g", "kv_norm_g", "ln1_g", "ln1_b", "ln2_g",
            "ln2_b", "ffn_conv_w", "ffn_conv_b")], 1))
    out["w1"] = np.concatenate(w1, 0)
    out["aw"] = np.stack(aw)
    out["par1"] = np.stack(par)
    out["x"] = np.asarray(a["x"])[0].T.reshape(C8, P, S).transpose(1, 0, 2)
    out["pos"] = np.repeat(np.asarray(a["positions"]).reshape(1, S), P, 0)
    cst = np.zeros((P, NCST), np.float32)
    cst[:, :P] = np.eye(P)
    cst[:, P:2 * P] = np.where(np.arange(P)[None, :] > np.arange(P)[:, None], -1e30, 0.0)
    half = ROPE // 2
    cst[:, 2 * P] = 10000.0 ** (-np.arange(P) % half * 0.0 - (np.arange(P) % half) * 2.0 / ROPE)
    cst[:, 2 * P + 1] = np.where((np.arange(P) >= 96) & (np.arange(P) < 96 + half), -1.0, 1.0)
    out["cst"] = cst
    return out


def _rows(v, rows=P):
    v = np.asarray(v, np.float32)
    v = v.reshape(v.shape[0], -1)
    return np.concatenate([v, np.zeros((P - v.shape[0], v.shape[1]), np.float32)], 0)


def _wide_units(w):
    return w.reshape(-1, 2, P, S).transpose(0, 2, 1, 3).reshape(-1, P, 2 * S)


def _tables():
    t = np.arange(S)
    f = np.arange(S) + 0.5
    ang = 2 * np.pi * np.outer(t, f) / (2 * S)
    fwd = np.concatenate([np.cos(ang), np.sin(ang)], 1)
    b = fwd.reshape(4, P, 2 * NF, P).transpose(2, 1, 0, 3)
    dft = b.reshape(NF, 2, P, 4 * P).transpose(0, 2, 1, 3).reshape(NF, P, 8 * P)
    idft = _wide_units(np.concatenate([np.cos(ang).T, np.sin(ang).T], 0) / S)
    cst = {}
    cst["ident"] = np.eye(P)
    perm = np.zeros((P, P))
    rd = 64 // 4
    cos, sin = np.ones((P, S)), np.zeros((P, S))
    inv = (500000.0 ** (-np.arange(0, rd, 2) / rd)).astype(np.float32)
    a = (t.astype(np.float32)[None, :] * inv[:, None]).astype(np.float64)
    for c in (0, 64):
        for i in range(rd // 2):
            perm[c + i + rd // 2, c + i] = -1.0
            perm[c + i, c + i + rd // 2] = 1.0
            for r in (c + i, c + i + rd // 2):
                cos[r], sin[r] = np.cos(a[i]), np.sin(a[i])
    cst["perm"], cst["cos"], cst["sin"] = perm, cos, sin
    tt = np.linspace(0.0, 1.0, S, dtype=np.float32)
    wp = (np.float32(2 * np.pi) * t.astype(np.float32) / np.float32(S)).astype(np.float32)
    bands = np.linspace(1e-4, (FEMB - 1) // 2 - 1, (FEMB - 1) // 2, dtype=np.float32)
    za = (wp[:, None] * bands[None, :]).astype(np.float64)
    cst["z"] = _rows(np.concatenate([tt[:, None], np.cos(za), -np.sin(za)], 1).T)
    deltas = np.linspace(np.log(1e-2) / 1.5, np.log(1e-2) / 0.3, HW)
    win = np.exp(-tt.astype(np.float64)[:, None] * np.abs(deltas)[None, :])
    cst["win"] = win.reshape(4, P, HW).transpose(1, 0, 2).reshape(P, 4 * HW)
    icnt = np.zeros((P, PC, S))
    for g, w in enumerate((2, 4, 8, 16)):
        lo, hi = np.clip(t - w // 2, 0, S - 1), np.clip(t + w // 2 - 1, 0, S - 1)
        icnt[64 * (g % 2):64 * (g % 2) + 64, g // 2] = 1.0 / (hi - lo + 1)
    cst["icnt"] = icnt.reshape(P, PC * S)
    return dft, idft, cst


def _second_layout(a):
    out = {}
    dft, idft, cst = _tables()
    cst["ln0_g"], cst["ln0_b"] = _cols(a["ln0_g_2"]), _cols(a["ln0_b_2"])
    out["cst2"] = np.concatenate([cst[n] for n in CST2], 1).astype(np.float32)
    w2, par = [], []
    for l in range(DEPTH):
        w_in = a["w_in_2"][l]
        q0 = 3 * HW
        v0 = q0 + 2 * AW
        p0 = v0 + AW
        w2 += [_units(w_in[:, :v0]), _wide_units(w_in[:, v0:p0]), _units(w_in[:, p0:]),
               dft.astype(np.float32), idft.astype(np.float32), _units(a["w_out_2"][l]), _units(a["ple_wg_2"][l])]
        b = _blocks(a["ple_wp_2"][l])
        w2.append(b.reshape(2, 4, P, 2 * P).transpose(0, 2, 1, 3).reshape(2, P, 8 * P))
        ex = [np.stack([_units(a[n][l][e]) for n in ("moe_w1_2", "moe_w3_2")], 1).reshape(2 * EC, P, 8 * P)
              for e in range(EXPERTS)]
        w2 += ex + [_units(a["moe_w2_2"][l].reshape(EXPERTS * DE, D))]
        lam0 = 0.8 - 0.6 * np.exp(-0.3 * l)
        full = lambda v: np.full((P, 1), v, np.float32)
        pw = []
        for n in range(PC):
            m = np.zeros((P, P), np.float32)
            m[:64, :64], m[64:, 64:] = a["pool_w_2"][l][2 * n], a["pool_w_2"][l][2 * n + 1]
            pw.append(m)
        router = np.concatenate([a["moe_wgc_2"][l], a["moe_wgf_2"][l]], 1)
        parts = {
            "hw": _cols(a["hy_conv_w_2"][l]), "hb": _cols(a["hy_conv_b_2"][l]),
            "fb1": _rows(a["hy_fb1_2"][l]), "fr1": _rows(a["hy_freq1_2"][l]),
            "fb2": _rows(a["hy_fb2_2"][l]), "fr2": _rows(a["hy_freq2_2"][l]),
            "bias": _cols(a["hy_bias_2"][l]),
            "lq1": _rows(a["att_lq1_2"][l]), "lq2": _rows(a["att_lq2_2"][l]),
            "lk1": _rows(a["att_lk1_2"][l]), "lk2": _rows(a["att_lk2_2"][l]),
            "lam0": full(lam0), "lam1": full(1.0 - lam0), "sub_g": _cols(a["att_subln_g_2"][l]),
            "pool_b": _cols(a["pool_b_2"][l]), "pool_s": _cols(a["pool_scale_2"][l]),
            "ln1_g": _cols(a["ln1_g_2"][l]), "ln1_b": _cols(a["ln1_b_2"][l]),
            "ln2_g": _cols(a["ln2_g_2"][l]), "ln2_b": _cols(a["ln2_b_2"][l]), "ple_b": _cols(a["ple_bg_2"][l]),
            "rbias": np.repeat(np.concatenate([a["moe_bgc_2"][l], a["moe_bgf_2"][l]])[None], P, 0),
            "fw1": _rows(a["hy_fw1_2"][l]), "fw2": _rows(a["hy_fw2_2"][l]), "fw3": _rows(a["hy_fw3_2"][l]),
            "poolw": np.concatenate(pw, 1),
            "router": router.reshape(C8, P, 20).transpose(1, 0, 2).reshape(P, C8 * 20),
        }
        par.append(np.concatenate([parts[n] for n in PAR2], 1))
    out["w2"] = np.concatenate(w2, 0)
    out["par2"] = np.stack(par)
    out["p"] = a["p_2"][:, 0].transpose(0, 2, 1).reshape(DEPTH, 2, P, S).transpose(0, 2, 1, 3)
    return out


def _layout(inputs):
    a = {k: np.asarray(v) for k, v in inputs.items()}
    out = {**_first_layout(a), **_second_layout(a)}
    return {k: np.ascontiguousarray(v) for k, v in out.items()}


def kernel(**inputs):
    import concourse.bacc as bacc
    from concourse.bass_utils import run_bass_kernel_spmd

    nc = bacc.Bacc("TRN2", target_bir_lowering=False, num_devices=1)
    arrays = _layout(inputs)
    d = {k: nc.dram_tensor("in_" + k, v.shape, mybir.dt.from_np(v.dtype), kind="ExternalInput").ap()
         for k, v in arrays.items()}
    out = nc.dram_tensor("out", (P, C8, S), F32, kind="ExternalOutput").ap()
    build(nc, d, out)
    r = run_bass_kernel_spmd(nc, [{"in_" + k: v for k, v in arrays.items()}], core_ids=[0])
    y = r.results[0]["out"]
    return np.ascontiguousarray(y.transpose(1, 0, 2).reshape(D, S).T).reshape(1, S, D)
```

```python
from contextlib import ExitStack

import numpy as np

import concourse.bass as bass
from concourse import mybir

F32 = mybir.dt.float32
F32R = mybir.dt.float32r
I32 = mybir.dt.int32
ALU = mybir.AluOpType
ACT = mybir.ActivationFunctionType
AXX = mybir.AxisListType.X
ds = bass.ds

P = 128
S = 512
D = 1024
DEPTH = 2
HEAD = 1
C8 = D // P
ALPHA = float((2 * DEPTH) ** 0.25)

HEADS = 16
NOPE, ROPE, VH = 64, 32, 64
QC, KVC = 3, 2
FF = 3 * D
FC = FF // P
SCALE1 = float((NOPE + ROPE) ** -0.5)
EPS1 = 1e-6
PAIRS = HEADS // 2
RAW = 4
SPLIT = 2
PROJ_UNITS = KVC + 1 + QC + 4 * C8
OUT_UNITS = C8
UP_UNITS = 2 * FC
DOWN_PER = FC // 8
U_V = PROJ_UNITS
U_ATT = U_V + KVC
U_OUT = U_ATT + PAIRS
U_UP = U_OUT + OUT_UNITS
U_DOWN = U_UP + UP_UNITS
U1 = U_DOWN + DOWN_PER * C8

TWO_PI = 6.283185307179586
PI2_A = 6.28125
PI2_B = 0.0019350051879882812
PI2_C = TWO_PI - PI2_A - PI2_B
MAGIC = 12582912.0
PI_DOWN = 3.1415925


def columns(spec):
    at, out = 0, {}
    for name, n in spec:
        out[name] = (at, n)
        at += n
    return out, at


PAR1, NPAR1 = columns([("conv_w", 4 * C8), ("conv_b", C8), ("gx_b", C8), ("ga_b", C8), ("lam", C8),
                       ("q_g", QC), ("kv_g", KVC), ("ln1_g", C8), ("ln1_b", C8), ("ln2_g", C8),
                       ("ln2_b", C8), ("ffw", 3 * 2 * FC), ("ffb", 2 * FC)])
CST, NCST = columns([("ident", P), ("mask", P), ("invf", 1), ("sign", 1)])


class Count:

    def __init__(self, sem):
        self.sem, self.n, self.off = sem, 0, 0

    def inc(self, ins):
        ins.then_inc(self.sem, 1)
        self.n += 1

    def now(self):
        return self.off + self.n

    def step(self, eng, ins):
        self.inc(ins)
        eng.wait_ge(self.sem, self.now())

    def enter(self, i, per):
        self.base, self.off, self.per = self.n, i * per, per

    def leave(self, times):
        assert self.n == self.base + self.per, (self.n, self.base, self.per)
        self.off, self.n = 0, self.base + self.per * times


def sems(nc, ctx, names):
    handles = {n: ctx.enter_context(nc.semaphore(n)) for n in names}
    nums = sorted(h.num for h in handles.values())
    assert nums == list(range(nums[0], nums[0] + len(nums)))
    return handles, range(nums[0], nums[-1] + 1)


class Memory:

    def __init__(self, nc):
        self.nc, self.base, self.end = nc, -(-nc.sbuf_base // 64) * 64, nc.sbuf_base + nc.sbuf_bytes_remaining

    def at(self, name, kb, shape, dt=F32):
        size = int(np.prod(shape[1:])) * 4
        off = self.base + int(kb * 1024)
        assert off + size <= self.end, (name, off + size - self.end)
        return self.nc.alloc_sbuf_tensor_at(name, shape, dt, offset=off)


class Shared:

    def __init__(self, nc, mem, ps):
        self.ps = ps
        self.xh = mem.at("xh", 0, [P, C8, S], F32R)
        self.xl = mem.at("xl", 16, [P, C8, S], F32R)
        self.ring = mem.at("ring", 32, [P, RAW, 8 * P])
        self.wh = mem.at("wh", 48, [P, SPLIT, 8, P], F32R)
        self.wl = mem.at("wl", 56, [P, SPLIT, 8, P], F32R)
        self.z = mem.at("z", 64, [P, C8, S])
        self.sq = mem.at("sq", 80, [P, C8, S])


def stream_units(sp, sem, ring, d_w, first, units):
    def load(slot, unit):
        sp.dma_start(ring[:, slot, :], d_w[ds(first + unit, 1)].rearrange("a p n -> p (a n)")
                     ).then_inc(sem[f"w_in{slot}"], 16)

    for j in range(RAW):
        load(j, j)
    turns = (units - RAW) // RAW
    with sp.Fori(0, turns) as i:
        for j in range(RAW):
            sp.wait_ge(sem["w_split"], i * RAW + (j + 1))
            load(j, i * RAW + (j + RAW))
    for u in range(turns * RAW, units - RAW):
        sp.wait_ge(sem["w_split"], u + 1)
        load(u % RAW, u + RAW)


def split_units(g, nc, sem, sh, units):
    def split(n, i, j):
        g.wait_ge(sem[f"w_in{j}"], i * 16 + 16)
        g.wait_ge(sem["unit_done"], n + 1)
        g.sem_inc(sem["w_turn"], 1)
        raw = sh.ring[:, j, :]
        hi, lo = (t[:, j % SPLIT, :, :].rearrange("p a b -> p (a b)") for t in (sh.wh, sh.wl))
        nc.gpsimd.tensor_scalar(hi, raw, 1.0, 0.0, ALU.mult, ALU.add).then_inc(sem["w_hi"], 1)
        g.wait_ge(sem["w_hi"], n + 1)
        nc.gpsimd.tensor_tensor(lo, raw, hi, ALU.subtract).then_inc(sem["w_split"], 1)

    turns = units // RAW
    with g.Fori(0, turns) as i:
        for j in range(RAW):
            split(i * RAW + j, i, j)
    for u in range(turns * RAW, units):
        split(u, turns, u % RAW)


def three(nc, out, wh, wl, xh, xl, first, last, **kw):
    nc.tensor.matmul(out, wh, xh, start=first, stop=False, **kw)
    nc.tensor.matmul(out, wh, xl, start=False, stop=False, **kw)
    return nc.tensor.matmul(out, wl, xh, start=False, stop=last, **kw)


def unit_products(pe, nc, sem, sh, xh, xl, bank, n, parity, first=True, last=True, chunks_from=None):
    pe.wait_ge(sem["w_split"], n + 1)
    for k in range(8):
        if chunks_from is not None:
            pe.wait_ge(sem["x_ready"], chunks_from + k + 1)
        mm = three(nc, bank, sh.wh[:, parity, k, :], sh.wl[:, parity, k, :], xh[:, k, :], xl[:, k, :],
                   first and k == 0, last and k == 7)
    mm.then_inc(sem["unit_done"], 1)


def layer_norm_engines(rounds_before, sem, sh, ones_d, eps, par, g0, b0, stat):
    r, z, sq, xh, xl = rounds_before, sh.z, sh.sq, sh.xh, sh.xl
    ps_mean, ps_var = sh.ps[:, 4, :], sh.ps[:, 5, :]

    def tensor(pe, nc):
        pe.wait_ge(sem["z_ready"], r * C8 + C8)
        nc.tensor.matmul(ps_mean, ones_d, stat[:, 0, :], start=True, stop=True).then_inc(sem["mean_mm"], 1)
        for k in range(C8):
            pe.wait_ge(sem["sq_ready"], r * C8 + k + 1)
            mm = nc.tensor.matmul(ps_var, ones_d, sq[:, k, :], start=(k == 0), stop=(k == C8 - 1))
        mm.then_inc(sem["var_mm"], 1)

    def vector(dve, nc):
        dve.wait_ge(sem["mean_mm"], r + 1)
        for k in range(C8):
            nc.vector.tensor_tensor(z[:, k, :], z[:, k, :], ps_mean, ALU.subtract).then_inc(sem["xc_ready"], 1)
        dve.wait_ge(sem["std_ready"], r + 1)
        nc.vector.reciprocal(stat[:, 0, :], stat[:, 1, :]).then_inc(sem["rstd_ready"], 1)
        dve.wait_ge(sem["rstd_ready"], r + 1)
        dve.wait_ge(sem["xc_ready"], r * C8 + C8)
        for k in range(C8 + 1):
            if k < C8:
                nc.vector.tensor_tensor(z[:, k, :], z[:, k, :], stat[:, 0, :], ALU.mult).then_inc(sem["xn_ready"], 1)
            if k:
                dve.wait_ge(sem["xa_ready"], r * C8 + k)
                nc.vector.tensor_tensor(xl[:, k - 1, :], z[:, k - 1, :], xh[:, k - 1, :], ALU.subtract
                                        ).then_inc(sem["x_ready"], 1)

    def scalar(act, nc):
        for k in range(C8):
            act.wait_ge(sem["xc_ready"], r * C8 + k + 1)
            nc.scalar.activation(sq[:, k, :], z[:, k, :], ACT.Square).then_inc(sem["sq_ready"], 1)
        act.wait_ge(sem["var_mm"], r + 1)
        nc.scalar.activation(stat[:, 1, :], ps_var, ACT.Sqrt, bias=eps).then_inc(sem["std_ready"], 1)
        for k in range(C8):
            act.wait_ge(sem["xn_ready"], r * C8 + k + 1)
            g, b = par[:, g0 + k:g0 + k + 1], par[:, b0 + k:b0 + k + 1]
            nc.scalar.activation(xh[:, k, :], z[:, k, :], ACT.Identity, scale=g, bias=b)
            nc.scalar.activation(z[:, k, :], z[:, k, :], ACT.Identity, scale=g, bias=b).then_inc(sem["xa_ready"], 1)

    return tensor, vector, scalar


def residual_chunk(dve, nc, do, sem, sh, m, bank, stat, extra=None, signal=True):
    V, z = nc.vector, sh.z[:, m, :]
    do(V.scalar_tensor_tensor(z, sh.xh[:, m, :], ALPHA, bank, ALU.mult, ALU.add))
    ins = V.scalar_tensor_tensor(z, sh.xl[:, m, :], ALPHA, z, ALU.mult, ALU.add)
    if extra is not None:
        do(ins)
        ins = V.tensor_tensor(z, z, extra, ALU.add)
    return ins


def sum_chunk(dve, nc, do, sem, sh, m, stat):
    V, z, acc = nc.vector, sh.z[:, m, :], stat[:, 0, :]
    ins = V.tensor_tensor(acc, acc, z, ALU.add) if m else V.tensor_copy(acc, z)
    ins.then_inc(sem["z_ready"], 1)


LN_SEMS = ["z_ready", "mean_mm", "xc_ready", "sq_ready", "var_mm", "std_ready", "rstd_ready", "xn_ready",
           "xa_ready", "x_ready"]
STREAM_SEMS = [f"w_in{j}" for j in range(RAW)] + ["w_turn", "w_hi", "w_split", "unit_done"]


def reduce_angle(dve, nc, step, r, ang, n):
    step.step(dve, nc.vector.tensor_scalar(n, ang, 1.0 / TWO_PI, MAGIC, ALU.mult, ALU.add))
    step.step(dve, nc.vector.tensor_scalar(n, n, -MAGIC, None, ALU.add))
    step.step(dve, nc.vector.scalar_tensor_tensor(r, n, -PI2_A, ang, ALU.mult, ALU.add))
    step.step(dve, nc.vector.scalar_tensor_tensor(r, n, -PI2_B, r, ALU.mult, ALU.add))
    step.step(dve, nc.vector.scalar_tensor_tensor(r, n, -PI2_C, r, ALU.mult, ALU.add))
    step.step(dve, nc.vector.tensor_scalar(r, r, PI_DOWN, -PI_DOWN, ALU.min, ALU.max))


def first_block(nc, mem, sh, d_x, d_pos, d_cst, d_w, d_gw, d_par):
    with ExitStack() as ctx:
        ps = sh.ps
        at = mem.at
        qt = at("qt", 64, [P, 2, S])
        rt = at("rt", 68, [P, 2, S])
        kt = at("kt", 72, [P, 2, 2, S])
        hid_h = at("hid_h", 80, [P, FC, S], F32R)
        hid_l = at("hid_l", 128, [P, FC, S], F32R)
        gate_r = at("gate_r", 80, [P, C8, S])
        merged_h = at("merged_h", 80, [P, C8, S], F32R)
        rnn_in = at("rnn_in", 96, [P, C8, S])
        vals = at("vals", 112, [P, 4, D])
        gate_b = at("gate_b", 128, [P, C8, S])
        merged_l = at("merged_l", 128, [P, C8, S], F32R)
        lat_h = at("lat_h", 144, [P, KVC + QC, S], F32R)
        lat_l = at("lat_l", 154, [P, KVC + QC, S], F32R)
        gw = at("gw", 164, [P, 2, 2, P])
        lat_sq = at("lat_sq", 166, [P, KVC + QC, S])
        sx, sa, th, av, m2 = (at(n, 166 + 2 * k, [P, S]) for k, n in enumerate(("sx", "sa", "th", "av", "m2")))
        lat = at("lat", 176, [P, KVC + 1 + QC, S])
        pb = at("pb", 176, [P, 4, S])
        taps = at("taps", 176, [P, 2, 2, S])
        sig_a = at("sig_a", 188, [P, 2, S])
        pt = at("pt", 184, [P, 4, S])
        stat = at("stat", 192, [P, 2, S])
        osb = at("osb", 192, [P, 2, 4, P])
        tmp = at("tmp", 196, [P, 2, S])
        rope = at("rope", 200, [P, S])
        par = at("par", 202, [P, NPAR1])
        cst = at("cst", 203.5, [P, NCST])
        ones_d = at("ones_d", 204.75, [P, P])
        small = at("small", 205.25, [P, 4, 16])
        lru = at("lru", 205.5, [P, 6, C8])
        eps = at("eps", 205.75, [P, 1])
        kvraw, krope, qraw = lat[:, 0:KVC, :], lat[:, KVC, :], lat[:, KVC + 1:, :]

        names = (STREAM_SEMS + LN_SEMS + ["gw_in0", "gw_in1", "par_in", "cst_in", "x_in",
                 "proj_evac", "proj_tap", "lat_sq", "lat_mm", "lat_std", "lat_rstd", "lat_ready",
                 "kpe_ready", "dve_step", "ang_ready", "sin_ready", "abs_ready", "expl_ready", "lru_ready",
                 "q_mm", "k_mm", "v_mm", "qn_ready", "qr_ready", "k_ready", "v_ready", "s_mm", "nmax_ready",
                 "p_ready", "t_mm", "pt_ready", "o_mm", "o_ready", "y_mm", "merged", "conv_ready", "gate_mm",
                 "gate_sig", "a_ready", "m2_ready", "mu_ready", "rnn_done", "gated_r",
                 "ff_tap", "ff_conv", "ff_gelu", "ff_done"])
        sem, sem_range = sems(nc, ctx, names)

        def chunk(t, k):
            return t[:, k, :] if isinstance(k, int) else t[:, ds(k, 1), :]

        def one(t, k):
            return t[:, k:k + 1] if isinstance(k, int) else t[:, ds(k, 1)]

        def col(name, k=0):
            return one(par, k + PAR1[name][0])

        ident = cst[:, CST["ident"][0]:CST["ident"][0] + P]
        mask = cst[:, CST["mask"][0]:CST["mask"][0] + P]

        ln1 = layer_norm_engines(0, sem, sh, ones_d[:, :], eps[:, 0:1], par, PAR1["ln1_g"][0], PAR1["ln1_b"][0], stat)
        ln2 = layer_norm_engines(1, sem, sh, ones_d[:, :], eps[:, 0:1], par, PAR1["ln2_g"][0], PAR1["ln2_b"][0], stat)
        pos = at("pos", 196, [P, S], I32)

        with nc.Block() as block:
            @block.sync
            def _(sp):
                sp.dma_start(pos[:, :], d_pos).then_inc(sem["par_in"], 16)
                sp.dma_start(cst[:, :], d_cst).then_inc(sem["cst_in"], 16)
                sp.dma_start(sh.z[:, :, :], d_x).then_inc(sem["x_in"], 16)

            @block.gpsimd
            def _(pool):
                nc.gpsimd.memset(ones_d[:, :], 1.0 / D)
                nc.gpsimd.memset(eps[:, :], EPS1)

            @block.vector
            def _(dve):
                step = Count(sem["dve_step"])
                dve.wait_ge(sem["xa_ready"], C8)
                nc.vector.tensor_tensor(sh.xl[:, :, :], sh.z[:, :, :], sh.xh[:, :, :], ALU.subtract)
                fr, sg = CST["invf"][0], CST["sign"][0]
                dve.wait_ge(sem["par_in"], 16)
                dve.wait_ge(sem["cst_in"], 16)
                hi = slice(64, P)
                ang, n, r = pb[hi, 0, :], pb[hi, 1, :], pb[hi, 2, :]
                step.step(dve, nc.vector.tensor_copy(ang, pos[hi, :]))
                step.step(dve, nc.vector.tensor_scalar(ang, ang, cst[hi, fr:fr + 1], None, ALU.mult))
                reduce_angle(dve, nc, step, r, ang, n)
                c = pb[64:96, 2, :]
                step.step(dve, nc.vector.tensor_scalar(pb[64:96, 3, :], c, -1.0, None, ALU.mult))
                step.step(dve, nc.vector.tensor_tensor(c, c, pb[64:96, 3, :], ALU.max))
                nc.vector.tensor_scalar(c, c, -1.0, TWO_PI / 4, ALU.mult, ALU.add).then_inc(sem["ang_ready"], 1)
                dve.wait_ge(sem["sin_ready"], 1)
                nc.vector.tensor_scalar(rope[hi, :], rope[hi, :], cst[hi, sg:sg + 1], None, ALU.mult)

            @block.scalar
            def _(act):
                act.wait_ge(sem["x_in"], 16)
                for k in range(C8):
                    nc.scalar.activation(sh.xh[:, k, :], sh.z[:, k, :], ACT.Copy).then_inc(sem["xa_ready"], 1)
                act.wait_ge(sem["ang_ready"], 1)
                nc.scalar.activation(rope[64:P, :], pb[64:P, 2, :], ACT.Sin).then_inc(sem["sin_ready"], 1)

        nc.all_engine_barrier(sems_to_clear=sem_range)

        with nc.Fori(0, DEPTH) as layer:
            with nc.Block() as block:
                @block.sync
                def _(sp):
                    sp.dma_start(par[:, :], d_par[ds(layer, 1)].rearrange("a p n -> p (a n)")).then_inc(sem["par_in"], 16)

                    def load_gates(slot, pair):
                        sp.dma_start(gw[:, slot], d_gw[ds(layer * PAIRS + pair, 1)].rearrange("a p (k m) -> p (a k) m", m=P)
                                     ).then_inc(sem[f"gw_in{slot}"], 16)

                    for j in range(2):
                        load_gates(j, j)
                    stream_units(sp, sem, sh.ring, d_w, layer * U1, U1)

                @block.gpsimd
                def _(g):
                    split_units(g, nc, sem, sh, U1)

                @block.tensor
                def _(pe):
                    for n in ("t_mm", "o_mm"):
                        pe.sem_inc(sem[n], HEAD)
                    pe.sem_inc(sem["unit_done"], SPLIT)

                    def unit(bank, n, parity, xh=sh.xh, xl=sh.xl, **kw):
                        unit_products(pe, nc, sem, sh, xh, xl, bank, n, parity, **kw)

                    head = KVC + 1 + QC
                    for u in range(head):
                        pe.wait_ge(sem["proj_evac"], u + 1)
                        unit(ps[:, u % 4, :], u, u % 2)
                    with pe.Fori(0, 6) as i:
                        for j in range(4):
                            pe.wait_ge(sem["proj_evac"], i * 4 + (head + j + 1))
                            unit(ps[:, (head + j) % 4, :], i * 4 + (head + j), j % 2)
                    pe.wait_ge(sem["lat_sq"], KVC + QC)
                    for k in range(KVC):
                        mm = nc.tensor.matmul(ps[:, 4, :], ones_d[:, :], lat_sq[:, k, :], start=(k == 0), stop=(k == KVC - 1))
                    mm.then_inc(sem["lat_mm"], 1)
                    for k in range(QC):
                        mm = nc.tensor.matmul(ps[:, 5, :], ones_d[:, :], lat_sq[:, KVC + k, :], start=(k == 0), stop=(k == QC - 1))
                    mm.then_inc(sem["lat_mm"], 1)
                    for u in range(head + 24, PROJ_UNITS):
                        pe.wait_ge(sem["proj_evac"], u + 1)
                        unit(ps[:, u % 4, :], u, u % 2)

                    def project_q(par_, half):
                        for c in range(QC):
                            mm = three(nc, ps[:, 0, :], sh.wh[:, par_, half * 3 + c, :], sh.wl[:, par_, half * 3 + c, :],
                                       lat_h[:, KVC + c, :], lat_l[:, KVC + c, :], c == 0, c == QC - 1)
                        mm.then_inc(sem["unit_done" if half else "q_mm"], 1)

                    def project_k(par_):
                        for c in range(KVC):
                            mm = three(nc, ps[:, 1, :], sh.wh[:, par_, 6 + c, :], sh.wl[:, par_, 6 + c, :],
                                       lat_h[:, c, :], lat_l[:, c, :], c == 0, c == KVC - 1)
                        mm.then_inc(sem["k_mm"], 1)

                    def scores(pp, hb, b):
                        n = (b + 1) * P
                        nc.tensor.matmul(ps[:, 2 + b % 2, 0:n], qt[0:96, hb, b * P:b * P + P], kt[0:96, pp, hb, 0:n],
                                         start=True, stop=True).then_inc(sem["s_mm"], 1)

                    def turn(b):
                        for j in range(b + 1):
                            mm = nc.tensor.transpose(ps[:, 4 + b % 2, j * P:j * P + P], pb[:, b, j * P:j * P + P], ident)
                        mm.then_inc(sem["t_mm"], 1)

                    def weigh(h, b):
                        for j in range(b + 1):
                            mm = nc.tensor.matmul(ps[:, 6, b * 64:b * 64 + 64],
                                                  pt[:, b, j * P:j * P + P], vals[:, j, ds(h * 64, 64)] if not isinstance(h, int)
                                                  else vals[:, j, h * 64:h * 64 + 64],
                                                  start=(j == 0), stop=(j == b))
                        mm.then_inc(sem["o_mm"], 1)

                    def turn_out(pp):
                        for b in range(4):
                            mm = nc.tensor.transpose(ps[:, 7, b * P:b * P + P], osb[:, pp, b, :], ident)
                        mm.then_inc(sem["y_mm"], 1)

                    pe.wait_ge(sem["lat_ready"], KVC + QC)
                    pe.wait_ge(sem["proj_evac"], PROJ_UNITS + 4)
                    for c in range(KVC):
                        n = U_V + c
                        pe.wait_ge(sem["w_split"], n + 1)
                        for t in range(4):
                            tok = slice(t * P, t * P + P)
                            for g in range(2):
                                wh, wl = (w[:, n % 2, 4 * g:4 * g + 4, :].rearrange("p a b -> p (a b)") for w in (sh.wh, sh.wl))
                                mm = three(nc, ps[:, 2 * t + g, :], lat_h[:, c, tok], lat_l[:, c, tok], wh, wl,
                                           c == 0, c == KVC - 1, skip_group_check=True)
                                if c == KVC - 1 and 2 * t + g < 7:
                                    mm.then_inc(sem["v_mm"], 1)
                        mm.then_inc(sem["unit_done"], 1)
                    pe.wait_ge(sem["w_split"], U_ATT + 1)
                    pe.wait_ge(sem["v_ready"], 2)
                    project_q(0, 0)
                    project_k(0)
                    pe.wait_ge(sem["v_ready"], 8)
                    pe.wait_ge(sem["kpe_ready"], 4)

                    def four_heads(i, last):
                        for hh in range(4):
                            pp, hb = hh // 2, hh % 2
                            h4, h, p = i * 16 + hh * 4, i * 4 + hh, i * 2 + pp
                            pe.wait_ge(sem["qn_ready"], h + 1)
                            pe.wait_ge(sem["qr_ready"], h + 1)
                            pe.wait_ge(sem["k_ready"], p + 1)
                            pe.wait_ge(sem["p_ready"], HEAD + h4)
                            scores(pp, hb, 0)
                            scores(pp, hb, 1)
                            if not (last and hh == 3):
                                pe.wait_ge(sem["gate_sig"], HEAD + p * 2 + 2 * hb)
                                if hb == 0:
                                    project_q(pp, 1)
                                else:
                                    pe.wait_ge(sem["w_split"], p + (U_ATT + 2))
                                    project_q(1 - pp, 0)
                                    project_k(1 - pp)
                            pe.wait_ge(sem["pt_ready"], HEAD + h4)
                            pe.wait_ge(sem["p_ready"], HEAD + h4 + 1)
                            turn(0)
                            scores(pp, hb, 2)
                            pe.wait_ge(sem["p_ready"], HEAD + h4 + 2)
                            turn(1)
                            scores(pp, hb, 3)
                            pe.wait_ge(sem["o_ready"], HEAD + h)
                            pe.wait_ge(sem["pt_ready"], HEAD + h4 + 1)
                            weigh(h, 0)
                            pe.wait_ge(sem["pt_ready"], HEAD + h4 + 2)
                            weigh(h, 1)
                            if hb == 0:
                                pe.wait_ge(sem["qn_ready"], h + 2)
                                pe.wait_ge(sem["qr_ready"], h + 2)
                                pe.wait_ge(sem[f"gw_in{pp}"], i * 16 + 16)
                                for g in range(2):
                                    nc.tensor.matmul(ps[:, g, :], gw[:, pp, g, :], chunk(rnn_in, p),
                                                     start=True, stop=True).then_inc(sem["gate_mm"], 1)
                            pe.wait_ge(sem["p_ready"], HEAD + h4 + 3)
                            turn(2)
                            pe.wait_ge(sem["p_ready"], HEAD + h4 + 4)
                            turn(3)
                            pe.wait_ge(sem["pt_ready"], HEAD + h4 + 3)
                            weigh(h, 2)
                            pe.wait_ge(sem["pt_ready"], HEAD + h4 + 4)
                            weigh(h, 3)
                            if hb == 1:
                                pe.wait_ge(sem["merged"], HEAD + p)
                                pe.wait_ge(sem["o_ready"], HEAD + h + 1)
                                turn_out(pp)

                    with pe.Fori(0, PAIRS // 2 - 1) as i:
                        four_heads(i, False)
                    four_heads(PAIRS // 2 - 1, True)

                    pe.wait_ge(sem["merged"], HEAD + PAIRS)
                    for m in range(C8):
                        if m >= 4:
                            pe.wait_ge(sem["z_ready"], m - 3)
                        unit(ps[:, m % 4, :], U_OUT + m, m % 2, merged_h, merged_l)
                    ln1[0](pe, nc)

                    with pe.Fori(0, FC // 4) as i:
                        for j in range(4):
                            pe.wait_ge(sem["ff_conv"], i * 4 + j + 1)
                            for half in range(2):
                                unit(ps[:, 2 * j + half, :], i * 8 + (U_UP + 2 * j + half), half,
                                     chunks_from=0 if j + half == 0 else None)
                    pe.wait_ge(sem["ff_done"], HEAD + FC)
                    with pe.Fori(0, C8 // 4) as i:
                        for m in range(4):
                            pe.wait_ge(sem["z_ready"], i * 4 + C8 + m - 3 if m >= 3 else i * 4 + C8)
                            for q in range(DOWN_PER):
                                unit(ps[:, m, :], i * 12 + (U_DOWN + m * DOWN_PER + q), (m + q) % 2,
                                     hid_h[:, q * 8:q * 8 + 8, :], hid_l[:, q * 8:q * 8 + 8, :],
                                     first=q == 0, last=q == DOWN_PER - 1)
                    ln2[0](pe, nc)

                @block.scalar
                def _(act):
                    for n in ("p_ready", "pt_ready", "gate_sig"):
                        act.sem_inc(sem[n], HEAD)
                    act.sem_inc(sem["proj_evac"], 4)
                    for u in range(KVC + 1 + QC):
                        act.wait_ge(sem["unit_done"], SPLIT + u + 1)
                        nc.scalar.activation(lat[:, u, :], ps[:, u % 4, :], ACT.Copy).then_inc(sem["proj_evac"], 1)
                    act.wait_ge(sem["proj_evac"], 4 + KVC + 1 + QC)
                    for k in range(KVC):
                        nc.scalar.activation(lat_sq[:, k, :], kvraw[:, k, :], ACT.Square).then_inc(sem["lat_sq"], 1)
                    for k in range(QC):
                        nc.scalar.activation(lat_sq[:, KVC + k, :], qraw[:, k, :], ACT.Square).then_inc(sem["lat_sq"], 1)
                    act.wait_ge(sem["par_in"], 16)
                    u0 = KVC + 1 + QC
                    with act.Fori(0, 2) as i:
                        for j in range(4):
                            act.wait_ge(sem["unit_done"], SPLIT + i * 4 + (u0 + j + 1))
                            nc.scalar.activation(chunk(rnn_in, i * 4 + j), ps[:, (u0 + j) % 4, :], ACT.Identity,
                                                 scale=col("conv_w", i * 4 + (3 * C8 + j)), bias=col("conv_b", i * 4 + j)
                                                 ).then_inc(sem["proj_tap"], 1)
                            act.wait_ge(sem["conv_ready"], i * 4 + j + 1)
                            act.sem_inc(sem["proj_evac"], 1)
                    u0 += C8
                    with act.Fori(0, 2) as i:
                        for j in range(4):
                            act.wait_ge(sem["unit_done"], SPLIT + i * 4 + (u0 + j + 1))
                            nc.scalar.activation(chunk(gate_r, i * 4 + j), ps[:, (u0 + j) % 4, :],
                                                 ACT.Gelu_apprx_tanh).then_inc(sem["proj_evac"], 1)
                    u0 += C8
                    act.wait_ge(sem["abs_ready"], 1)
                    nc.scalar.activation(lru[:, 1, :], lru[:, 0, :], ACT.Exp, scale=-1.0).then_inc(sem["expl_ready"], 1)
                    with act.Fori(0, 4) as i:
                        for j in range(2):
                            act.wait_ge(sem["unit_done"], SPLIT + i * 2 + (u0 + j + 1))
                            if j == 0:
                                act.wait_ge(sem["gated_r"], HEAD + i * 2)
                            bank = ps[:, ds((i * 2 + (u0 + j)) % 4, 1), :]
                            nc.scalar.activation(sig_a[:, j:j + 1, :], bank, ACT.Sigmoid).then_inc(sem["proj_evac"], 1)
                    u0 += C8
                    for m in range(C8):
                        if m == 4:
                            for n, (bank, width) in enumerate(((4, KVC * P), (5, QC * P))):
                                act.wait_ge(sem["lat_mm"], n + 1)
                                nc.scalar.activation(stat[:, n, :], ps[:, bank, :], ACT.Sqrt, scale=float(D) / width,
                                                     bias=eps[:, 0:1]).then_inc(sem["lat_std"], 1)
                        act.wait_ge(sem["unit_done"], SPLIT + u0 + m + 1)
                        nc.scalar.activation(gate_b[:, m, :], ps[:, (u0 + m) % 4, :], ACT.Sigmoid
                                             ).then_inc(sem["proj_evac"], 1)

                    def evac_q(h, p, buf):
                        if buf:
                            act.wait_ge(sem["unit_done"], SPLIT + p + (U_ATT + 1))
                        else:
                            act.wait_ge(sem["q_mm"], p + 1)
                        nc.scalar.activation(qt[0:64, buf, :], ps[0:64, 0, :], ACT.Copy).then_inc(sem["qn_ready"], 1)

                    def evac_k(p, pp):
                        act.wait_ge(sem["k_mm"], p + 1)
                        nc.scalar.activation(kt[0:64, pp, 0, :], ps[0:64, 1, :], ACT.Copy)
                        nc.scalar.activation(kt[0:64, pp, 1, :], ps[64:P, 1, :], ACT.Copy).then_inc(sem["k_ready"], 1)

                    def expo(hh, h4, b):
                        act.wait_ge(sem["nmax_ready"], h4 + b + 1)
                        c = hh * 4 + b
                        nc.scalar.activation(pb[:, b, 0:(b + 1) * P], ps[:, 2 + b % 2, 0:(b + 1) * P], ACT.Exp,
                                             scale=SCALE1, bias=small[:, 1, c:c + 1], accum_out=small[:, 2, c:c + 1]
                                             ).then_inc(sem["p_ready"], 1)

                    def evac_pt(h4, b):
                        act.wait_ge(sem["t_mm"], HEAD + h4 + b + 1)
                        nc.scalar.activation(pt[:, b, 0:(b + 1) * P], ps[:, 4 + b % 2, 0:(b + 1) * P], ACT.Copy
                                             ).then_inc(sem["pt_ready"], 1)

                    for n in range(8):
                        if n < 7:
                            act.wait_ge(sem["v_mm"], n + 1)
                        else:
                            act.wait_ge(sem["unit_done"], SPLIT + U_ATT)
                        nc.scalar.activation(vals[:, n // 2, n % 2 * S:n % 2 * S + S], ps[:, n, :], ACT.Copy
                                             ).then_inc(sem["v_ready"], 1)
                    evac_q(0, 0, 0)
                    evac_k(0, 0)

                    def four_heads(i, last):
                        for hh in range(4):
                            pp, hb = hh // 2, hh % 2
                            h4, h, p = i * 16 + hh * 4, i * 4 + hh, i * 2 + pp
                            act.wait_ge(sem["t_mm"], HEAD + h4)
                            expo(hh, h4, 0)
                            expo(hh, h4, 1)
                            if not (last and hh == 3):
                                evac_q(h + 1, p + hb, 1 - hb)
                                if hb == 1:
                                    evac_k(p + 1, 1 - pp)
                            if hb == 1:
                                act.wait_ge(sem["m2_ready"], p + 1)
                                nc.scalar.activation(m2[:, :], m2[:, :], ACT.Sqrt, scale=2.0).then_inc(sem["mu_ready"], 1)
                            act.wait_ge(sem["o_mm"], HEAD + h4)
                            evac_pt(h4, 0)
                            evac_pt(h4, 1)
                            expo(hh, h4, 2)
                            expo(hh, h4, 3)
                            if hb == 0:
                                act.wait_ge(sem["rnn_done"], HEAD + p)
                                for g, (name, out) in enumerate((("gx_b", sx), ("ga_b", sa))):
                                    act.wait_ge(sem["gate_mm"], p * 2 + g + 1)
                                    nc.scalar.activation(out[:, :], ps[:, g, :], ACT.Sigmoid, bias=col(name, p)
                                                         ).then_inc(sem["gate_sig"], 1)
                                act.wait_ge(sem["gate_sig"], HEAD + p * 2 + 2)
                                if not last:
                                    act.dma_start(gw[:, pp], d_gw[ds(layer * PAIRS + (p + 2), 1)]
                                                  .rearrange("a p (k m) -> p (a k) m", m=P)).then_inc(sem[f"gw_in{pp}"], 16)
                                act.wait_ge(sem["lru_ready"], 1)
                                nc.scalar.activation(th[:, :], sa[:, :], ACT.Tanh, scale=one(lru[:, 4, :], p)
                                                     ).then_inc(sem["a_ready"], 1)
                                nc.scalar.activation(av[:, :], sa[:, :], ACT.Exp, scale=one(lru[:, 5, :], p)
                                                     ).then_inc(sem["a_ready"], 1)
                            evac_pt(h4, 2)
                            evac_pt(h4, 3)

                    with act.Fori(0, PAIRS // 2 - 1) as i:
                        four_heads(i, False)
                    four_heads(PAIRS // 2 - 1, True)

                    ln1[2](act, nc)
                    with act.Fori(0, FC // 4) as i:
                        for j in range(4):
                            f = i * 4 + j
                            act.wait_ge(sem["ff_done"], HEAD + (f - 1 if j else f))
                            for half in range(2):
                                act.wait_ge(sem["unit_done"], SPLIT + f * 2 + (U_UP + half + 1))
                                nc.scalar.activation(taps[:, j % 2, half, :], ps[:, 2 * j + half, :], ACT.Identity,
                                                     scale=col("ffw", f + (2 * 2 * FC + half * FC)),
                                                     bias=col("ffb", f + half * FC)).then_inc(sem["ff_tap"], 1)
                            act.wait_ge(sem["ff_conv"], f + 5)
                            nc.scalar.activation(taps[:, j % 2, 0, :], taps[:, j % 2, 0, :], ACT.Gelu_apprx_tanh
                                                 ).then_inc(sem["ff_gelu"], 1)
                    ln2[2](act, nc)

                @block.vector
                def _(dve):
                    step = Count(sem["dve_step"])
                    V = nc.vector
                    def split(v, hi, lo, done):
                        step.step(dve, V.tensor_scalar(hi, v, 1.0, None, ALU.mult))
                        V.tensor_tensor(lo, v, hi, ALU.subtract).then_inc(sem[done], 1)

                    dve.sem_inc(sem["ff_conv"], 4)
                    for n in ("merged", "o_ready", "gated_r", "rnn_done", "ff_done"):
                        dve.sem_inc(sem[n], HEAD)
                    dve.wait_ge(sem["proj_evac"], 4 + KVC + 1)
                    step.step(dve, V.tensor_tensor(rt[64:96, 0, :], krope[96:P, :], rope[96:P, :], ALU.mult))
                    step.step(dve, V.tensor_tensor(rt[64:96, 1, :], krope[64:96, :], rope[64:96, :], ALU.mult))
                    for n in range(4):
                        V.tensor_tensor(kt[64:96, n // 2, n % 2, :], rt[64:96, 0, :], rt[64:96, 1, :], ALU.add
                                        ).then_inc(sem["kpe_ready"], 1)
                    dve.wait_ge(sem["par_in"], 16)
                    lam = par[:, PAR1["lam"][0]:PAR1["lam"][0] + C8]
                    L = [lru[:, n, :] for n in range(6)]
                    step.step(dve, V.tensor_scalar(L[2], lam, -1.0, None, ALU.mult))
                    V.tensor_tensor(L[0], L[2], lam, ALU.max).then_inc(sem["abs_ready"], 1)

                    u0 = KVC + 1 + QC
                    with dve.Fori(0, 2) as i:
                        step.enter(i, 8)
                        for j in range(4):
                            m, bank = i * 4 + j, ps[:, (u0 + j) % 4, :]
                            dve.wait_ge(sem["proj_tap"], i * 4 + j + 1)
                            for s in (1, 2, 3):
                                out = rnn_in[:, ds(m, 1), s:]
                                ins = V.scalar_tensor_tensor(out, bank[:, 0:S - s], col("conv_w", i * 4 + (j + (3 - s) * C8)),
                                                             out, ALU.mult, ALU.add)
                                if s < 3:
                                    step.step(dve, ins)
                                else:
                                    ins.then_inc(sem["conv_ready"], 1)
                        step.leave(2)

                    dve.wait_ge(sem["expl_ready"], 1)
                    z, t, s2 = L[1], L[3], L[0]
                    step.step(dve, V.tensor_scalar(t, z, 2.0, None, ALU.add))
                    step.step(dve, V.reciprocal(t, t))
                    step.step(dve, V.tensor_tensor(t, z, t, ALU.mult))
                    step.step(dve, V.tensor_tensor(s2, t, t, ALU.mult))
                    acc = L[4]
                    step.step(dve, V.tensor_scalar(acc, s2, 1.0 / 15, None, ALU.mult))
                    for n in (13, 11, 9, 7, 5, 3):
                        step.step(dve, V.scalar_tensor_tensor(acc, acc, 1.0 / n, s2, ALU.add, ALU.mult))
                    step.step(dve, V.scalar_tensor_tensor(acc, acc, 1.0, t, ALU.add, ALU.mult))
                    step.step(dve, V.tensor_scalar(L[2], L[2], 0.0, None, ALU.max))
                    step.step(dve, V.scalar_tensor_tensor(acc, acc, 2.0, L[2], ALU.mult, ALU.add))
                    step.step(dve, V.tensor_scalar(L[5], acc, -8.0, None, ALU.mult))
                    V.tensor_scalar(acc, acc, 8.0, None, ALU.mult).then_inc(sem["lru_ready"], 1)

                    u0 += 2 * C8
                    with dve.Fori(0, 4) as i:
                        for j in range(2):
                            dve.wait_ge(sem["proj_evac"], i * 2 + (u0 + j + 5))
                            g = chunk(gate_r, i * 2 + j)
                            V.tensor_tensor(g, g, sig_a[:, j:j + 1, :], ALU.mult).then_inc(sem["gated_r"], 1)

                    for n, (t, name, width) in enumerate(((kvraw, "kv_g", KVC), (qraw, "q_g", QC))):
                        dve.wait_ge(sem["lat_std"], n + 1)
                        V.reciprocal(stat[:, n, :], stat[:, n, :]).then_inc(sem["lat_rstd"], 1)
                        dve.wait_ge(sem["lat_rstd"], n + 1)
                        for k in range(width):
                            step.step(dve, V.scalar_tensor_tensor(t[:, k, :], t[:, k, :], col(name, k), stat[:, n, :],
                                                                  ALU.mult, ALU.mult))
                            split(t[:, k, :], lat_h[:, n * KVC + k, :], lat_l[:, n * KVC + k, :], "lat_ready")

                    def rotate_q(h, p, buf):
                        if buf:
                            dve.wait_ge(sem["unit_done"], SPLIT + p + (U_ATT + 1))
                        else:
                            dve.wait_ge(sem["q_mm"], p + 1)
                        step.step(dve, V.tensor_tensor(rt[64:96, buf, :], ps[96:P, 0, :], rope[96:P, :], ALU.mult))
                        step.step(dve, V.tensor_tensor(qt[64:96, buf, :], ps[64:96, 0, :], rope[64:96, :], ALU.mult))
                        V.tensor_tensor(qt[64:96, buf, :], qt[64:96, buf, :], rt[64:96, buf, :], ALU.add
                                        ).then_inc(sem["qr_ready"], 1)

                    def row_max(hh, h4, b):
                        dve.wait_ge(sem["s_mm"], h4 + b + 1)
                        bank, c = ps[:, 2 + b % 2, :], hh * 4 + b
                        own = bank[:, b * P:b * P + P]
                        step.step(dve, V.tensor_tensor(own, own, mask, ALU.add))
                        step.step(dve, V.reduce_max(small[:, 0, c:c + 1], bank[:, 0:(b + 1) * P], AXX))
                        V.tensor_scalar(small[:, 1, c:c + 1], small[:, 0, c:c + 1], -SCALE1, None, ALU.mult
                                        ).then_inc(sem["nmax_ready"], 1)

                    def normalise_out(hh, h):
                        pp, hb, c = hh // 2, hh % 2, hh * 4
                        dve.wait_ge(sem["o_mm"], HEAD + h * 4 + 4)
                        step.step(dve, V.reciprocal(small[:, 3, c:c + 4], small[:, 2, c:c + 4]))
                        V.tensor_tensor(osb[:, pp, :, hb * 64:hb * 64 + 64],
                                        ps[:, 6, 0:256].rearrange("p (b e) -> p b e", b=4),
                                        small[:, 3, c:c + 4].unsqueeze(2).to_broadcast([P, 4, 64]), ALU.mult
                                        ).then_inc(sem["o_ready"], 1)

                    rotate_q(0, 0, 0)

                    def four_heads(i, last):
                        for hh in range(4):
                            pp, hb = hh // 2, hh % 2
                            h4, h, p = i * 16 + hh * 4, i * 4 + hh, i * 2 + pp
                            row_max(hh, h4, 0)
                            row_max(hh, h4, 1)
                            if not (last and hh == 3):
                                rotate_q(h + 1, p + hb, 1 - hb)
                            row_max(hh, h4, 2)
                            row_max(hh, h4, 3)
                            normalise_out(hh, h)
                            if hb == 0:
                                dve.wait_ge(sem["a_ready"], p * 2 + 1)
                                step.step(dve, V.tensor_scalar(m2[:, :], th[:, :], 1.0, None, ALU.add))
                                step.step(dve, V.reciprocal(m2[:, :], m2[:, :]))
                                V.tensor_tensor(m2[:, :], th[:, :], m2[:, :], ALU.mult).then_inc(sem["m2_ready"], 1)
                            else:
                                dve.wait_ge(sem["mu_ready"], p + 1)
                                step.step(dve, V.tensor_tensor(sx[:, :], sx[:, :], chunk(rnn_in, p)[:, 0, :]
                                                               if not isinstance(p, int) else rnn_in[:, p, :], ALU.mult))
                                step.step(dve, V.tensor_tensor(sx[:, :], sx[:, :], m2[:, :], ALU.mult))
                                dve.wait_ge(sem["a_ready"], p * 2 + 2)
                                step.step(dve, V.tensor_tensor_scan(sa[:, :], av[:, :], sx[:, :], 0.0, ALU.mult, ALU.add))
                                g = chunk(gate_r, p)
                                V.tensor_tensor(g, g, sa[:, :], ALU.mult).then_inc(sem["rnn_done"], 1)
                                dve.wait_ge(sem["y_mm"], p + 1)
                                dve.wait_ge(sem["rnn_done"], HEAD + p + 1)
                                v = tmp[:, 0, :]
                                gb, gr = (t[:, p, :] if isinstance(p, int) else chunk(t, p)[:, 0, :] for t in (gate_b, gate_r))
                                mh, ml = (t[:, p, :] if isinstance(p, int) else chunk(t, p)[:, 0, :]
                                          for t in (merged_h, merged_l))
                                step.step(dve, V.tensor_tensor(v, gb, ps[:, 7, :], ALU.mult))
                                step.step(dve, V.tensor_tensor(v, v, gr, ALU.add))
                                split(v, mh, ml, "merged")

                    per = 4 * (2 + 8 + 1) + 2 * 2 + 2 * 6
                    with dve.Fori(0, PAIRS // 2 - 1) as i:
                        step.enter(i, per)
                        four_heads(i, False)
                        step.leave(PAIRS // 2 - 1)
                    four_heads(PAIRS // 2 - 1, True)

                    def do(ins):
                        step.step(dve, ins)

                    def residual(u0, per_tile):
                        for m in range(C8):
                            dve.wait_ge(sem["unit_done"], SPLIT + u0 + (m + 1) * per_tile)
                            do(residual_chunk(dve, nc, do, sem, sh, m, ps[:, m % 4, :], stat))
                            sum_chunk(dve, nc, do, sem, sh, m, stat)

                    residual(U_OUT, 1)
                    dve.wait_ge(sem["z_ready"], C8)
                    ln1[1](dve, nc)
                    with dve.Fori(0, FC // 4) as i:
                        step.enter(i, 4 * 5)
                        for j in range(4):
                            f = i * 4 + j
                            for half in range(2):
                                dve.wait_ge(sem["ff_tap"], f * 2 + half + 1)
                                for s in (1, 2):
                                    out = taps[:, j % 2, half, s:]
                                    ins = V.scalar_tensor_tensor(
                                        out, ps[:, 2 * j + half, 0:S - s], col("ffw", f + ((2 - s) * 2 * FC + half * FC)),
                                        out, ALU.mult, ALU.add)
                                    if half == 1 and s == 2:
                                        ins.then_inc(sem["ff_conv"], 1)
                                    else:
                                        step.step(dve, ins)
                            dve.wait_ge(sem["ff_gelu"], f + 1)
                            dve.wait_ge(sem["ff_conv"], f + 5)
                            v = taps[:, j % 2, 0:1, :]
                            step.step(dve, V.tensor_tensor(v, v, taps[:, j % 2, 1:2, :], ALU.mult))
                            split(v, chunk(hid_h, f), chunk(hid_l, f), "ff_done")
                        step.leave(FC // 4)
                    residual(U_DOWN, DOWN_PER)
                    dve.wait_ge(sem["z_ready"], 2 * C8)
                    ln2[1](dve, nc)

            nc.all_engine_barrier(sems_to_clear=sem_range)


HW, AW, PW = D // 4, D // 2, D // 4
AHEADS = 4
HYC, AC, PC = HW // P, AW // P, PW // P
LN_EPS = 1e-5
FH = 64
FEMB = 33
EXPERTS, GROUPS, DE = 16, 4, 256
EC = DE // P
PLE = 256
NF = S // P
HALF = EXPERTS // 2
EXP_UNITS = 2 * EC * HALF
DOWN_HALF = HALF * EC // 8
V_POOL = 0
V_HY = V_POOL + PC
V_QK = V_HY + 3 * HYC
V_V = V_QK + 2 * AC
V_DFT = V_V + AC
V_IDFT = V_DFT + NF
V_OUT = V_IDFT + NF
V_PLEG = V_OUT + C8
V_PLEP = V_PLEG + C8
V_EXP = [V_PLEP + 2, V_PLEP + 2 + EXP_UNITS + C8 * DOWN_HALF]
V_DOWN = [v + EXP_UNITS for v in V_EXP]
U2 = V_DOWN[1] + C8 * DOWN_HALF

PAR2, NPAR2 = columns([("hw", 9 * HYC), ("hb", 3 * HYC), ("fb1", 1), ("fr1", 1), ("fb2", 1), ("fr2", 1),
                       ("bias", HYC), ("lq1", 1), ("lq2", 1), ("lk1", 1), ("lk2", 1), ("lam0", 1), ("lam1", 1),
                       ("sub_g", 1), ("pool_b", PC), ("pool_s", PC), ("ln1_g", C8), ("ln1_b", C8), ("ln2_g", C8),
                       ("ln2_b", C8), ("ple_b", C8), ("rbias", 20), ("fw1", FH), ("fw2", FH), ("fw3", 2 * HW),
                       ("poolw", PC * P), ("router", C8 * 20)])
CST2, NCST2 = columns([("ident", P), ("perm", P), ("ln0_g", C8), ("ln0_b", C8)])
TAB, NTAB = columns([("z", S), ("win", 4 * HW), ("trig", 2 * S), ("icnt", PC * S)])
PADW = 8


def second_block(nc, mem, sh, d_cst, d_tab, d_w, d_par, d_p):
    with ExitStack() as ctx:
        ps, z, xh, xl = sh.ps, sh.z, sh.xh, sh.xl
        at_ = mem.at
        pexp = at_("pexp", 64, [P, 2, 2, S])
        filt = at_("filt", 64, [P, 4, 2, HW])
        at = at_("at", 72, [P, 2, S])
        trig = at_("trig", 72, [P, 2, S])
        osb = at_("osb2", 76, [P, 2, 4, P])
        win = at_("win", 76, [P, 4, HW])
        hy = at_("hy", 80, [P, 3 * HYC, S])
        qk = at_("qk", 92, [P, 2 * AC, S])
        v4 = at_("v4", 108, [P, 4, AW])
        mix_h = at_("mix_h", 116, [P, C8, S], F32R)
        mix_l = at_("mix_l", 132, [P, C8, S], F32R)
        icnt = at_("icnt", 132, [P, PC, S])
        emb = at_("emb", 136, [P, S])
        rhs3_h = at_("rhs3_h", 148, [P, 4, 3 * HW], F32R)
        rhs3_l = at_("rhs3_l", 160, [P, 4, 3 * HW], F32R)
        ys_h = at_("ys_h", 148, [P, 2 * NF, HW], F32R)
        ytmp = at_("ytmp", 156, [P, NF, HW])
        ys_l = at_("ys_l", 160, [P, 2 * NF, HW], F32R)
        yfull = at_("yfull", 168, [P, NF, HW])
        pool = at_("pool", 172, [P, PC, S + 2 * PADW])
        pacc = at_("pacc", 176.25, [P, PC, S + 2 * PADW])
        pw = at_("pw", 180.5, [P, 2, S + 2 * PADW])
        spec = at_("spec", 172, [P, 8, S])
        act_h = at_("act_h", 80, [P, HALF * EC, S], F32R)
        act_l = at_("act_l", 112, [P, HALF * EC, S], F32R)
        pT = at_("pT", 144, [P, 2, S])
        pT_h = at_("pT_h", 148, [P, 2, S], F32R)
        pT_l = at_("pT_l", 152, [P, 2, S], F32R)
        gT = at_("gT", 156, [EXPERTS, S])
        gm = at_("gm", 158, [EXPERTS, 2, S])
        rtr = at_("rtr", 162, [P, 12, 4, 20])
        router_h = at_("router_h", 166, [P, C8 * 20], F32R)
        router_l = at_("router_l", 167, [P, C8 * 20], F32R)
        stat = at_("stat2", 188, [P, 2, S])
        hid = at_("hid", 192, [P, 2, S])
        tmp = at_("tmp2", 196, [P, 2, S])
        par = at_("par2", 200, [P, NPAR2])
        cst = at_("cst2", 204.625, [P, NCST2])
        ones = at_("ones2", 205.75, [P, P])
        ones_d = at_("ones_d2", 206.25, [P, P])
        small = at_("small2", 206.75, [P, 2, 12])
        headv = at_("headv", 206.875, [P, 2, 12])
        lamt = at_("lamt", 207, [P, 8])
        eps = at_("eps2", 207.0625, [P, 2])

        names = (STREAM_SEMS + LN_SEMS + ["par_in2", "cst_in2", "tab_in", "p_in", "proj_evac2", "hy_tap",
                 "hy_ready", "hy_v", "f1_mm", "ang1", "sin1", "f2_mm", "ang2", "sin2", "filt_mm", "kf_win", "kf_done",
                 "sqk", "norm_mm", "nstd", "rot_mm", "qk_ready", "v_ready2", "pool_in", "pool_zero", "pool_y",
                 "poolm_mm", "pool_done", "vt_mm", "vt_hi", "vt_ready", "dft_mm", "spec_evac", "ys_ready",
                 "hy_done", "lam_prod", "lam_mm", "lam_exp", "s_mm2", "nmax2", "p_ready2", "a_ready2",
                 "t_mm2", "at_ready", "o_mm2", "o_sc", "o_sq", "o_std", "o_nrm", "ot_mm", "att_done", "dve_step2",
                 "router_ready", "route_mm", "r_a", "r_ea", "r_b", "r_eb", "gates", "gt_mm", "gt_ready", "gm_ready",
                 "g_mm", "silu", "ex_done", "pg_sig", "pp_done", "pt_hi", "pt_lo", "down_evac"])
        sem, sem_range = sems(nc, ctx, names)

        def chunk(t, k):
            return t[:, k, :] if isinstance(k, int) else t[:, ds(k, 1), :]

        def col(name, k=0, n=1, rows=P):
            at_ = PAR2[name][0] + k
            return par[0:rows, at_:at_ + n]

        def con(name, k=0, n=None):
            at_, w = CST2[name]
            return cst[:, at_ + k:at_ + k + (w if n is None else n)]

        ident = con("ident")
        ln0 = layer_norm_engines(0, sem, sh, ones_d[:, :], eps[:, 0:1], cst, CST2["ln0_g"][0], CST2["ln0_b"][0], stat)
        ln1 = layer_norm_engines(0, sem, sh, ones_d[:, :], eps[:, 0:1], par, PAR2["ln1_g"][0], PAR2["ln1_b"][0], stat)
        ln2 = layer_norm_engines(1, sem, sh, ones_d[:, :], eps[:, 0:1], par, PAR2["ln2_g"][0], PAR2["ln2_b"][0], stat)

        with nc.Block() as block:
            @block.sync
            def _(sp):
                sp.dma_start(cst[:, :], d_cst).then_inc(sem["cst_in2"], 16)
                sp.wait_ge(sem["cst_in2"], 16)

            @block.gpsimd
            def _(g):
                nc.gpsimd.memset(ones[:, :], 1.0)
                nc.gpsimd.memset(eps[:, 0:1], LN_EPS)
                nc.gpsimd.memset(eps[:, 1:2], 1e-6)
                nc.gpsimd.memset(ones_d[:, :], 1.0 / D)

        nc.all_engine_barrier(sems_to_clear=sem_range)
        with nc.Block() as block:
            @block.tensor
            def _(pe):
                ln0[0](pe, nc)

            @block.scalar
            def _(act):
                ln0[2](act, nc)

            @block.vector
            def _(dve):
                for m in range(C8):
                    if m:
                        dve.wait_ge(sem["z_ready"], m)
                    sum_chunk(dve, nc, None, sem, sh, m, stat)
                ln0[1](dve, nc)

        nc.all_engine_barrier(sems_to_clear=sem_range)

        with nc.Fori(0, DEPTH) as layer:
            with nc.Block() as block:
                @block.sync
                def _(sp):
                    sp.dma_start(par[:, :], d_par[ds(layer, 1)].rearrange("a p n -> p (a n)")).then_inc(sem["par_in2"], 16)

                    for t, (a, w) in ((emb[:, :], TAB["z"]), (win[:, :, :], TAB["win"]), (trig[:, :, :], TAB["trig"]),
                                      (icnt[:, :, :], TAB["icnt"])):
                        src = d_tab[:, a:a + w]
                        if len(t.shape) == 3:
                            src = src.rearrange("p (a n) -> p a n", a=t.shape[1])
                        sp.dma_start(t, src).then_inc(sem["tab_in"], 16)
                    stream_units(sp, sem, sh.ring, d_w, layer * U2, U2)

                @block.gpsimd
                def _(g):
                    nc.gpsimd.memset(pool[:, :, :], 0.0).then_inc(sem["pool_zero"], 1)
                    split_units(g, nc, sem, sh, U2)

                @block.tensor
                def _(pe):
                    T = nc.tensor

                    def unit(bank, n, parity, rh=xh, rl=xl, **kw):
                        unit_products(pe, nc, sem, sh, rh, rl, bank, n, parity, **kw)

                    def flat(w, n, half):
                        return w[:, n % 2, half * 4:half * 4 + 4, :].rearrange("p a b -> p (a b)")

                    for n in ("g_mm",):
                        pe.sem_inc(sem[n], HEAD)
                    pe.sem_inc(sem["unit_done"], SPLIT)
                    pe.wait_ge(sem["par_in2"], 16)
                    pe.wait_ge(sem["tab_in"], 64)
                    T.matmul(ps[0:FH, 6, :], col("fw1", 0, FH, FEMB), emb[0:FEMB, :],
                             start=True, stop=True).then_inc(sem["f1_mm"], 1)
                    pe.wait_ge(sem["lam_prod"], 1)
                    T.matmul(ps[:, 7, 0:2], ones[:, :], lamt[:, 0:2], start=True, stop=True).then_inc(sem["lam_mm"], 1)
                    for n in range(PC):
                        unit(ps[:, 4 + n, :], V_POOL + n, n % 2)
                    for n in range(3 * HYC):
                        pe.wait_ge(sem["proj_evac2"], n + 1)
                        unit(ps[:, n % 4, :], V_HY + n, n % 2)
                    pe.wait_ge(sem["sin1"], 1)
                    pe.wait_ge(sem["lam_exp"], 1)
                    T.matmul(ps[0:FH, 7, :], col("fw2", 0, FH, FH), hid[0:FH, 0, :], start=True, stop=True
                             ).then_inc(sem["f2_mm"], 1)
                    q0 = 3 * HYC
                    pe.wait_ge(sem["pool_in"], PC)

                    def rotate(n):
                        pe.wait_ge(sem["proj_evac2"], 4 + q0 + n + 1)
                        if n >= 2:
                            pe.wait_ge(sem["qk_ready"], n - 1)
                        T.matmul(ps[:, 4 + n % 2, :], con("perm"), qk[:, n, :], start=True, stop=True
                                 ).then_inc(sem["rot_mm"], 1)

                    def filters(t):
                        if t >= 2:
                            pe.wait_ge(sem["kf_win"], t - 1)
                        T.matmul(ps[:, 6 + t % 2, :], hid[0:FH, 1, t * P:t * P + P], col("fw3", 0, 2 * HW, FH),
                                 start=True, stop=True).then_inc(sem["filt_mm"], 1)

                    for n in range(2 * AC):
                        pe.wait_ge(sem["proj_evac2"], q0 + n + 1)
                        unit(ps[:, (q0 + n) % 4, :], V_QK + n, n % 2)
                        if n:
                            rotate(n - 1)
                        if n == 5:
                            pe.wait_ge(sem["sin2"], 1)
                        if n >= 5:
                            filters(n - 5)
                    pe.wait_ge(sem["proj_evac2"], 4 + q0 + 2 * AC - 1)
                    for q in range(AC):
                        n = V_V + q
                        if q == 1:
                            rotate(2 * AC - 1)
                            filters(3)
                        if q == 0:
                            pe.wait_ge(sem["proj_evac2"], 4 + q0 + 2 * AC)
                        if q == 3:
                            pe.wait_ge(sem["hy_v"], HYC)
                            pe.wait_ge(sem["kf_win"], 4)
                            for c in range(HYC):
                                for t in range(4):
                                    mm = T.transpose(ps[:, 6 + c, t * P:t * P + P], hy[:, 4 + c, t * P:t * P + P], ident)
                                mm.then_inc(sem["vt_mm"], 1)
                        pe.wait_ge(sem["w_split"], n + 1)
                        for kk in range(2):
                            k = 2 * q + kk
                            for t in range(4):
                                tok = slice(t * P, t * P + P)
                                mm = three(nc, ps[:, t, :], xh[:, k, tok], xl[:, k, tok], flat(sh.wh, n, kk), flat(sh.wl, n, kk),
                                           k == 0, k == 7, skip_group_check=True)
                        mm.then_inc(sem["unit_done"], 1)
                    pe.wait_ge(sem["qk_ready"], 2 * AC)
                    for n in range(PC):
                        pe.wait_ge(sem["pool_y"], n + 1)
                        T.matmul(ps[:, 4 + n, :], col("poolw", n * P, P), pacc[:, n, 0:S], start=True, stop=True
                                 ).then_inc(sem["poolm_mm"], 1)
                    pe.wait_ge(sem["v_ready2"], 4)
                    pe.wait_ge(sem["vt_ready"], HYC)
                    pe.wait_ge(sem["kf_done"], 8)
                    for n in range(2 * NF):
                        u = V_DFT + n // 2
                        if n % 2 == 0:
                            pe.wait_ge(sem["w_split"], u + 1)
                        if n >= 4:
                            pe.wait_ge(sem["spec_evac"], n - 3)
                        cols = slice(0, 2 * HW) if n < NF else slice(HW, 3 * HW)
                        for t in range(4):
                            b_ = (n % 2) * 4 + t
                            mm = three(nc, ps[:, n % 4, :], sh.wh[:, u % 2, b_, :], sh.wl[:, u % 2, b_, :],
                                       rhs3_h[:, t, cols], rhs3_l[:, t, cols], t == 0, t == 3)
                        mm.then_inc(sem["dft_mm" if n % 2 == 0 else "unit_done"], 1)
                    pe.wait_ge(sem["sqk"], 1)
                    for c in range(HYC):
                        for t in range(4):
                            for w in range(2):
                                mm = T.matmul(ps[:, 6, c:c + 1], filt[:, t, w, c * P:c * P + P], ones[:, 0:1],
                                              start=(t + w == 0), stop=(t == 3 and w == 1), skip_group_check=True)
                    mm.then_inc(sem["norm_mm"], 1)
                    pe.wait_ge(sem["spec_evac"], 2 * NF)
                    pe.wait_ge(sem["pool_done"], PC)
                    pe.wait_ge(sem["nstd"], 1)

                    def scores(n):
                        h, b = n // 4, n % 4
                        if n >= 2:
                            pe.wait_ge(sem["p_ready2"], 2 * (n - 1))
                        for c in range(2):
                            lo = slice(64 * c, 64 * c + 64)
                            T.matmul(ps[:, 2 * (n % 2) + c, :], qk[lo, h, b * P:b * P + P], qk[lo, AC + h, :],
                                     start=True, stop=True).then_inc(sem["s_mm2"], 1)

                    def turn(n):
                        pe.wait_ge(sem["a_ready2"], n + 1)
                        if n >= 2:
                            pe.wait_ge(sem["at_ready"], n - 1)
                        for j in range(4):
                            mm = T.transpose(ps[:, 4 + n % 2, j * P:j * P + P], pexp[:, n % 2, 0, j * P:j * P + P], ident)
                        mm.then_inc(sem["t_mm2"], 1)

                    def weigh(n):
                        h = n // 4
                        pe.wait_ge(sem["at_ready"], n + 1)
                        pe.wait_ge(sem["o_sc"], n)
                        for j in range(4):
                            mm = T.matmul(ps[:, 6, 0:P], at[:, n % 2, j * P:j * P + P], v4[:, j, h * P:h * P + P],
                                          start=(j == 0), stop=(j == 3))
                        mm.then_inc(sem["o_mm2"], 1)

                    def turn_out(h):
                        pe.wait_ge(sem["o_nrm"], h + 1)
                        pe.wait_ge(sem["att_done"], h)
                        for b in range(4):
                            mm = T.transpose(ps[:, 7, b * P:b * P + P], osb[:, h % 2, b, :], ident)
                        mm.then_inc(sem["ot_mm"], 1)

                    scores(0)
                    for n in range(4 * AHEADS):
                        if n + 1 < 4 * AHEADS:
                            scores(n + 1)
                        turn(n)
                        if n:
                            weigh(n - 1)
                        if n >= 6 and n % 4 == 2:
                            turn_out((n - 6) // 4)
                    weigh(4 * AHEADS - 1)
                    pe.wait_ge(sem["ys_ready"], 2)
                    pe.wait_ge(sem["p_ready2"], 8 * AHEADS)
                    for q in range(NF):
                        n = V_IDFT + q
                        pe.wait_ge(sem["w_split"], n + 1)
                        for kk in range(2):
                            f = 2 * q + kk
                            for c in range(HYC):
                                ch = slice(c * P, c * P + P)
                                mm = three(nc, ps[:, c, :], ys_h[:, f, ch], ys_l[:, f, ch], flat(sh.wh, n, kk),
                                           flat(sh.wl, n, kk), f == 0, f == 7, skip_group_check=True)
                        mm.then_inc(sem["unit_done"], 1)
                    turn_out(AHEADS - 1)

                    pe.wait_ge(sem["hy_done"], HYC)
                    pe.wait_ge(sem["pool_done"], PC)
                    pe.wait_ge(sem["att_done"], AHEADS)
                    for m in range(C8):
                        if m >= 4:
                            pe.wait_ge(sem["z_ready"], m - 3)
                        unit(ps[:, m % 4, :], V_OUT + m, m % 2, mix_h, mix_l)
                    ln1[0](pe, nc)

                    pe.wait_ge(sem["router_ready"], 1)
                    for t in range(4):
                        tok = slice(t * P, t * P + P)
                        for k in range(C8):
                            if t == 0:
                                pe.wait_ge(sem["x_ready"], k + 1)
                            mm = three(nc, ps[:, 6, t * 20:t * 20 + 20], xh[:, k, tok], xl[:, k, tok],
                                       router_h[:, k * 20:k * 20 + 20], router_l[:, k * 20:k * 20 + 20], k == 0, k == C8 - 1)
                    mm.then_inc(sem["route_mm"], 1)
                    for m in range(C8):
                        if m >= 4:
                            pe.wait_ge(sem["pg_sig"], m - 3)
                        unit(ps[:, m % 4, :], V_PLEG + m, m % 2)
                    pe.wait_ge(sem["pt_lo"], 1)
                    for m in range(C8):
                        n = V_PLEP + m // 4
                        if m % 4 == 0:
                            pe.wait_ge(sem["w_split"], n + 1)
                        if m < 4:
                            pe.wait_ge(sem["pg_sig"], C8)
                        else:
                            pe.wait_ge(sem["pp_done"], m - 3)
                        for k in range(2):
                            b_ = (m % 4) * 2 + k
                            mm = three(nc, ps[:, m % 4, :], sh.wh[:, n % 2, b_, :], sh.wl[:, n % 2, b_, :],
                                       pT_h[:, k, :], pT_l[:, k, :], k == 0, k == 1)
                        mm.then_inc(sem["unit_done" if m % 4 == 3 else "dft_mm"], 1)
                    pe.wait_ge(sem["gates"], 1)
                    for t in range(4):
                        mm = T.transpose(ps[0:EXPERTS, 7, t * P:t * P + P], rtr[:, 11, t, 0:16], ident)
                    mm.then_inc(sem["gt_mm"], 1)
                    pe.wait_ge(sem["pp_done"], C8)
                    for part in range(2):
                        with pe.Fori(0, HALF // 2) as i:
                            for e in range(2):
                                for f in range(EC):
                                    pe.wait_ge(sem["ex_done"], i * 4 + (part * HALF * EC + 2 * e + f + 1))
                                    for half in range(2):
                                        unit(ps[:, 2 * f + half, :], i * 8 + (V_EXP[part] + 4 * e + 2 * f + half), half)
                                    if f == 0:
                                        pe.wait_ge(sem["gm_ready"], i * 2 + (part * HALF + e + 1))
                                        T.matmul(ps[:, 4 + e, :], ones[0:EXPERTS, :], gm[:, e, :], start=True, stop=True
                                                 ).then_inc(sem["g_mm"], 1)
                        pe.wait_ge(sem["ex_done"], (part + 1) * HALF * EC + 2)
                        with pe.Fori(0, C8 // 2) as i:
                            for m in range(2):
                                pe.wait_ge(sem["down_evac"], i * 2 + (part * C8 + m + 1))
                                for q in range(DOWN_HALF):
                                    unit(ps[:, 6 + m, :], i * 2 * DOWN_HALF + (V_DOWN[part] + m * DOWN_HALF + q), q % 2,
                                         act_h[:, q * 8:q * 8 + 8, :], act_l[:, q * 8:q * 8 + 8, :],
                                         first=q == 0, last=q == DOWN_HALF - 1)
                    ln2[0](pe, nc)

                @block.scalar
                def _(act):
                    A = nc.scalar.activation
                    act.sem_inc(sem["proj_evac2"], 4)
                    act.wait_ge(sem["par_in2"], 16)

                    def hy_tile(u):
                        act.wait_ge(sem["unit_done"], SPLIT + V_HY + u + 1)
                        A(hy[:, u, :], ps[:, u % 4, :], ACT.Identity, scale=col("hw", 3 * HYC + u), bias=col("hb", u)
                          ).then_inc(sem["hy_tap"], 1)
                        act.wait_ge(sem["hy_ready"], u + 1)
                        act.sem_inc(sem["proj_evac2"], 1)

                    def filter_sin(n):
                        act.wait_ge(sem[f"ang{n + 1}"], 1)
                        A(hid[0:FH, n, :], hid[0:FH, n, :], ACT.Sin).then_inc(sem[f"sin{n + 1}"], 1)

                    act.wait_ge(sem["pool_zero"], 1)
                    for n in range(PC):
                        act.wait_ge(sem["unit_done"], SPLIT + V_POOL + n + 1)
                        A(pool[:, n, PADW:PADW + S], ps[:, 4 + n, :], ACT.Copy).then_inc(sem["pool_in"], 1)
                    filter_sin(0)
                    for u in range(3 * HYC):
                        hy_tile(u)
                    act.wait_ge(sem["lam_mm"], 1)
                    A(lamt[:, 2:4], ps[:, 7, 0:2], ACT.Exp).then_inc(sem["lam_exp"], 1)
                    for n in range(2 * AC):
                        u = 3 * HYC + n
                        act.wait_ge(sem["unit_done"], SPLIT + V_QK + n + 1)
                        A(qk[:, n, :], ps[:, u % 4, :], ACT.Copy).then_inc(sem["proj_evac2"], 1)
                        if n == 4:
                            filter_sin(1)
                    for c in range(HYC):
                        act.wait_ge(sem["vt_mm"], c + 1)
                        A(rhs3_h[:, :, HW + c * P:HW + c * P + P], ps[:, 6 + c, :].rearrange("p (t e) -> p t e", e=P), ACT.Copy
                          ).then_inc(sem["vt_hi"], 1)
                    act.wait_ge(sem["unit_done"], SPLIT + V_DFT)
                    for t in range(4):
                        A(v4[:, t, :], ps[:, t, :], ACT.Copy).then_inc(sem["v_ready2"], 1)
                    act.wait_ge(sem["kf_done"], 8)
                    A(filt[:, :, :, :], filt[:, :, :, :], ACT.Square).then_inc(sem["sqk"], 1)
                    for n in range(2 * NF):
                        if n % 2:
                            act.wait_ge(sem["unit_done"], SPLIT + V_DFT + n // 2 + 1)
                        else:
                            act.wait_ge(sem["dft_mm"], n // 2 + 1)
                        A(spec[:, n, :], ps[:, n % 4, :], ACT.Copy).then_inc(sem["spec_evac"], 1)
                    act.wait_ge(sem["norm_mm"], 1)
                    A(lamt[:, 6:8], ps[:, 6, 0:2], ACT.Sqrt, bias=eps[:, 1:2]).then_inc(sem["nstd"], 1)

                    def expo(n):
                        for c in range(2):
                            act.wait_ge(sem["nmax2"], 2 * n + c + 1)
                            if n >= 2:
                                act.wait_ge(sem["t_mm2"], n - 1)
                            A(pexp[:, n % 2, c, :], ps[:, 2 * (n % 2) + c, :], ACT.Exp, scale=0.125,
                              bias=small[:, n % 2, 2 + c:3 + c], accum_out=small[:, n % 2, 4 + c:5 + c]
                              ).then_inc(sem["p_ready2"], 1)

                    def evac_at(n):
                        act.wait_ge(sem["t_mm2"], n + 1)
                        if n >= 2:
                            act.wait_ge(sem["o_mm2"], n - 1)
                        A(at[:, n % 2, :], ps[:, 4 + n % 2, :], ACT.Copy).then_inc(sem["at_ready"], 1)

                    def squares(n):
                        h, b = n // 4, n % 4
                        act.wait_ge(sem["o_sc"], n + 1)
                        A(hid[:, 0, 0:P], osb[:, h % 2, b, :], ACT.Square, accum_out=headv[:, h % 2, b:b + 1]
                          ).then_inc(sem["o_sq"], 1)
                        act.wait_ge(sem["o_sq"], n + 1)
                        if b == 3:
                            A(headv[:, h % 2, 4:8], headv[:, h % 2, 0:4], ACT.Sqrt, scale=1.0 / P, bias=eps[:, 0:1]
                              ).then_inc(sem["o_std"], 1)

                    expo(0)
                    for n in range(4 * AHEADS):
                        if n + 1 < 4 * AHEADS:
                            expo(n + 1)
                        evac_at(n)
                        if n >= 2:
                            squares(n - 2)
                    squares(4 * AHEADS - 2)
                    squares(4 * AHEADS - 1)
                    act.wait_ge(sem["unit_done"], SPLIT + V_PLEG)
                    act.dma_start(pT[:, :, :], d_p[ds(layer, 1)].rearrange("a p k t -> p (a k) t")).then_inc(sem["p_in"], 16)
                    ln1[2](act, nc)
                    act.wait_ge(sem["p_in"], 16)
                    A(pT_h[:, :, :], pT[:, :, :], ACT.Copy).then_inc(sem["pt_hi"], 1)

                    for m in range(C8):
                        act.wait_ge(sem["unit_done"], SPLIT + V_PLEG + m + 1)
                        A(spec[:, m, :], ps[:, m % 4, :], ACT.Sigmoid, bias=col("ple_b", m)).then_inc(sem["pg_sig"], 1)
                        if m == 3:
                            act.wait_ge(sem["r_a"], 1)
                            A(rtr[:, 1, :, 0:4], rtr[:, 1, :, 0:4], ACT.Exp).then_inc(sem["r_ea"], 1)
                            act.wait_ge(sem["r_b"], 1)
                            A(rtr[:, 6, :, 0:1], rtr[:, 6, :, 0:1], ACT.Exp).then_inc(sem["r_eb"], 1)
                    act.wait_ge(sem["gt_mm"], 1)
                    A(gT[:, :], ps[0:EXPERTS, 7, :], ACT.Copy).then_inc(sem["gt_ready"], 1)
                    for part in range(2):
                        with act.Fori(0, HALF // 2) as i:
                            for n in range(4):
                                f = n % 2
                                act.wait_ge(sem["ex_done"], i * 4 + (part * HALF * EC + n + 1))
                                act.wait_ge(sem["unit_done"], SPLIT + i * 8 + (V_EXP[part] + 2 * n + 1))
                                A(hid[:, f, :], ps[:, 2 * f, :], ACT.Silu).then_inc(sem["silu"], 1)
                    ln2[2](act, nc)

                @block.vector
                def _(dve):
                    V = nc.vector
                    step = Count(sem["dve_step2"])

                    def do(ins):
                        step.step(dve, ins)

                    def split(v, hi, lo, done=None):
                        do(V.tensor_scalar(hi, v, 1.0, None, ALU.mult))
                        ins = V.tensor_tensor(lo, v, hi, ALU.subtract)
                        if done:
                            ins.then_inc(sem[done], 1)
                        else:
                            do(ins)

                    dve.sem_inc(sem["ex_done"], 2)
                    dve.sem_inc(sem["down_evac"], 2)
                    dve.wait_ge(sem["par_in2"], 16)
                    V.tensor_tensor(lamt[:, 0:2], col("lq1", 0, 2), col("lk1", 0, 2), ALU.mult).then_inc(sem["lam_prod"], 1)

                    def angles(n, bank):
                        dve.wait_ge(sem[f"f{n + 1}_mm"], 1)
                        r, a, k = hid[0:FH, n, :], tmp[0:FH, 0, :], tmp[0:FH, 1, :]
                        do(V.tensor_scalar(a, ps[0:FH, bank, :], col(f"fb{n + 1}", 0, 1, FH), col(f"fr{n + 1}", 0, 1, FH),
                                           ALU.add, ALU.mult))
                        reduce_angle(dve, nc, step, r, a, k)
                        dve.sem_inc(sem[f"ang{n + 1}"], 1)

                    def hy_taps(u):
                        dve.wait_ge(sem["hy_tap"], u + 1)
                        bank = ps[:, u % 4, :]
                        do(V.scalar_tensor_tensor(hy[:, u, 1:], bank[:, 0:S - 1], col("hw", u), hy[:, u, 1:], ALU.mult, ALU.add))
                        V.scalar_tensor_tensor(hy[:, u, 0:S - 1], bank[:, 1:], col("hw", 6 * HYC + u), hy[:, u, 0:S - 1],
                                               ALU.mult, ALU.add).then_inc(sem["hy_ready"], 1)

                    angles(0, 6)
                    def pooling(n):
                        dve.wait_ge(sem["pool_in"], n + 1)
                        src = pool[:, n, :]
                        cur, width, have, k = src, S + 2 * PADW, 1, 0
                        for half in range(2):
                            window = 2 ** (2 * n + half + 1)
                            while have < window:
                                out_, width = pw[:, k % 2, :], width - have
                                do(V.tensor_tensor(out_[:, 0:width], cur[:, 0:width], cur[:, have:have + width], ALU.add))
                                cur, have, k = out_, 2 * have, k + 1
                            lo = PADW - window // 2
                            rows = slice(64 * half, 64 * half + 64)
                            do(V.tensor_tensor(pacc[rows, n, 0:S], cur[rows, lo:lo + S], icnt[rows, n, :], ALU.mult))
                        V.tensor_tensor(pacc[:, n, 0:S], pacc[:, n, 0:S], src[:, PADW:PADW + S], ALU.subtract
                                        ).then_inc(sem["pool_y"], 1)

                    dve.wait_ge(sem["tab_in"], 64)
                    for u in range(3 * HYC):
                        hy_taps(u)
                        if u in (1, 3):
                            pooling(u // 2)
                    dve.wait_ge(sem["hy_ready"], 3 * HYC)
                    for c in range(HYC):
                        V.tensor_tensor(hy[:, 4 + c, :], hy[:, 4 + c, :], hy[:, 2 + c, :], ALU.mult).then_inc(sem["hy_v"], 1)
                    dve.wait_ge(sem["lam_exp"], 1)
                    do(V.tensor_tensor(lamt[:, 4:5], lamt[:, 3:4], lamt[:, 2:3], ALU.subtract))
                    do(V.tensor_scalar(lamt[:, 4:5], lamt[:, 4:5], col("lam0"), None, ALU.subtract))
                    do(V.tensor_scalar(lamt[:, 5:6], col("sub_g"), col("lam1"), None, ALU.mult))
                    angles(1, 7)
                    def window(t):
                        dve.wait_ge(sem["filt_mm"], t + 1)
                        do(V.tensor_tensor(filt[:, t, 0, :], ps[:, 6 + t % 2, 0:HW], win[:, t, :], ALU.mult))
                        V.tensor_tensor(filt[:, t, 1, :], ps[:, 6 + t % 2, HW:2 * HW], win[:, t, :], ALU.mult
                                        ).then_inc(sem["kf_win"], 1)

                    for n in range(2 * AC):
                        dve.wait_ge(sem["rot_mm"], n + 1)
                        do(V.tensor_tensor(tmp[:, n % 2, :], ps[:, 4 + n % 2, :], trig[:, 1, :], ALU.mult))
                        do(V.tensor_tensor(qk[:, n, :], qk[:, n, :], trig[:, 0, :], ALU.mult))
                        V.tensor_tensor(qk[:, n, :], qk[:, n, :], tmp[:, n % 2, :], ALU.add).then_inc(sem["qk_ready"], 1)
                        if n >= 4:
                            window(n - 4)
                    dve.wait_ge(sem["qk_ready"], 2 * AC)
                    dve.wait_ge(sem["kf_win"], 4)
                    do(V.memset(filt[0:1, 0, 1, :], 0.0))
                    for t in range(4):
                        for w, op in ((0, ALU.add), (2, ALU.subtract)):
                            v = tmp[:, t % 2, w * P:w * P + HW]
                            do(V.tensor_tensor(v, filt[:, t, 0, :], filt[:, t, 1, :], op))
                            split(v, rhs3_h[:, t, w * HW:w * HW + HW], rhs3_l[:, t, w * HW:w * HW + HW], "kf_done")
                            dve.wait_ge(sem["kf_done"], 2 * t + w // 2 + 1)
                    for c in range(HYC):
                        dve.wait_ge(sem["vt_hi"], c + 1)
                        cols = slice(HW + c * P, HW + c * P + P)
                        V.tensor_tensor(rhs3_l[:, :, cols], ps[:, 6 + c, :].rearrange("p (t e) -> p t e", e=P), rhs3_h[:, :, cols],
                                        ALU.subtract).then_inc(sem["vt_ready"], 1)

                    def spectrum():
                        dve.wait_ge(sem["spec_evac"], 2 * NF)
                        kr, vr = spec[:, 0:NF, 0:HW], spec[:, 0:NF, HW:2 * HW]
                        vs, ks = spec[:, NF:2 * NF, 0:HW], spec[:, NF:2 * NF, HW:2 * HW]
                        for part, (a, b_, op) in enumerate(((kr, ks, ALU.subtract), (ks, kr, ALU.add))):
                            do(V.tensor_tensor(yfull[:, :, :], vr, a, ALU.mult))
                            do(V.tensor_tensor(ytmp[:, :, :], vs, b_, ALU.mult))
                            do(V.tensor_tensor(yfull[:, :, :], yfull[:, :, :], ytmp[:, :, :], op))
                            rows = slice(part * NF, part * NF + NF)
                            split(yfull[:, :, :], ys_h[:, rows, :], ys_l[:, rows, :], "ys_ready")
                            dve.wait_ge(sem["ys_ready"], part + 1)
                        dve.wait_ge(sem["nstd"], 1)
                        do(V.reciprocal(lamt[:, 6:8], lamt[:, 6:8]))

                    for n in range(PC):
                        dve.wait_ge(sem["poolm_mm"], n + 1)
                        do(V.tensor_scalar(tmp[:, n, :], ps[:, 4 + n, :], col("pool_b", n), col("pool_s", n), ALU.add, ALU.mult))
                        split(tmp[:, n, :], mix_h[:, HYC + AC + n, :], mix_l[:, HYC + AC + n, :], "pool_done")

                    def row_max(n):
                        for c in range(2):
                            dve.wait_ge(sem["s_mm2"], 2 * n + c + 1)
                            sm = small[:, n % 2, :]
                            do(V.reduce_max(sm[:, c:c + 1], ps[:, 2 * (n % 2) + c, :], AXX))
                            V.tensor_scalar(sm[:, 2 + c:3 + c], sm[:, c:c + 1], -0.125, None, ALU.mult).then_inc(sem["nmax2"], 1)

                    def difference(n):
                        dve.wait_ge(sem["p_ready2"], 2 * n + 2)
                        sm = small[:, n % 2, :]
                        do(V.reciprocal(sm[:, 6:8], sm[:, 4:6]))
                        do(V.tensor_scalar(sm[:, 8:9], sm[:, 7:8], sm[:, 4:5], lamt[:, 4:5], ALU.mult, ALU.mult))
                        do(V.tensor_copy(headv[:, n // 4 % 2, 8 + n % 4:9 + n % 4], sm[:, 6:7]))
                        V.scalar_tensor_tensor(pexp[:, n % 2, 0, :], pexp[:, n % 2, 1, :], sm[:, 8:9], pexp[:, n % 2, 0, :],
                                               ALU.mult, ALU.add).then_inc(sem["a_ready2"], 1)

                    def scale_out(n):
                        h, b = n // 4, n % 4
                        dve.wait_ge(sem["o_mm2"], n + 1)
                        V.tensor_scalar(osb[:, h % 2, b, :], ps[:, 6, 0:P], headv[:, h % 2, 8 + b:9 + b], None, ALU.mult
                                        ).then_inc(sem["o_sc"], 1)

                    def norm_out(h):
                        dve.wait_ge(sem["o_std"], h + 1)
                        do(V.reciprocal(headv[:, h % 2, 4:8], headv[:, h % 2, 4:8]))
                        V.tensor_tensor(osb[:, h % 2, :, :], osb[:, h % 2, :, :],
                                        headv[:, h % 2, 4:8].unsqueeze(2).to_broadcast([P, 4, P]), ALU.mult
                                        ).then_inc(sem["o_nrm"], 1)

                    def att_out(h):
                        dve.wait_ge(sem["ot_mm"], h + 1)
                        do(V.tensor_scalar(tmp[:, h % 2, :], ps[:, 7, :], lamt[:, 5:6], None, ALU.mult))
                        split(tmp[:, h % 2, :], mix_h[:, HYC + h, :], mix_l[:, HYC + h, :], "att_done")

                    row_max(0)
                    for n in range(4 * AHEADS):
                        if n + 1 < 4 * AHEADS:
                            row_max(n + 1)
                        difference(n)
                        if n >= 2:
                            scale_out(n - 2)
                        if n >= 5 and n % 4 == 1:
                            norm_out((n - 5) // 4 )
                        if n >= 7 and n % 4 == 3:
                            att_out((n - 7) // 4)
                        if n == 2:
                            spectrum()
                    scale_out(4 * AHEADS - 2)
                    scale_out(4 * AHEADS - 1)
                    norm_out(AHEADS - 1)
                    dve.wait_ge(sem["att_done"], AHEADS - 1)
                    dve.wait_ge(sem["unit_done"], SPLIT + V_OUT)
                    for c in range(HYC):
                        do(V.tensor_scalar(tmp[:, c, :], hy[:, 4 + c, :], col("bias", c), None, ALU.mult))
                        do(V.scalar_tensor_tensor(tmp[:, c, :], ps[:, c, :], lamt[:, 6 + c:7 + c], tmp[:, c, :], ALU.mult, ALU.add))
                        do(V.tensor_tensor(tmp[:, c, :], tmp[:, c, :], hy[:, c, :], ALU.mult))
                        split(tmp[:, c, :], mix_h[:, c, :], mix_l[:, c, :], "hy_done")
                    dve.wait_ge(sem["hy_done"], HYC)
                    att_out(AHEADS - 1)
                    split(col("router", 0, C8 * 20), router_h[:, :], router_l[:, :], "router_ready")

                    for m in range(C8):
                        dve.wait_ge(sem["unit_done"], SPLIT + V_OUT + m + 1)
                        do(residual_chunk(dve, nc, do, sem, sh, m, ps[:, m % 4, :], stat))
                        if m:
                            dve.wait_ge(sem["z_ready"], m)
                        sum_chunk(dve, nc, do, sem, sh, m, stat)
                    dve.wait_ge(sem["z_ready"], C8)
                    ln1[1](dve, nc)

                    dve.wait_ge(sem["pt_hi"], 1)
                    V.tensor_tensor(pT_l[:, :, :], pT[:, :, :], pT_h[:, :, :], ALU.subtract).then_inc(sem["pt_lo"], 1)
                    R = [rtr[:, n, :, :] for n in range(12)]

                    def bc(a, n):
                        return a.to_broadcast([P, 4, n])

                    def first_max(src, n, mx, oh):
                        do(V.reduce_max(mx, src, AXX))
                        do(V.tensor_tensor(oh, src, bc(mx, n), ALU.is_equal))
                        for j in range(n):
                            if j:
                                do(V.tensor_tensor(oh[:, :, j:j + 1], oh[:, :, j:j + 1], R[10][:, :, 4:5], ALU.is_gt))
                                do(V.tensor_tensor(R[10][:, :, 4:5], R[10][:, :, 4:5], oh[:, :, j:j + 1], ALU.add))
                            else:
                                do(V.tensor_copy(R[10][:, :, 4:5], oh[:, :, 0:1]))

                    dve.wait_ge(sem["route_mm"], 1)
                    rb = col("rbias", 0, 20).unsqueeze(1).to_broadcast([P, 4, 20])
                    do(V.tensor_tensor(R[0], ps[:, 6, 0:80].rearrange("p (t n) -> p t n", n=20), rb, ALU.add))
                    gl, fl = R[0][:, :, 0:4], R[0][:, :, 4:20]
                    ohg = R[2][:, :, 0:4]
                    first_max(gl, 4, R[2][:, :, 4:5], ohg)
                    V.tensor_tensor(R[1][:, :, 0:4], gl, bc(R[2][:, :, 4:5], 4), ALU.subtract).then_inc(sem["r_a"], 1)
                    for gidx in range(GROUPS):
                        do(V.tensor_tensor(R[3][:, :, 4 * gidx:4 * gidx + 4], fl[:, :, 4 * gidx:4 * gidx + 4],
                                           bc(ohg[:, :, gidx:gidx + 1], 4), ALU.mult))
                    fs = R[4][:, :, 0:4]
                    do(V.tensor_tensor(fs, R[3][:, :, 0:4], R[3][:, :, 4:8], ALU.add))
                    do(V.tensor_tensor(fs, fs, R[3][:, :, 8:12], ALU.add))
                    do(V.tensor_tensor(fs, fs, R[3][:, :, 12:16], ALU.add))
                    m1, oh1 = R[4][:, :, 8:9], R[5][:, :, 0:4]
                    first_max(fs, 4, m1, oh1)
                    fs2 = R[5][:, :, 4:8]
                    do(V.scalar_tensor_tensor(fs2, oh1, -1e30, fs, ALU.mult, ALU.add))
                    m2_, oh2 = R[5][:, :, 12:13], R[5][:, :, 8:12]
                    first_max(fs2, 4, m2_, oh2)
                    V.tensor_tensor(R[6][:, :, 0:1], m2_, m1, ALU.subtract).then_inc(sem["r_b"], 1)
                    dve.wait_ge(sem["r_ea"], 1)
                    do(V.reduce_sum(R[7][:, :, 0:1], R[1][:, :, 0:4], AXX))
                    dve.wait_ge(sem["r_eb"], 1)
                    do(V.tensor_scalar(R[7][:, :, 1:2], R[6][:, :, 0:1], 1.0, None, ALU.add))
                    do(V.tensor_tensor(R[7][:, :, 2:3], R[7][:, :, 1:2], R[7][:, :, 0:1], ALU.mult))
                    do(V.reciprocal(R[7][:, :, 3:4], R[7][:, :, 2:3]))
                    do(V.tensor_tensor(R[7][:, :, 4:5], R[7][:, :, 3:4], R[6][:, :, 0:1], ALU.mult))
                    do(V.tensor_tensor(oh1, oh1, bc(R[7][:, :, 3:4], 4), ALU.mult))
                    do(V.tensor_tensor(oh2, oh2, bc(R[7][:, :, 4:5], 4), ALU.mult))
                    do(V.tensor_tensor(oh1, oh1, oh2, ALU.add))
                    for gidx in range(GROUPS):
                        ins = V.tensor_tensor(R[11][:, :, 4 * gidx:4 * gidx + 4], oh1, bc(ohg[:, :, gidx:gidx + 1], 4), ALU.mult)
                        if gidx < GROUPS - 1:
                            do(ins)
                        else:
                            ins.then_inc(sem["gates"], 1)
                    for m in range(C8):
                        if m % 4 == 3:
                            dve.wait_ge(sem["unit_done"], SPLIT + V_PLEP + m // 4 + 1)
                        else:
                            dve.wait_ge(sem["dft_mm"], NF + m // 4 * 3 + m % 4 + 1)
                        V.tensor_tensor(spec[:, m, :], spec[:, m, :], ps[:, m % 4, :], ALU.mult).then_inc(sem["pp_done"], 1)
                    dve.wait_ge(sem["gt_ready"], 1)

                    def mask_gate(e, slot):
                        one = cst[0:EXPERTS, e:e + 1] if isinstance(e, int) else cst[0:EXPERTS, ds(e, 1)]
                        V.tensor_scalar(gm[:, slot, :], gT[:, :], one, None, ALU.mult).then_inc(sem["gm_ready"], 1)

                    for part in range(2):
                        e0 = part * HALF
                        with dve.Fori(0, HALF // 2) as i:
                            step.enter(i, 4 * 3)
                            for n in range(4):
                                e, f = n // 2, n % 2
                                if n == 0:
                                    dve.wait_ge(sem["g_mm"], HEAD + i * 2 + e0)
                                    mask_gate(i * 2 + e0, 0)
                                    mask_gate(i * 2 + (e0 + 1), 1)
                                dve.wait_ge(sem["silu"], i * 4 + (e0 * EC + n + 1))
                                dve.wait_ge(sem["unit_done"], SPLIT + i * 8 + (V_EXP[part] + 2 * n + 2))
                                h = hid[:, f, :]
                                do(V.tensor_tensor(h, h, ps[:, 2 * f + 1, :], ALU.mult))
                                dve.wait_ge(sem["g_mm"], HEAD + i * 2 + (e0 + e + 1))
                                do(V.tensor_tensor(h, h, ps[:, 4 + e, :], ALU.mult))
                                do(V.tensor_scalar(act_h[:, ds(i * 4 + n, 1), :], hid[:, f:f + 1, :], 1.0, None, ALU.mult))
                                V.tensor_tensor(act_l[:, ds(i * 4 + n, 1), :], hid[:, f:f + 1, :], act_h[:, ds(i * 4 + n, 1), :],
                                                ALU.subtract).then_inc(sem["ex_done"], 1)
                            step.leave(HALF // 2)
                        for m in range(C8):
                            dve.wait_ge(sem["unit_done"], SPLIT + V_DOWN[part] + DOWN_HALF * (m + 1))
                            zm, bank = z[:, m, :], ps[:, 6 + m % 2, :]
                            if part == 0:
                                V.scalar_tensor_tensor(zm, zm, ALPHA, bank, ALU.mult, ALU.add).then_inc(sem["down_evac"], 1)
                                dve.wait_ge(sem["down_evac"], 2 + m + 1)
                                do(V.tensor_tensor(zm, zm, spec[:, m, :], ALU.add))
                            else:
                                V.tensor_tensor(zm, zm, bank, ALU.add).then_inc(sem["down_evac"], 1)
                                dve.wait_ge(sem["down_evac"], 2 + C8 + m + 1)
                                if m:
                                    dve.wait_ge(sem["z_ready"], C8 + m)
                                sum_chunk(dve, nc, do, sem, sh, m, stat)
                    dve.wait_ge(sem["z_ready"], 2 * C8)
                    ln2[1](dve, nc)

            nc.all_engine_barrier(sems_to_clear=sem_range)


def build(nc, d, out, only=0):
    with ExitStack() as ctx:
        ps = ctx.enter_context(nc.psum_tensor("ps", [P, 8, S], F32))
        stored = ctx.enter_context(nc.semaphore("stored"))
        mem = Memory(nc)
        sh = Shared(nc, mem, ps)
        if only != 2:
            first_block(nc, mem, sh, d["x"], d["pos"], d["cst"], d["w1"], d["gw"], d["par1"])
        if only == 2:
            with nc.Block() as block:
                @block.sync
                def _(sp):
                    sp.dma_start(sh.z[:, :, :], d["x"]).then_inc(stored, 16)
                    sp.wait_ge(stored, 16)
            nc.all_engine_barrier(sems_to_clear=range(stored.num, stored.num + 1))
        if only != 1:
            second_block(nc, mem, sh, d["cst2"], d["tab"], d["w2"], d["par2"], d["p"])
        with nc.Block() as block:
            @block.sync
            def _(sp):
                sp.dma_start(out, sh.z[:, :, :]).then_inc(stored, 16)
                sp.wait_ge(stored, 16)


def _blocks(w):
    k, m = w.shape
    return w.reshape(k // P, P, m // P, P).transpose(2, 1, 0, 3)


def _units(w):
    b = _blocks(w)
    m, p, k, n = b.shape
    return b.reshape(m, p, k // 8, 8 * n).transpose(0, 2, 1, 3).reshape(m * (k // 8), p, 8 * n)


def _cols(v):
    return np.asarray(v).reshape(-1, P).T


def _swap(w):
    h = w.shape[-1] // 2
    return np.concatenate([w[..., h:], w[..., :h]], -1)


def _first_layout(a):
    out = {}
    w1, gw, par = [], [], []
    for l in range(DEPTH):
        w_in = a["w_in"][l]
        q0 = 2 * D
        kv0 = q0 + QC * P
        r0 = kv0 + KVC * P
        ga0 = r0 + ROPE
        gb0 = ga0 + D
        wr = w_in[:, r0:ga0]
        tile = np.concatenate([np.zeros((D, 64), np.float32), wr, _swap(wr)], 1)
        order = [w_in[:, kv0:r0], tile, w_in[:, q0:kv0], w_in[:, 0:D], w_in[:, D:2 * D], w_in[:, ga0:gb0], w_in[:, gb0:]]
        w1.append(_units(np.concatenate(order, 1)))
        uq = a["w_uq"][l].reshape(QC, P, HEADS, NOPE + ROPE)
        uq = np.concatenate([uq, _swap(uq[..., NOPE:])], -1)
        ukv = a["w_ukv"][l].reshape(KVC, P, HEADS, NOPE + VH)
        w1.append(ukv[..., NOPE:].reshape(KVC, P, HEADS * VH))
        for p in range(PAIRS):
            bl = [uq[c, :, 2 * p + h] for h in range(2) for c in range(QC)]
            bl += [ukv[c, :, 2 * p:2 * p + 2, :NOPE].reshape(P, P) for c in range(KVC)]
            w1.append(np.concatenate(bl, 1)[None])
            tile = np.zeros((P, 2, P), np.float32)
            for n, g in enumerate(("gx_w", "ga_w")):
                tile[:64, n, :64], tile[64:, n, 64:] = a[g][l][2 * p], a[g][l][2 * p + 1]
            gw.append(tile.reshape(P, 2 * P))
        w1.append(_units(a["w_out"][l]))
        up = _units(a["w_up"][l]).reshape(2, FC, P, 1024).transpose(1, 0, 2, 3).reshape(2 * FC, P, 1024)
        w1 += [up, _units(a["w_down"][l])]
        par.append(np.concatenate([_cols(a[n][l]) for n in (
            "conv_w", "conv_b", "gx_b", "ga_b", "lru_lambda", "q_norm_g", "kv_norm_g", "ln1_g", "ln1_b", "ln2_g",
            "ln2_b", "ffn_conv_w", "ffn_conv_b")], 1))
    out["w1"] = np.concatenate(w1, 0)
    out["gw"] = np.stack(gw)
    out["par1"] = np.stack(par)
    out["x"] = np.asarray(a["x"])[0].T.reshape(C8, P, S).transpose(1, 0, 2)
    out["pos"] = np.repeat(np.asarray(a["positions"]).reshape(1, S), P, 0)
    cst = np.zeros((P, NCST), np.float32)
    cst[:, :P] = np.eye(P)
    cst[:, P:2 * P] = np.where(np.arange(P)[None, :] > np.arange(P)[:, None], -1e30, 0.0)
    half = ROPE // 2
    cst[:, 2 * P] = 10000.0 ** (-np.arange(P) % half * 0.0 - (np.arange(P) % half) * 2.0 / ROPE)
    cst[:, 2 * P + 1] = np.where((np.arange(P) >= 96) & (np.arange(P) < 96 + half), -1.0, 1.0)
    out["cst"] = cst
    return out


def _rows(v, rows=P):
    v = np.asarray(v, np.float32)
    v = v.reshape(v.shape[0], -1)
    return np.concatenate([v, np.zeros((P - v.shape[0], v.shape[1]), np.float32)], 0)


def _wide_units(w):
    return w.reshape(-1, 2, P, S).transpose(0, 2, 1, 3).reshape(-1, P, 2 * S)


def _tables():
    t = np.arange(S)
    f = np.arange(S) + 0.5
    ang = 2 * np.pi * np.outer(t, f) / (2 * S)
    fwd = np.concatenate([np.cos(ang), np.sin(ang)], 1)
    b = fwd.reshape(4, P, 2 * NF, P).transpose(2, 1, 0, 3)
    dft = b.reshape(NF, 2, P, 4 * P).transpose(0, 2, 1, 3).reshape(NF, P, 8 * P)
    idft = _wide_units(np.concatenate([np.cos(ang).T, np.sin(ang).T], 0) / S)
    cst = {}
    cst["ident"] = np.eye(P)
    perm = np.zeros((P, P))
    rd = 64 // 4
    cos, sin = np.ones((P, S)), np.zeros((P, S))
    inv = (500000.0 ** (-np.arange(0, rd, 2) / rd)).astype(np.float32)
    a = (t.astype(np.float32)[None, :] * inv[:, None]).astype(np.float64)
    for c in (0, 64):
        for i in range(rd // 2):
            perm[c + i + rd // 2, c + i] = -1.0
            perm[c + i, c + i + rd // 2] = 1.0
            for r in (c + i, c + i + rd // 2):
                cos[r], sin[r] = np.cos(a[i]), np.sin(a[i])
    cst["perm"], cst["trig"] = perm, np.concatenate([cos, sin], 1)
    tt = np.linspace(0.0, 1.0, S, dtype=np.float32)
    wp = (np.float32(2 * np.pi) * t.astype(np.float32) / np.float32(S)).astype(np.float32)
    bands = np.linspace(1e-4, (FEMB - 1) // 2 - 1, (FEMB - 1) // 2, dtype=np.float32)
    za = (wp[:, None] * bands[None, :]).astype(np.float64)
    cst["z"] = _rows(np.concatenate([tt[:, None], np.cos(za), -np.sin(za)], 1).T)
    deltas = np.linspace(np.log(1e-2) / 1.5, np.log(1e-2) / 0.3, HW)
    win = np.exp(-tt.astype(np.float64)[:, None] * np.abs(deltas)[None, :])
    cst["win"] = win.reshape(4, P, HW).transpose(1, 0, 2).reshape(P, 4 * HW)
    icnt = np.zeros((P, PC, S))
    for g, w in enumerate((2, 4, 8, 16)):
        lo, hi = np.clip(t - w // 2, 0, S - 1), np.clip(t + w // 2 - 1, 0, S - 1)
        icnt[64 * (g % 2):64 * (g % 2) + 64, g // 2] = 1.0 / (hi - lo + 1)
    cst["icnt"] = icnt.reshape(P, PC * S)
    return dft, idft, cst


def _second_layout(a):
    out = {}
    dft, idft, cst = _tables()
    cst["ln0_g"], cst["ln0_b"] = _cols(a["ln0_g_2"]), _cols(a["ln0_b_2"])
    out["tab"] = np.concatenate([cst[n] for n in TAB], 1).astype(np.float32)
    out["cst2"] = np.concatenate([cst[n] for n in CST2], 1).astype(np.float32)
    w2, par = [], []
    for l in range(DEPTH):
        w_in = a["w_in_2"][l]
        q0 = 3 * HW
        v0 = q0 + 2 * AW
        p0 = v0 + AW
        w2 += [_units(w_in[:, p0:]), _units(w_in[:, :v0]), _wide_units(w_in[:, v0:p0]),
               dft.astype(np.float32), idft.astype(np.float32), _units(a["w_out_2"][l]), _units(a["ple_wg_2"][l])]
        b = _blocks(a["ple_wp_2"][l])
        w2.append(b.reshape(2, 4, P, 2 * P).transpose(0, 2, 1, 3).reshape(2, P, 8 * P))
        ex = [np.stack([_units(a[n][l][e]) for n in ("moe_w1_2", "moe_w3_2")], 1).reshape(2 * EC, P, 8 * P)
              for e in range(EXPERTS)]
        for e in (0, HALF):
            w2 += ex[e:e + HALF] + [_units(a["moe_w2_2"][l][e:e + HALF].reshape(HALF * DE, D))]
        lam0 = 0.8 - 0.6 * np.exp(-0.3 * l)
        full = lambda v: np.full((P, 1), v, np.float32)
        pw = []
        for n in range(PC):
            m = np.zeros((P, P), np.float32)
            m[:64, :64], m[64:, 64:] = a["pool_w_2"][l][2 * n], a["pool_w_2"][l][2 * n + 1]
            pw.append(m)
        router = np.concatenate([a["moe_wgc_2"][l], a["moe_wgf_2"][l]], 1)
        parts = {
            "hw": _cols(a["hy_conv_w_2"][l]), "hb": _cols(a["hy_conv_b_2"][l]),
            "fb1": _rows(a["hy_fb1_2"][l]), "fr1": _rows(a["hy_freq1_2"][l]),
            "fb2": _rows(a["hy_fb2_2"][l]), "fr2": _rows(a["hy_freq2_2"][l]),
            "bias": _cols(a["hy_bias_2"][l]),
            "lq1": _rows(a["att_lq1_2"][l]), "lq2": _rows(a["att_lq2_2"][l]),
            "lk1": _rows(a["att_lk1_2"][l]), "lk2": _rows(a["att_lk2_2"][l]),
            "lam0": full(lam0), "lam1": full(1.0 - lam0), "sub_g": _cols(a["att_subln_g_2"][l]),
            "pool_b": _cols(a["pool_b_2"][l]), "pool_s": _cols(a["pool_scale_2"][l]),
            "ln1_g": _cols(a["ln1_g_2"][l]), "ln1_b": _cols(a["ln1_b_2"][l]),
            "ln2_g": _cols(a["ln2_g_2"][l]), "ln2_b": _cols(a["ln2_b_2"][l]), "ple_b": _cols(a["ple_bg_2"][l]),
            "rbias": np.repeat(np.concatenate([a["moe_bgc_2"][l], a["moe_bgf_2"][l]])[None], P, 0),
            "fw1": _rows(a["hy_fw1_2"][l]), "fw2": _rows(a["hy_fw2_2"][l]), "fw3": _rows(a["hy_fw3_2"][l]),
            "poolw": np.concatenate(pw, 1),
            "router": router.reshape(C8, P, 20).transpose(1, 0, 2).reshape(P, C8 * 20),
        }
        par.append(np.concatenate([parts[n] for n in PAR2], 1))
    out["w2"] = np.concatenate(w2, 0)
    out["par2"] = np.stack(par)
    out["p"] = a["p_2"][:, 0].transpose(0, 2, 1).reshape(DEPTH, 2, P, S).transpose(0, 2, 1, 3)
    return out


def _layout(inputs):
    a = {k: np.asarray(v) for k, v in inputs.items()}
    out = {**_first_layout(a), **_second_layout(a)}
    return {k: np.ascontiguousarray(v) for k, v in out.items()}


def kernel(**inputs):
    import concourse.bacc as bacc
    from concourse.bass_utils import run_bass_kernel_spmd

    nc = bacc.Bacc("TRN2", target_bir_lowering=False, num_devices=1)
    arrays = _layout(inputs)
    d = {k: nc.dram_tensor("in_" + k, v.shape, mybir.dt.from_np(v.dtype), kind="ExternalInput").ap()
         for k, v in arrays.items()}
    out = nc.dram_tensor("out", (P, C8, S), F32, kind="ExternalOutput").ap()
    build(nc, d, out)
    r = run_bass_kernel_spmd(nc, [{"in_" + k: v for k, v in arrays.items()}], core_ids=[0])
    y = r.results[0]["out"]
    return np.ascontiguousarray(y.transpose(1, 0, 2).reshape(D, S).T).reshape(1, S, D)
```

```python
from contextlib import ExitStack

import numpy as np

import concourse.bass as bass
from concourse import mybir

F32 = mybir.dt.float32
F32R = mybir.dt.float32r
I32 = mybir.dt.int32
ALU = mybir.AluOpType
ACT = mybir.ActivationFunctionType
AXX = mybir.AxisListType.X
ds = bass.ds

P = 128
S = 512
D = 1024
DEPTH = 2
HEAD = 1
C8 = D // P
ALPHA = float((2 * DEPTH) ** 0.25)

HEADS = 16
NOPE, ROPE, VH = 64, 32, 64
QC, KVC = 3, 2
FF = 3 * D
FC = FF // P
SCALE1 = float((NOPE + ROPE) ** -0.5)
EPS1 = 1e-6
PAIRS = HEADS // 2
RAW = 4
SPLIT = 2
SINGLE = 4
PROJ_UNITS = KVC + 1 + QC + 2 * C8
PER_PAIR = 3
OUT_UNITS = C8
UP_UNITS = 2 * FC
DOWN_PER = FC // 8
U_V = PROJ_UNITS
U_ATT = U_V + KVC
U_OUT = U_ATT + PER_PAIR * PAIRS
U_UP = U_OUT + OUT_UNITS
U_DOWN = U_UP + UP_UNITS
U1 = U_DOWN + DOWN_PER * C8

TWO_PI = 6.283185307179586
PI2_A = 6.28125
PI2_B = 0.0019350051879882812
PI2_C = TWO_PI - PI2_A - PI2_B
MAGIC = 12582912.0
PI_DOWN = 3.1415925


def columns(spec):
    at, out = 0, {}
    for name, n in spec:
        out[name] = (at, n)
        at += n
    return out, at


PAR1, NPAR1 = columns([("conv_w", 4 * C8), ("conv_b", C8), ("gx_b", C8), ("ga_b", C8), ("lam", C8),
                       ("q_g", QC), ("kv_g", KVC), ("ln1_g", C8), ("ln1_b", C8), ("ln2_g", C8),
                       ("ln2_b", C8), ("ffw", 3 * 2 * FC), ("ffb", 2 * FC)])
CST, NCST = columns([("ident", P), ("mask", P), ("invf", 1), ("sign", 1)])


class Count:

    def __init__(self, sem):
        self.sem, self.n, self.off = sem, 0, 0

    def inc(self, ins):
        ins.then_inc(self.sem, 1)
        self.n += 1

    def now(self):
        return self.off + self.n

    def step(self, eng, ins):
        self.inc(ins)
        eng.wait_ge(self.sem, self.now())

    def enter(self, i, per):
        self.base, self.off, self.per = self.n, i * per, per

    def leave(self, times):
        assert self.n == self.base + self.per, (self.n, self.base, self.per)
        self.off, self.n = 0, self.base + self.per * times


def sems(nc, ctx, names):
    handles = {n: ctx.enter_context(nc.semaphore(n)) for n in names}
    nums = sorted(h.num for h in handles.values())
    assert nums == list(range(nums[0], nums[0] + len(nums)))
    return handles, range(nums[0], nums[-1] + 1)


class Memory:

    def __init__(self, nc):
        self.nc, self.base, self.end = nc, -(-nc.sbuf_base // 64) * 64, nc.sbuf_base + nc.sbuf_bytes_remaining

    def at(self, name, kb, shape, dt=F32):
        size = int(np.prod(shape[1:])) * 4
        off = self.base + int(kb * 1024)
        assert off + size <= self.end, (name, off + size - self.end)
        return self.nc.alloc_sbuf_tensor_at(name, shape, dt, offset=off)


class Shared:

    def __init__(self, nc, mem, ps):
        self.ps = ps
        self.xh = mem.at("xh", 0, [P, C8, S], F32R)
        self.xl = mem.at("xl", 16, [P, C8, S], F32R)
        self.ring = mem.at("ring", 32, [P, RAW, 8 * P])
        self.wh = mem.at("wh", 48, [P, SPLIT, 8, P], F32R)
        self.wl = mem.at("wl", 56, [P, SPLIT, 8, P], F32R)
        self.z = mem.at("z", 64, [P, C8, S])
        self.sq = mem.at("sq", 80, [P, C8, S])


def arrivals(slot, units):
    return len(range(slot + RAW, units, RAW))


def first_units_there(sp, sem):
    for j in range(SPLIT, RAW):
        sp.wait_ge(sem[f"w_in{j}"], 16)


def load_unit(sp, sem, ring, d_w, slot, unit):
    sp.dma_start(ring[:, slot, :], d_w[ds(unit, 1)].rearrange("a p n -> p (a n)")).then_inc(sem[f"w_in{slot}"], 16)


def split_unit(g, nc, sem, sh, slot, split_slot, n):
    g.sem_inc(sem["w_turn"], 1)
    raw = sh.ring[:, slot, :]
    hi, lo = (t[:, split_slot, :, :].rearrange("p a b -> p (a b)") for t in (sh.wh, sh.wl))
    nc.gpsimd.tensor_scalar(hi, raw, 1.0, 0.0, ALU.mult, ALU.add).then_inc(sem["w_hi"], 1)
    g.wait_ge(sem["w_hi"], n + 1)
    nc.gpsimd.tensor_tensor(lo, raw, hi, ALU.subtract).then_inc(sem["w_split"], 1)


def first_units_in(sp, sem, sh, d_w, first):
    for j in range(RAW):
        load_unit(sp, sem, sh.ring, d_w, j, first + j)


def first_units_split(g, nc, sem, sh):
    for j in range(SPLIT):
        g.wait_ge(sem[f"w_in{j}"], 16)
        split_unit(g, nc, sem, sh, j, j, j)


def stream_units(sp, sem, ring, d_w, first, units):
    turns = (units - RAW) // RAW
    with sp.Fori(0, turns) as i:
        for j in range(RAW):
            sp.wait_ge(sem["w_split"], i * RAW + (j + 1))
            load_unit(sp, sem, ring, d_w, j, first + (i * RAW + (j + RAW)))
    for u in range(turns * RAW, units - RAW):
        sp.wait_ge(sem["w_split"], u + 1)
        load_unit(sp, sem, ring, d_w, u % RAW, first + (u + RAW))
    sp.wait_ge(sem["w_split"], units)
    for j in range(RAW):
        load_unit(sp, sem, ring, d_w, j, first + (units + j))
    for j in range(SPLIT, RAW):
        sp.wait_ge(sem[f"w_in{j}"], 16 * (arrivals(j, units) + 1))


def split_units(g, nc, sem, sh, units, interlude=None):
    g.sem_inc(sem["w_split"], SPLIT)

    def split(n, arrived, slot, split_slot):
        if arrived is not None:
            g.wait_ge(sem[f"w_in{slot}"], arrived)
        g.wait_ge(sem["unit_done"], n + 1)
        split_unit(g, nc, sem, sh, slot, split_slot, n - SPLIT)

    for n in range(SPLIT, RAW):
        split(n, None, n, n % SPLIT)

    def stretch(start, stop):
        n = start
        while n < stop:
            turns = (stop - n) // RAW
            if n % RAW or not turns:
                split(n, n // RAW * 16, n % RAW, n % SPLIT)
                n += 1
                continue
            with g.Fori(0, turns) as i:
                for j in range(RAW):
                    split(i * RAW + (n + j), i * 16 + n // RAW * 16, j, j % SPLIT)
            n += turns * RAW

    if interlude is None:
        stretch(RAW, units)
    else:
        stretch(RAW, interlude[0])
        interlude[1]()
        stretch(interlude[0], units)
    for j in range(SPLIT):
        split(units + j, arrivals(j, units) * 16 + 16, j, j)


def three(nc, out, wh, wl, xh, xl, first, last, **kw):
    nc.tensor.matmul(out, wh, xh, start=first, stop=False, **kw)
    nc.tensor.matmul(out, wh, xl, start=False, stop=False, **kw)
    return nc.tensor.matmul(out, wl, xh, start=False, stop=last, **kw)


def unit_products(pe, nc, sem, sh, xh, xl, bank, n, parity, first=True, last=True, ready=None, order=range(8)):
    pe.wait_ge(sem["w_split"], n + 1)
    for k in order:
        if ready is not None and k in ready:
            pe.wait_ge(sem[ready[k][0]], ready[k][1])
        mm = three(nc, bank, sh.wh[:, parity, k, :], sh.wl[:, parity, k, :], xh[:, k, :], xl[:, k, :],
                   first and k == order[0], last and k == order[-1])
    mm.then_inc(sem["unit_done"], 1)


def two_units(pe, nc, sem, sh, xh, xl, banks, n, parity, ready):
    pe.wait_ge(sem["w_split"], n + 2)
    for k in range(C8):
        pe.wait_ge(sem["x_ready"], ready + k + 1)
        for j in range(2):
            u = (parity + j) % 2
            mm = three(nc, banks[j], sh.wh[:, u, k, :], sh.wl[:, u, k, :], xh[:, k, :], xl[:, k, :],
                       k == 0, k == C8 - 1, skip_group_check=True)
            if k == C8 - 1:
                mm.then_inc(sem["unit_done"], 1)


def layer_norm_engines(rounds_before, sem, sh, ones_d, eps, eps_copy, par, g0, b0, stat):
    r, z, sq, xh, xl = rounds_before, sh.z, sh.sq, sh.xh, sh.xl
    ps_mean, ps_var = sh.ps[:, 4, :], sh.ps[:, 5, :]

    def tensor(pe, nc):
        pe.wait_ge(sem["z_ready"], r * C8 + C8)
        nc.tensor.matmul(ps_mean, ones_d, stat[:, 0, :], start=True, stop=True).then_inc(sem["mean_mm"], 1)
        for k in range(SINGLE):
            pe.wait_ge(sem["sq_ready"], r * C8 + k + 1)
            nc.tensor.matmul(ps_var, ones_d, sq[:, k, :], start=(k == 0), stop=False)
        pe.wait_ge(sem["sq_sum"], r + 1)
        nc.tensor.matmul(ps_var, ones_d, sq[:, C8 - 1, :], start=False, stop=True).then_inc(sem["var_mm"], 1)

    def vector(dve, nc):
        dve.wait_ge(sem["mean_mm"], r + 1)
        for k in range(C8):
            nc.vector.tensor_tensor(z[:, k, :], z[:, k, :], ps_mean, ALU.subtract).then_inc(sem["xc_ready"], 1)
        for k in range(SINGLE, C8 - 1):
            dve.wait_ge(sem["sq_ready"], r * C8 + k + 2)
            if k > SINGLE:
                dve.wait_ge(sem["sq_step"], r * (C8 - 2 - SINGLE) + k - SINGLE)
            ins = nc.vector.tensor_tensor(sq[:, k + 1, :], sq[:, k + 1, :], sq[:, k, :], ALU.add)
            ins.then_inc(sem["sq_step" if k < C8 - 2 else "sq_sum"], 1)
        dve.wait_ge(sem["std_ready"], r + 1)
        nc.vector.reciprocal(stat[:, 0, :], stat[:, 1, :]).then_inc(sem["rstd_ready"], 1)
        dve.wait_ge(sem["rstd_ready"], r + 1)
        dve.wait_ge(sem["xc_ready"], r * C8 + C8)
        for k in range(C8 + 1):
            if k < C8:
                nc.vector.tensor_tensor(z[:, k, :], z[:, k, :], stat[:, 0, :], ALU.mult).then_inc(sem["xn_ready"], 1)
            if k:
                dve.wait_ge(sem["xa_ready"], r * C8 + k)
                nc.vector.tensor_tensor(xl[:, k - 1, :], z[:, k - 1, :], xh[:, k - 1, :], ALU.subtract
                                        ).then_inc(sem["x_ready"], 1)

    def scalar(act, nc, gains=None):
        nc.scalar.activation(eps_copy, eps, ACT.Sqrt).then_inc(sem["sqrt_there"], 1)
        for k in range(C8):
            act.wait_ge(sem["xc_ready"], r * C8 + k + 1)
            nc.scalar.activation(sq[:, k, :], z[:, k, :], ACT.Square).then_inc(sem["sq_ready"], 1)
        act.wait_ge(sem["var_mm"], r + 1)
        nc.scalar.activation(stat[:, 1, :], ps_var, ACT.Sqrt, bias=eps).then_inc(sem["std_ready"], 1)
        if gains is not None:
            act.wait_ge(*gains)
        for k in range(C8):
            act.wait_ge(sem["xn_ready"], r * C8 + k + 1)
            g, b = par[:, g0 + k:g0 + k + 1], par[:, b0 + k:b0 + k + 1]
            nc.scalar.activation(xh[:, k, :], z[:, k, :], ACT.Identity, scale=g, bias=b)
            nc.scalar.activation(z[:, k, :], z[:, k, :], ACT.Identity, scale=g, bias=b).then_inc(sem["xa_ready"], 1)

    return tensor, vector, scalar


def residual_before(nc, do, sh, m):
    V, z = nc.vector, sh.z[:, m, :]
    do(V.tensor_scalar(z, sh.xh[:, m, :], ALPHA, None, ALU.mult))
    do(V.scalar_tensor_tensor(z, sh.xl[:, m, :], ALPHA, z, ALU.mult, ALU.add))


def residual_chunk(nc, do, sh, m, bank):
    do(nc.vector.tensor_tensor(sh.z[:, m, :], sh.z[:, m, :], bank, ALU.add))


def sum_chunk(dve, nc, do, sem, sh, m, stat):
    V, z, acc = nc.vector, sh.z[:, m, :], stat[:, 0, :]
    ins = V.tensor_tensor(acc, acc, z, ALU.add) if m else V.tensor_copy(acc, z)
    ins.then_inc(sem["z_ready"], 1)


LN_SEMS = ["z_ready", "mean_mm", "xc_ready", "sq_ready", "sq_step", "sq_sum", "var_mm", "sqrt_there", "std_ready", "rstd_ready", "xn_ready",
           "xa_ready", "x_ready"]
STREAM_SEMS = [f"w_in{j}" for j in range(RAW)] + ["w_turn", "w_hi", "w_split", "unit_done"]


def reduce_angle(dve, nc, step, r, ang, n):
    step.step(dve, nc.vector.tensor_scalar(n, ang, 1.0 / TWO_PI, MAGIC, ALU.mult, ALU.add))
    step.step(dve, nc.vector.tensor_scalar(n, n, -MAGIC, None, ALU.add))
    step.step(dve, nc.vector.scalar_tensor_tensor(r, n, -PI2_A, ang, ALU.mult, ALU.add))
    step.step(dve, nc.vector.scalar_tensor_tensor(r, n, -PI2_B, r, ALU.mult, ALU.add))
    step.step(dve, nc.vector.scalar_tensor_tensor(r, n, -PI2_C, r, ALU.mult, ALU.add))
    step.step(dve, nc.vector.tensor_scalar(r, r, PI_DOWN, -PI_DOWN, ALU.min, ALU.max))


def first_block(nc, mem, sh, d_x, d_pos, d_cst, d_w, d_gw, d_par):
    with ExitStack() as ctx:
        ps, xh, xl = sh.ps, sh.xh, sh.xl
        at = mem.at
        qt = at("qt", 64, [P, 2, S])
        rt = at("rt", 68, [P, 2, S])
        kt = at("kt", 72, [P, 2, 2, S])
        hid_h = at("hid_h", 80, [P, FC, S], F32R)
        hid_l = at("hid_l", 128, [P, FC, S], F32R)
        gate_r = at("gate_r", 80, [P, C8, S])
        merged_h = at("merged_h", 80, [P, C8, S], F32R)
        rnn_in = at("rnn_in", 96, [P, C8, S])
        vals = at("vals", 112, [P, 4, D])
        gate_b = at("gate_b", 128, [P, C8, S])
        merged_l = at("merged_l", 128, [P, C8, S], F32R)
        lat_h = at("lat_h", 144, [P, KVC + QC, S], F32R)
        lat_l = at("lat_l", 154, [P, KVC + QC, S], F32R)
        gw = at("gw", 164, [P, 2, 2, P])
        lat_sq = at("lat_sq", 166, [P, KVC + QC, S])
        sx, sa, th, av, m2 = (at(n, 166 + 2 * k, [P, S]) for k, n in enumerate(("sx", "sa", "th", "av", "m2")))
        lat = at("lat", 176, [P, KVC + 1 + QC, S])
        pb = at("pb", 176, [P, 4, S])
        taps = at("taps", 176, [P, 2, 2, S])
        sig_a = at("sig_a", 194, [P, S])
        pt = at("pt", 184, [P, 4, S])
        stat = at("stat", 192, [P, 2, S])
        osb = at("osb", 192, [P, 4, P])
        tmp = at("tmp", 196, [P, 2, S])
        rope = at("rope", 200, [P, S])
        par = at("par", 202, [P, NPAR1])
        cst = at("cst", 203.5, [P, NCST])
        ones_d = at("ones_d", 204.75, [P, P])
        small = at("small", 205.25, [P, 4, 16])
        lru = at("lru", 205.5, [P, 6, C8])
        eps = at("eps", 205.75, [P, 2])
        kvraw, krope, qraw = lat[:, 0:KVC, :], lat[:, KVC, :], lat[:, KVC + 1:, :]

        names = (STREAM_SEMS + LN_SEMS + ["gw_in0", "gw_in1", "par_in", "cst_in", "x_in0", "x_in1", "x_in2", "x_in3",
                 "proj_evac", "proj_tap", "lat_sq", "lat_mm", "lat_std", "lat_rstd", "lat_ready",
                 "kpe_ready", "dve_step", "ang_ready", "sin_ready", "abs_ready", "expl_ready", "lru_ready",
                 "q_mm", "k_mm", "v_mm", "qn_ready", "qr_ready", "k_ready", "v_ready", "s_mm", "nmax_ready",
                 "p_ready", "t_mm", "pt_ready", "o_mm", "o_ready", "y_mm", "merged", "conv_ready", "gate_mm",
                 "gate_sig", "a_ready", "m2_ready", "mu_ready", "rnn_done", "gb_raw", "ga_sig", "gb_sig",
                 "ff_tap", "ff_conv", "ff_gelu", "ff_done"])
        sem, sem_range = sems(nc, ctx, names)

        def chunk(t, k):
            return t[:, k, :] if isinstance(k, int) else t[:, ds(k, 1), :]

        def one(t, k):
            return t[:, k:k + 1] if isinstance(k, int) else t[:, ds(k, 1)]

        def col(name, k=0):
            return one(par, k + PAR1[name][0])

        ident = cst[:, CST["ident"][0]:CST["ident"][0] + P]
        mask = cst[:, CST["mask"][0]:CST["mask"][0] + P]

        ln1 = layer_norm_engines(0, sem, sh, ones_d[:, :], eps[:, 0:1], eps[:, 1:2], par, PAR1["ln1_g"][0], PAR1["ln1_b"][0], stat)
        ln2 = layer_norm_engines(1, sem, sh, ones_d[:, :], eps[:, 0:1], eps[:, 1:2], par, PAR1["ln2_g"][0], PAR1["ln2_b"][0], stat)
        pos = at("pos", 196, [P, S], I32)

        with nc.Block() as block:
            @block.sync
            def _(sp):
                sp.dma_start(pos[:, :], d_pos).then_inc(sem["par_in"], 16)
                sp.dma_start(cst[:, :], d_cst).then_inc(sem["cst_in"], 16)
                for q in range(4):
                    two = slice(2 * q, 2 * q + 2)
                    sp.dma_start(sh.z[:, two, :], d_x[:, two, :]).then_inc(sem[f"x_in{q}"], 16)
                    if q == 1:
                        first_units_in(sp, sem, sh, d_w, 0)
                first_units_there(sp, sem)

            @block.gpsimd
            def _(g):
                nc.gpsimd.memset(ones_d[:, :], 1.0 / D)
                nc.gpsimd.memset(eps[:, 0:1], EPS1)
                first_units_split(g, nc, sem, sh)

            @block.vector
            def _(dve):
                step = Count(sem["dve_step"])
                fr, sg = CST["invf"][0], CST["sign"][0]
                dve.wait_ge(sem["par_in"], 16)
                dve.wait_ge(sem["cst_in"], 16)
                hi = slice(64, P)
                ang, n, r = pb[hi, 0, :], pb[hi, 1, :], pb[hi, 2, :]
                step.step(dve, nc.vector.tensor_copy(ang, pos[hi, :]))
                step.step(dve, nc.vector.tensor_scalar(ang, ang, cst[hi, fr:fr + 1], None, ALU.mult))
                reduce_angle(dve, nc, step, r, ang, n)
                c = pb[64:96, 2, :]
                step.step(dve, nc.vector.tensor_scalar(pb[64:96, 3, :], c, -1.0, None, ALU.mult))
                step.step(dve, nc.vector.tensor_tensor(c, c, pb[64:96, 3, :], ALU.max))
                nc.vector.tensor_scalar(c, c, -1.0, TWO_PI / 4, ALU.mult, ALU.add).then_inc(sem["ang_ready"], 1)
                for k in range(C8):
                    dve.wait_ge(sem["xa_ready"], k + 1)
                    nc.vector.tensor_tensor(xl[:, k, :], sh.z[:, k, :], xh[:, k, :], ALU.subtract)
                dve.wait_ge(sem["sin_ready"], 1)
                nc.vector.tensor_scalar(rope[hi, :], rope[hi, :], cst[hi, sg:sg + 1], None, ALU.mult)

            @block.scalar
            def _(act):
                for k in range(C8):
                    act.wait_ge(sem[f"x_in{k // 2}"], 16)
                    nc.scalar.activation(xh[:, k, :], sh.z[:, k, :], ACT.Copy).then_inc(sem["xa_ready"], 1)
                    if k == 3:
                        act.wait_ge(sem["ang_ready"], 1)
                        nc.scalar.activation(rope[64:P, :], pb[64:P, 2, :], ACT.Sin).then_inc(sem["sin_ready"], 1)

        nc.all_engine_barrier(sems_to_clear=sem_range)

        with nc.Fori(0, DEPTH) as layer:
            with nc.Block() as block:
                @block.sync
                def _(sp):
                    sp.dma_start(par[:, :], d_par[ds(layer, 1)].rearrange("a p n -> p (a n)")).then_inc(sem["par_in"], 16)

                    def load_gates(slot, pair):
                        sp.dma_start(gw[:, slot], d_gw[ds(layer * PAIRS + pair, 1)].rearrange("a p (k m) -> p (a k) m", m=P)
                                     ).then_inc(sem[f"gw_in{slot}"], 16)

                    for j in range(2):
                        load_gates(j, j)
                    stream_units(sp, sem, sh.ring, d_w, layer * U1, U1)

                @block.gpsimd
                def _(g):
                    split_units(g, nc, sem, sh, U1)

                @block.tensor
                def _(pe):
                    for n in ("t_mm", "o_mm"):
                        pe.sem_inc(sem[n], HEAD)
                    pe.sem_inc(sem["unit_done"], SPLIT)

                    def unit(bank, n, parity, xh=sh.xh, xl=sh.xl, **kw):
                        unit_products(pe, nc, sem, sh, xh, xl, bank, n, parity, **kw)

                    head = KVC + 1 + QC
                    for u in range(head):
                        pe.wait_ge(sem["proj_evac"], u + 1)
                        unit(ps[:, u % 4, :], u, u % 2)

                    def eight_tiles(u0):
                        with pe.Fori(0, 2) as i:
                            for j in range(4):
                                pe.wait_ge(sem["proj_evac"], i * 4 + (u0 + j + 1))
                                unit(ps[:, (u0 + j) % 4, :], i * 4 + (u0 + j), (u0 + j) % 2)

                    eight_tiles(head)
                    pe.wait_ge(sem["lat_sq"], KVC + QC)
                    for k in range(KVC):
                        mm = nc.tensor.matmul(ps[:, 4, :], ones_d[:, :], lat_sq[:, k, :], start=(k == 0), stop=(k == KVC - 1))
                    mm.then_inc(sem["lat_mm"], 1)
                    for k in range(QC):
                        mm = nc.tensor.matmul(ps[:, 5, :], ones_d[:, :], lat_sq[:, KVC + k, :], start=(k == 0), stop=(k == QC - 1))
                    mm.then_inc(sem["lat_mm"], 1)
                    eight_tiles(head + C8)

                    def slot(pp, k):
                        return (U_ATT + PER_PAIR * pp + k) % 2

                    def number(p, k):
                        return p * PER_PAIR + (U_ATT + k)

                    def project_q(pp, half):
                        u = slot(pp, 1)
                        for c in range(QC):
                            mm = three(nc, ps[:, 0, :], sh.wh[:, u, half * 3 + c, :], sh.wl[:, u, half * 3 + c, :],
                                       lat_h[:, KVC + c, :], lat_l[:, KVC + c, :], c == 0, c == QC - 1)
                        mm.then_inc(sem["unit_done" if half else "q_mm"], 1)

                    def project_k(pp):
                        u = slot(pp, 1)
                        for c in range(KVC):
                            mm = three(nc, ps[:, 1, :], sh.wh[:, u, 6 + c, :], sh.wl[:, u, 6 + c, :],
                                       lat_h[:, c, :], lat_l[:, c, :], c == 0, c == KVC - 1)
                        mm.then_inc(sem["k_mm"], 1)

                    def scores(pp, hb, b):
                        n = (b + 1) * P
                        nc.tensor.matmul(ps[:, 2 + b % 2, 0:n], qt[0:96, hb, b * P:b * P + P], kt[0:96, pp, hb, 0:n],
                                         start=True, stop=True).then_inc(sem["s_mm"], 1)

                    def turn(b):
                        for j in range(b + 1):
                            mm = nc.tensor.transpose(ps[:, 4 + b % 2, j * P:j * P + P], pb[:, b, j * P:j * P + P], ident)
                        mm.then_inc(sem["t_mm"], 1)

                    def weigh(h, b):
                        for j in range(b + 1):
                            mm = nc.tensor.matmul(ps[:, 6, b * 64:b * 64 + 64],
                                                  pt[:, b, j * P:j * P + P], vals[:, j, ds(h * 64, 64)] if not isinstance(h, int)
                                                  else vals[:, j, h * 64:h * 64 + 64],
                                                  start=(j == 0), stop=(j == b))
                        mm.then_inc(sem["o_mm"], 1)

                    def turn_out(h, gate_tiles):
                        pe.wait_ge(sem["gb_raw"], gate_tiles)
                        pe.wait_ge(sem["o_ready"], HEAD + h + 1)
                        for b in range(4):
                            mm = nc.tensor.transpose(ps[:, 7, b * P:b * P + P], osb[:, b, :], ident)
                        mm.then_inc(sem["y_mm"], 1)

                    pe.wait_ge(sem["lat_ready"], KVC + QC)
                    pe.wait_ge(sem["proj_evac"], PROJ_UNITS + 4)
                    for c in range(KVC):
                        n = U_V + c
                        pe.wait_ge(sem["w_split"], n + 1)
                        for t in range(4):
                            tok = slice(t * P, t * P + P)
                            for g in range(2):
                                wh, wl = (w[:, n % 2, 4 * g:4 * g + 4, :].rearrange("p a b -> p (a b)") for w in (sh.wh, sh.wl))
                                mm = three(nc, ps[:, 2 * t + g, :], lat_h[:, c, tok], lat_l[:, c, tok], wh, wl,
                                           c == 0, c == KVC - 1, skip_group_check=True)
                                if c == KVC - 1 and 2 * t + g < 7:
                                    mm.then_inc(sem["v_mm"], 1)
                        mm.then_inc(sem["unit_done"], 1)
                    pe.wait_ge(sem["v_ready"], 8)
                    unit(ps[:, 7, :], number(0, 0), slot(0, 0))
                    pe.wait_ge(sem["w_split"], number(0, 1) + 1)
                    project_q(0, 0)
                    project_k(0)
                    pe.wait_ge(sem["kpe_ready"], 4)
                    pe.wait_ge(sem["qn_ready"], 1)
                    pe.wait_ge(sem["qr_ready"], 1)
                    pe.wait_ge(sem["k_ready"], 1)
                    scores(0, 0, 0)
                    scores(0, 0, 1)
                    project_q(0, 1)

                    def four_heads(i, last):
                        for hh in range(4):
                            pp, hb, end = hh // 2, hh % 2, last and hh == 3
                            h4, h, p = i * 16 + hh * 4, i * 4 + hh, i * 2 + pp
                            if hb == 1 and not end:
                                pe.wait_ge(sem["ga_sig"], p + 1)
                                unit(ps[:, 7, :], number(p + 1, 0), slot(1 - pp, 0))
                                pe.wait_ge(sem["w_split"], number(p + 1, 1) + 1)
                                pe.wait_ge(sem["gate_sig"], HEAD + p * 2 + 2)
                                project_q(1 - pp, 0)
                                project_k(1 - pp)
                            pe.wait_ge(sem["pt_ready"], HEAD + h4)
                            for b in (0, 1):
                                pe.wait_ge(sem["p_ready"], HEAD + h4 + b + 1)
                                turn(b)
                                scores(pp, hb, b + 2)
                            pe.wait_ge(sem["o_ready"], HEAD + h)
                            for b in (0, 1):
                                pe.wait_ge(sem["pt_ready"], HEAD + h4 + b + 1)
                                weigh(h, b)
                            if hb == 0:
                                pe.wait_ge(sem["qn_ready"], h + 2)
                                pe.wait_ge(sem["qr_ready"], h + 2)
                                pe.wait_ge(sem[f"gw_in{pp}"], i * 16 + 16)
                                for g in range(2):
                                    nc.tensor.matmul(ps[:, g, :], gw[:, pp, g, :], chunk(rnn_in, p),
                                                     start=True, stop=True).then_inc(sem["gate_mm"], 1)
                            for b in (2, 3):
                                pe.wait_ge(sem["p_ready"], HEAD + h4 + b + 1)
                                turn(b)
                            if not end:
                                pe.wait_ge(sem["qn_ready"], h + 2)
                                pe.wait_ge(sem["qr_ready"], h + 2)
                                pe.wait_ge(sem["k_ready"], p + 1 + hb)
                                scores(pp if hb == 0 else 1 - pp, 1 - hb, 0)
                                scores(pp if hb == 0 else 1 - pp, 1 - hb, 1)
                            if hb == 0:
                                pe.wait_ge(sem["merged"], HEAD + p)
                                unit(ps[:, 7, :], number(p, 2), slot(pp, 2))
                            for b in (2, 3):
                                pe.wait_ge(sem["pt_ready"], HEAD + h4 + b + 1)
                                weigh(h, b)
                            if hb == 1:
                                if not end:
                                    project_q(1 - pp, 1)
                                turn_out(h, PAIRS if end else p + 2)

                    with pe.Fori(0, PAIRS // 2 - 1) as i:
                        four_heads(i, False)
                    four_heads(PAIRS // 2 - 1, True)

                    pe.wait_ge(sem["merged"], HEAD + PAIRS - 1)
                    for m in range(C8):
                        if m >= 4:
                            pe.wait_ge(sem["z_ready"], m - 3)
                        unit(ps[:, m % 4, :], U_OUT + m, m % 2, merged_h, merged_l,
                             ready={C8 - 1: ("merged", HEAD + PAIRS)} if m == 0 else None)
                    ln1[0](pe, nc)

                    def up_tile(i, j):
                        pe.wait_ge(sem["ff_conv"], i * 4 + j + 1)
                        for half in range(2):
                            unit(ps[:, 2 * j + half, :], i * 8 + (U_UP + 2 * j + half), half)

                    pe.wait_ge(sem["ff_conv"], 1)
                    two_units(pe, nc, sem, sh, xh, xl, (ps[:, 0, :], ps[:, 1, :]), U_UP, U_UP % 2, 0)
                    for j in range(1, 4):
                        up_tile(0, j)
                    with pe.Fori(0, FC // 4 - 1) as i:
                        for j in range(4):
                            up_tile(i + 1, j)
                    pe.wait_ge(sem["ff_conv"], 4 + FC - 2)
                    with pe.Fori(0, C8 // 4) as i:
                        for m in range(4):
                            pe.wait_ge(sem["z_ready"], i * 4 + C8 + m - 3 if m >= 3 else i * 4 + C8)
                            for q in range(DOWN_PER):
                                if m == 0:
                                    pe.wait_ge(sem["ff_done"], HEAD + FC * (q + 1) // DOWN_PER)
                                unit(ps[:, m, :], i * 12 + (U_DOWN + m * DOWN_PER + q), (m + q) % 2,
                                     hid_h[:, q * 8:q * 8 + 8, :], hid_l[:, q * 8:q * 8 + 8, :],
                                     first=q == 0, last=q == DOWN_PER - 1)
                    ln2[0](pe, nc)

                @block.scalar
                def _(act):
                    for n in ("p_ready", "pt_ready", "gate_sig"):
                        act.sem_inc(sem[n], HEAD)
                    act.sem_inc(sem["proj_evac"], 4)
                    for u in range(KVC + 1 + QC):
                        act.wait_ge(sem["unit_done"], SPLIT + u + 1)
                        nc.scalar.activation(lat[:, u, :], ps[:, u % 4, :], ACT.Copy).then_inc(sem["proj_evac"], 1)
                    act.wait_ge(sem["proj_evac"], 4 + KVC + 1 + QC)
                    for k in range(KVC):
                        nc.scalar.activation(lat_sq[:, k, :], kvraw[:, k, :], ACT.Square).then_inc(sem["lat_sq"], 1)
                    for k in range(QC):
                        nc.scalar.activation(lat_sq[:, KVC + k, :], qraw[:, k, :], ACT.Square).then_inc(sem["lat_sq"], 1)
                    act.wait_ge(sem["par_in"], 16)
                    u0 = KVC + 1 + QC
                    with act.Fori(0, 2) as i:
                        for j in range(4):
                            act.wait_ge(sem["unit_done"], SPLIT + i * 4 + (u0 + j + 1))
                            nc.scalar.activation(chunk(rnn_in, i * 4 + j), ps[:, (u0 + j) % 4, :], ACT.Identity,
                                                 scale=col("conv_w", i * 4 + (3 * C8 + j)), bias=col("conv_b", i * 4 + j)
                                                 ).then_inc(sem["proj_tap"], 1)
                            act.wait_ge(sem["conv_ready"], i * 4 + j + 1)
                            act.sem_inc(sem["proj_evac"], 1)
                    u0 += C8
                    act.wait_ge(sem["abs_ready"], 1)
                    nc.scalar.activation(lru[:, 1, :], lru[:, 0, :], ACT.Exp, scale=-1.0).then_inc(sem["expl_ready"], 1)
                    for n, (bank, width) in enumerate(((4, KVC * P), (5, QC * P))):
                        act.wait_ge(sem["lat_mm"], n + 1)
                        nc.scalar.activation(stat[:, n, :], ps[:, bank, :], ACT.Sqrt, scale=float(D) / width,
                                             bias=eps[:, 0:1]).then_inc(sem["lat_std"], 1)
                    with act.Fori(0, 2) as i:
                        for j in range(4):
                            act.wait_ge(sem["unit_done"], SPLIT + i * 4 + (u0 + j + 1))
                            nc.scalar.activation(chunk(gate_r, i * 4 + j), ps[:, (u0 + j) % 4, :],
                                                 ACT.Gelu_apprx_tanh).then_inc(sem["proj_evac"], 1)

                    def number(p, k):
                        return p * PER_PAIR + (U_ATT + k)

                    def evac_q(h, p, buf):
                        if buf:
                            act.wait_ge(sem["unit_done"], SPLIT + number(p, 1) + 1)
                        else:
                            act.wait_ge(sem["q_mm"], p + 1)
                        nc.scalar.activation(qt[0:64, buf, :], ps[0:64, 0, :], ACT.Copy).then_inc(sem["qn_ready"], 1)

                    def evac_k(p, pp):
                        act.wait_ge(sem["k_mm"], p + 1)
                        nc.scalar.activation(kt[0:64, pp, 0, :], ps[0:64, 1, :], ACT.Copy)
                        nc.scalar.activation(kt[0:64, pp, 1, :], ps[64:P, 1, :], ACT.Copy).then_inc(sem["k_ready"], 1)

                    def expo(hh, h4, b):
                        act.wait_ge(sem["nmax_ready"], h4 + b + 1)
                        c = hh * 4 + b
                        nc.scalar.activation(pb[:, b, 0:(b + 1) * P], ps[:, 2 + b % 2, 0:(b + 1) * P], ACT.Exp,
                                             scale=SCALE1, bias=small[:, 1, c:c + 1], accum_out=small[:, 2, c:c + 1]
                                             ).then_inc(sem["p_ready"], 1)

                    def evac_pt(h4, b):
                        act.wait_ge(sem["t_mm"], HEAD + h4 + b + 1)
                        nc.scalar.activation(pt[:, b, 0:(b + 1) * P], ps[:, 4 + b % 2, 0:(b + 1) * P], ACT.Copy
                                             ).then_inc(sem["pt_ready"], 1)

                    for n in range(8):
                        if n < 7:
                            act.wait_ge(sem["v_mm"], n + 1)
                        else:
                            act.wait_ge(sem["unit_done"], SPLIT + U_ATT)
                        nc.scalar.activation(vals[:, n // 2, n % 2 * S:n % 2 * S + S], ps[:, n, :], ACT.Copy
                                             ).then_inc(sem["v_ready"], 1)

                    def gate_b_out(p):
                        act.wait_ge(sem["unit_done"], SPLIT + number(p, 0) + 1)
                        nc.scalar.activation(chunk(gate_b, p), ps[:, 7:8, :] if not isinstance(p, int) else ps[:, 7, :],
                                             ACT.Copy).then_inc(sem["gb_raw"], 1)

                    gate_b_out(0)
                    evac_q(0, 0, 0)
                    evac_k(0, 0)
                    expo(0, 0, 0)
                    expo(0, 0, 1)
                    evac_q(1, 0, 1)

                    def four_heads(i, last):
                        for hh in range(4):
                            pp, hb, end = hh // 2, hh % 2, last and hh == 3
                            h4, h, p = i * 16 + hh * 4, i * 4 + hh, i * 2 + pp
                            if hb == 1:
                                act.wait_ge(sem["m2_ready"], p + 1)
                                nc.scalar.activation(m2[:, :], m2[:, :], ACT.Sqrt).then_inc(sem["mu_ready"], 1)
                            if hb == 1 and not end:
                                gate_b_out(p + 1)
                                evac_q(h + 1, p + 1, 0)
                                evac_k(p + 1, 1 - pp)
                            act.wait_ge(sem["o_mm"], HEAD + h4)
                            evac_pt(h4, 0)
                            evac_pt(h4, 1)
                            expo(hh, h4, 2)
                            expo(hh, h4, 3)
                            evac_pt(h4, 2)
                            evac_pt(h4, 3)
                            if not end:
                                expo((hh + 1) % 4, h4 + 4, 0)
                                expo((hh + 1) % 4, h4 + 4, 1)
                            if hb == 0:
                                act.wait_ge(sem["rnn_done"], HEAD + p)
                                for g, (name, out) in enumerate((("gx_b", sx), ("ga_b", sa))):
                                    act.wait_ge(sem["gate_mm"], p * 2 + g + 1)
                                    nc.scalar.activation(out[:, :], ps[:, g, :], ACT.Sigmoid, bias=col(name, p)
                                                         ).then_inc(sem["gate_sig"], 1)
                                act.wait_ge(sem["gate_sig"], HEAD + p * 2 + 2)
                                if not last:
                                    act.dma_start(gw[:, pp], d_gw[ds(layer * PAIRS + (p + 2), 1)]
                                                  .rearrange("a p (k m) -> p (a k) m", m=P)).then_inc(sem[f"gw_in{pp}"], 16)
                                act.wait_ge(sem["gb_raw"], p + 1)
                                act.wait_ge(sem["lru_ready"], 1)
                                nc.scalar.activation(th[:, :], sa[:, :], ACT.Tanh, scale=one(lru[:, 4, :], p)
                                                     ).then_inc(sem["a_ready"], 1)
                                nc.scalar.activation(chunk(gate_b, p), chunk(gate_b, p), ACT.Sigmoid).then_inc(sem["gb_sig"], 1)
                                act.wait_ge(sem["unit_done"], SPLIT + number(p, 2) + 1)
                                nc.scalar.activation(sig_a[:, :], ps[:, 7, :], ACT.Sigmoid).then_inc(sem["ga_sig"], 1)
                                nc.scalar.activation(av[:, :], sa[:, :], ACT.Exp, scale=one(lru[:, 5, :], p)
                                                     ).then_inc(sem["a_ready"], 1)
                            elif not end:
                                evac_q(h + 2, p + 1, 1)

                    with act.Fori(0, PAIRS // 2 - 1) as i:
                        four_heads(i, False)
                    four_heads(PAIRS // 2 - 1, True)

                    ln1[2](act, nc)
                    with act.Fori(0, FC // 4) as i:
                        for j in range(4):
                            f = i * 4 + j
                            act.wait_ge(sem["ff_done"], HEAD + (f - 1 if j else f))
                            for half in range(2):
                                act.wait_ge(sem["unit_done"], SPLIT + f * 2 + (U_UP + half + 1))
                                nc.scalar.activation(taps[:, j % 2, half, :], ps[:, 2 * j + half, :], ACT.Identity,
                                                     scale=col("ffw", f + (2 * 2 * FC + half * FC)),
                                                     bias=col("ffb", f + half * FC)).then_inc(sem["ff_tap"], 1)
                            act.wait_ge(sem["ff_conv"], f + 5)
                            nc.scalar.activation(taps[:, j % 2, 0, :], taps[:, j % 2, 0, :], ACT.Gelu_apprx_tanh
                                                 ).then_inc(sem["ff_gelu"], 1)
                    ln2[2](act, nc)

                @block.vector
                def _(dve):
                    step = Count(sem["dve_step"])
                    V = nc.vector
                    def split(v, hi, lo, done):
                        step.step(dve, V.tensor_scalar(hi, v, 1.0, None, ALU.mult))
                        V.tensor_tensor(lo, v, hi, ALU.subtract).then_inc(sem[done], 1)

                    dve.sem_inc(sem["ff_conv"], 4)
                    for n in ("merged", "o_ready", "rnn_done", "ff_done"):
                        dve.sem_inc(sem[n], HEAD)
                    dve.wait_ge(sem["proj_evac"], 4 + KVC + 1)
                    step.step(dve, V.tensor_tensor(rt[64:96, 0, :], krope[96:P, :], rope[96:P, :], ALU.mult))
                    step.step(dve, V.tensor_tensor(rt[64:96, 1, :], krope[64:96, :], rope[64:96, :], ALU.mult))
                    for n in range(4):
                        V.tensor_tensor(kt[64:96, n // 2, n % 2, :], rt[64:96, 0, :], rt[64:96, 1, :], ALU.add
                                        ).then_inc(sem["kpe_ready"], 1)
                    dve.wait_ge(sem["par_in"], 16)
                    lam = par[:, PAR1["lam"][0]:PAR1["lam"][0] + C8]
                    L = [lru[:, n, :] for n in range(6)]
                    step.step(dve, V.tensor_scalar(L[2], lam, -1.0, None, ALU.mult))
                    V.tensor_tensor(L[0], L[2], lam, ALU.max).then_inc(sem["abs_ready"], 1)

                    u0 = KVC + 1 + QC
                    with dve.Fori(0, 2) as i:
                        step.enter(i, 8)
                        for j in range(4):
                            m, bank = i * 4 + j, ps[:, (u0 + j) % 4, :]
                            dve.wait_ge(sem["proj_tap"], i * 4 + j + 1)
                            for s in (1, 2, 3):
                                out = rnn_in[:, ds(m, 1), s:]
                                ins = V.scalar_tensor_tensor(out, bank[:, 0:S - s], col("conv_w", i * 4 + (j + (3 - s) * C8)),
                                                             out, ALU.mult, ALU.add)
                                if s < 3:
                                    step.step(dve, ins)
                                else:
                                    ins.then_inc(sem["conv_ready"], 1)
                        step.leave(2)

                    for n, (t, name, width) in enumerate(((kvraw, "kv_g", KVC), (qraw, "q_g", QC))):
                        dve.wait_ge(sem["lat_std"], n + 1)
                        V.reciprocal(stat[:, n, :], stat[:, n, :]).then_inc(sem["lat_rstd"], 1)
                        dve.wait_ge(sem["lat_rstd"], n + 1)
                        for k in range(width):
                            step.step(dve, V.scalar_tensor_tensor(t[:, k, :], t[:, k, :], col(name, k), stat[:, n, :],
                                                                  ALU.mult, ALU.mult))
                            split(t[:, k, :], lat_h[:, n * KVC + k, :], lat_l[:, n * KVC + k, :], "lat_ready")

                    dve.wait_ge(sem["expl_ready"], 1)
                    z, t, s2 = L[1], L[3], L[0]
                    step.step(dve, V.tensor_scalar(t, z, 2.0, None, ALU.add))
                    step.step(dve, V.reciprocal(t, t))
                    step.step(dve, V.tensor_tensor(t, z, t, ALU.mult))
                    step.step(dve, V.tensor_tensor(s2, t, t, ALU.mult))
                    acc = L[4]
                    step.step(dve, V.tensor_scalar(acc, s2, 1.0 / 15, None, ALU.mult))
                    for n in (13, 11, 9, 7, 5, 3):
                        step.step(dve, V.scalar_tensor_tensor(acc, acc, 1.0 / n, s2, ALU.add, ALU.mult))
                    step.step(dve, V.scalar_tensor_tensor(acc, acc, 1.0, t, ALU.add, ALU.mult))
                    step.step(dve, V.tensor_scalar(L[2], L[2], 0.0, None, ALU.max))
                    step.step(dve, V.scalar_tensor_tensor(acc, acc, 2.0, L[2], ALU.mult, ALU.add))
                    step.step(dve, V.tensor_scalar(L[5], acc, -8.0, None, ALU.mult))
                    V.tensor_scalar(acc, acc, 8.0, None, ALU.mult).then_inc(sem["lru_ready"], 1)

                    def rotate_q(h, p, buf):
                        if buf:
                            dve.wait_ge(sem["unit_done"], SPLIT + p * PER_PAIR + (U_ATT + 2))
                        else:
                            dve.wait_ge(sem["q_mm"], p + 1)
                        step.step(dve, V.tensor_tensor(rt[64:96, buf, :], ps[96:P, 0, :], rope[96:P, :], ALU.mult))
                        step.step(dve, V.tensor_tensor(qt[64:96, buf, :], ps[64:96, 0, :], rope[64:96, :], ALU.mult))
                        V.tensor_tensor(qt[64:96, buf, :], qt[64:96, buf, :], rt[64:96, buf, :], ALU.add
                                        ).then_inc(sem["qr_ready"], 1)

                    def row_max(hh, h4, b):
                        dve.wait_ge(sem["s_mm"], h4 + b + 1)
                        bank, c = ps[:, 2 + b % 2, :], hh * 4 + b
                        own = bank[:, b * P:b * P + P]
                        step.step(dve, V.tensor_tensor(own, own, mask, ALU.add))
                        step.step(dve, V.reduce_max(small[:, 0, c:c + 1], bank[:, 0:(b + 1) * P], AXX))
                        V.tensor_scalar(small[:, 1, c:c + 1], small[:, 0, c:c + 1], -SCALE1, None, ALU.mult
                                        ).then_inc(sem["nmax_ready"], 1)

                    def normalise_out(hh, h):
                        hb, c = hh % 2, hh * 4
                        dve.wait_ge(sem["o_mm"], HEAD + h * 4 + 4)
                        step.step(dve, V.reciprocal(small[:, 3, c:c + 4], small[:, 2, c:c + 4]))
                        V.tensor_tensor(osb[:, :, hb * 64:hb * 64 + 64],
                                        ps[:, 6, 0:256].rearrange("p (b e) -> p b e", b=4),
                                        small[:, 3, c:c + 4].unsqueeze(2).to_broadcast([P, 4, 64]), ALU.mult
                                        ).then_inc(sem["o_ready"], 1)

                    def recurrence(p):
                        dve.wait_ge(sem["mu_ready"], p + 1)
                        step.step(dve, V.tensor_tensor(sx[:, :], sx[:, :], tile(rnn_in, p), ALU.mult))
                        step.step(dve, V.tensor_tensor(sx[:, :], sx[:, :], m2[:, :], ALU.mult))
                        step.step(dve, V.tensor_tensor_scan(sa[:, :], av[:, :], sx[:, :], 0.0, ALU.mult, ALU.add))
                        dve.wait_ge(sem["ga_sig"], p + 1)
                        step.step(dve, V.tensor_tensor(sa[:, :], sa[:, :], sig_a[:, :], ALU.mult))
                        V.tensor_tensor(tile(gate_r, p), tile(gate_r, p), sa[:, :], ALU.mult).then_inc(sem["rnn_done"], 1)

                    def tile(t, p):
                        return t[:, p, :] if isinstance(p, int) else chunk(t, p)[:, 0, :]

                    def merge(p):
                        dve.wait_ge(sem["y_mm"], p + 1)
                        dve.wait_ge(sem["gb_sig"], p + 1)
                        dve.wait_ge(sem["rnn_done"], HEAD + p + 1)
                        v = tmp[:, 0, :]
                        step.step(dve, V.tensor_tensor(v, tile(gate_b, p), ps[:, 7, :], ALU.mult))
                        step.step(dve, V.tensor_tensor(v, v, tile(gate_r, p), ALU.add))
                        split(v, tile(merged_h, p), tile(merged_l, p), "merged")

                    rotate_q(0, 0, 0)
                    row_max(0, 0, 0)
                    row_max(0, 0, 1)
                    rotate_q(1, 0, 1)

                    def four_heads(i, last):
                        for hh in range(4):
                            pp, hb, end = hh // 2, hh % 2, last and hh == 3
                            h4, h, p = i * 16 + hh * 4, i * 4 + hh, i * 2 + pp
                            if hb == 1:
                                recurrence(p)
                                if not end:
                                    rotate_q(h + 1, p + 1, 0)
                            row_max(hh, h4, 2)
                            row_max(hh, h4, 3)
                            if not end:
                                row_max((hh + 1) % 4, h4 + 4, 0)
                                row_max((hh + 1) % 4, h4 + 4, 1)
                            normalise_out(hh, h)
                            if hb == 0:
                                dve.wait_ge(sem["a_ready"], p * 2 + 2)
                                step.step(dve, V.tensor_tensor(m2[:, :], av[:, :], av[:, :], ALU.mult))
                                V.scalar_tensor_tensor(m2[:, :], m2[:, :], 1.0, th[:, :], ALU.add, ALU.mult
                                                       ).then_inc(sem["m2_ready"], 1)
                            else:
                                if not end:
                                    rotate_q(h + 2, p + 1, 1)
                                merge(p)

                    per = 4 * (2 + 8 + 1) + 2 * 1 + 2 * (4 + 3)
                    with dve.Fori(0, PAIRS // 2 - 1) as i:
                        step.enter(i, per)
                        four_heads(i, False)
                        step.leave(PAIRS // 2 - 1)
                    four_heads(PAIRS // 2 - 1, True)

                    def do(ins):
                        step.step(dve, ins)

                    def residual(u0, per_tile):
                        for m in range(C8):
                            residual_before(nc, do, sh, m)
                            dve.wait_ge(sem["unit_done"], SPLIT + u0 + (m + 1) * per_tile)
                            residual_chunk(nc, do, sh, m, ps[:, m % 4, :])
                            sum_chunk(dve, nc, do, sem, sh, m, stat)

                    residual(U_OUT, 1)
                    dve.wait_ge(sem["z_ready"], C8)
                    ln1[1](dve, nc)
                    with dve.Fori(0, FC // 4) as i:
                        step.enter(i, 4 * 5)
                        for j in range(4):
                            f = i * 4 + j
                            for half in range(2):
                                dve.wait_ge(sem["ff_tap"], f * 2 + half + 1)
                                for s in (1, 2):
                                    out = taps[:, j % 2, half, s:]
                                    ins = V.scalar_tensor_tensor(
                                        out, ps[:, 2 * j + half, 0:S - s], col("ffw", f + ((2 - s) * 2 * FC + half * FC)),
                                        out, ALU.mult, ALU.add)
                                    if half == 1 and s == 2:
                                        ins.then_inc(sem["ff_conv"], 1)
                                    else:
                                        step.step(dve, ins)
                            dve.wait_ge(sem["ff_gelu"], f + 1)
                            dve.wait_ge(sem["ff_conv"], f + 5)
                            v = taps[:, j % 2, 0:1, :]
                            step.step(dve, V.tensor_tensor(v, v, taps[:, j % 2, 1:2, :], ALU.mult))
                            split(v, chunk(hid_h, f), chunk(hid_l, f), "ff_done")
                        step.leave(FC // 4)
                    residual(U_DOWN, DOWN_PER)
                    dve.wait_ge(sem["z_ready"], 2 * C8)
                    ln2[1](dve, nc)

            nc.all_engine_barrier(sems_to_clear=sem_range)


HW, AW, PW = D // 4, D // 2, D // 4
AHEADS = 4
HYC, AC, PC = HW // P, AW // P, PW // P
LN_EPS = 1e-5
FH = 64
FEMB = 33
EXPERTS, GROUPS, DE = 16, 4, 256
EC = DE // P
PLE = 256
NF = S // P
HALF = EXPERTS // 2
EXP_UNITS = 2 * EC * HALF
DOWN_HALF = HALF * EC // 8
V_POOL = 0
V_HY = V_POOL + PC
V_QK = V_HY + 3 * HYC
V_V = V_QK + 2 * AC
V_DFT = V_V + AC
V_IDFT = V_DFT + NF
V_OUT = V_IDFT + NF
V_PLEG = V_OUT + C8
V_PLEP = V_PLEG + C8
V_EXP = [V_PLEP + 2, V_PLEP + 2 + EXP_UNITS + C8 * DOWN_HALF]
V_DOWN = [v + EXP_UNITS for v in V_EXP]
U2 = V_DOWN[1] + C8 * DOWN_HALF

PAR2, NPAR2 = columns([("hw", 9 * HYC), ("hb", 3 * HYC), ("fb1", 1), ("fr1", 1), ("fb2", 1), ("fr2", 1),
                       ("bias", HYC), ("lq1", 1), ("lq2", 1), ("lk1", 1), ("lk2", 1), ("lam0", 1), ("lam1", 1),
                       ("sub_g", 1), ("pool_b", PC), ("pool_s", PC), ("in_g", C8), ("in_b", C8), ("ln1_g", C8),
                       ("ln1_b", C8), ("ple_b", C8), ("rbias", 20), ("fw1", FH), ("fw2", FH), ("fw3", 2 * HW),
                       ("poolw", PC * P), ("router", C8 * 20)])
CST2, NCST2 = columns([("ident", P), ("perm", P), ("out_g", C8), ("out_b", C8)])
TAB, NTAB = columns([("z", S), ("win", 4 * HW), ("trig", 2 * S), ("icnt", PC * S)])
PADW = 8


def second_block(nc, mem, sh, d_cst, d_tab, d_w, first_unit, d_par, d_p, out):
    with ExitStack() as ctx:
        ps, z, xh, xl = sh.ps, sh.z, sh.xh, sh.xl
        at_ = mem.at
        pexp = at_("pexp", 64, [P, 2, 2, S])
        filt = at_("filt", 64, [P, 4, 2, HW])
        at = at_("at", 72, [P, 2, S])
        trig = at_("trig", 72, [P, 2, S])
        osb = at_("osb2", 76, [P, 2, 4, P])
        win = at_("win", 76, [P, 4, HW])
        hy = at_("hy", 80, [P, 3 * HYC, S])
        qk = at_("qk", 92, [P, 2 * AC, S])
        v4 = at_("v4", 108, [P, 4, AW])
        mix_h = at_("mix_h", 116, [P, C8, S], F32R)
        mix_l = at_("mix_l", 132, [P, C8, S], F32R)
        icnt = at_("icnt", 132, [P, PC, S])
        emb = at_("emb", 136, [P, S])
        rhs3_h = at_("rhs3_h", 148, [P, 4, 3 * HW], F32R)
        rhs3_l = at_("rhs3_l", 160, [P, 4, 3 * HW], F32R)
        ys_h = at_("ys_h", 148, [P, 2 * NF, HW], F32R)
        ytmp = at_("ytmp", 156, [P, NF, HW])
        ys_l = at_("ys_l", 160, [P, 2 * NF, HW], F32R)
        yfull = at_("yfull", 168, [P, NF, HW])
        pool = at_("pool", 172, [P, PC, S + 2 * PADW])
        pacc = at_("pacc", 176.25, [P, PC, S + 2 * PADW])
        pw = at_("pw", 180.5, [P, 2, S + 2 * PADW])
        spec = at_("spec", 172, [P, 8, S])
        act_h = at_("act_h", 80, [P, HALF * EC, S], F32R)
        act_l = at_("act_l", 112, [P, HALF * EC, S], F32R)
        pT = at_("pT", 144, [P, 2, S])
        pT_h = at_("pT_h", 148, [P, 2, S], F32R)
        pT_l = at_("pT_l", 152, [P, 2, S], F32R)
        gT = at_("gT", 156, [EXPERTS, S])
        gm = at_("gm", 158, [EXPERTS, 2, S])
        rtr = at_("rtr", 162, [P, 12, 4, 20])
        router_h = at_("router_h", 96, [P, C8, P], F32R)
        router_l = at_("router_l", 100, [P, C8, P], F32R)
        logits = at_("logits", 104, [20, S])
        stat = at_("stat2", 188, [P, 2, S])
        hid = at_("hid", 192, [P, 2, S])
        tmp = at_("tmp2", 196, [P, 2, S])
        par = at_("par2", 200, [P, NPAR2])
        cst = at_("cst2", 204.625, [P, NCST2])
        ones = at_("ones2", 205.75, [P, P])
        ones_d = at_("ones_d2", 206.25, [P, P])
        small = at_("small2", 206.75, [P, 2, 12])
        headv = at_("headv", 206.875, [P, 2, 12])
        lamt = at_("lamt", 207, [P, 8])
        eps = at_("eps2", 207.0625, [P, 3])

        names = (STREAM_SEMS + LN_SEMS + ["par_in2", "cst_in2", "tab_in", "trig_in", "p_in", "proj_evac2", "hy_tap",
                 "hy_ready", "hy_v", "f1_mm", "ang1", "sin1", "f2_mm", "ang2", "sin2", "filt_mm", "kf_win", "kf_done",
                 "sqk", "norm_mm", "norm_raw", "norm_std", "rot_mm", "qk_ready", "v_ready2", "pool_in", "pool_zero", "pool_step", "pool_y",
                 "poolm_mm", "pool_done", "vt_mm", "vt_hi", "vt_ready", "dft_mm", "spec_evac", "ys_ready",
                 "hy_done", "lam_prod", "lam_mm", "lam_exp", "s_mm2", "nmax2", "p_ready2", "a_ready2",
                 "t_mm2", "at_ready", "o_mm2", "o_sc", "o_sq", "o_std", "o_nrm", "ot_mm", "att_done", "dve_step2",
                 "router_ready", "logit_mm", "logits", "route_mm", "r_a", "r_ea", "r_b", "r_eb", "gates", "gt_mm", "gt_ready", "gm_ready",
                 "g_mm", "silu", "ex_done", "pg_sig", "pp_done", "pt_hi", "pt_lo", "down_evac", "stored"])
        sem, sem_range = sems(nc, ctx, names)

        def chunk(t, k):
            return t[:, k, :] if isinstance(k, int) else t[:, ds(k, 1), :]

        def col(name, k=0, n=1, rows=P):
            at_ = PAR2[name][0] + k
            return par[0:rows, at_:at_ + n]

        def con(name, k=0, n=None):
            at_, w = CST2[name]
            return cst[:, at_ + k:at_ + k + (w if n is None else n)]

        ident = con("ident")
        ln_in = layer_norm_engines(0, sem, sh, ones_d[:, :], eps[:, 0:1], eps[:, 2:3], par, PAR2["in_g"][0], PAR2["in_b"][0], stat)
        ln1 = layer_norm_engines(1, sem, sh, ones_d[:, :], eps[:, 0:1], eps[:, 2:3], par, PAR2["ln1_g"][0], PAR2["ln1_b"][0], stat)
        ln_out = layer_norm_engines(0, sem, sh, ones_d[:, :], eps[:, 0:1], eps[:, 2:3], cst, CST2["out_g"][0], CST2["out_b"][0], stat)

        with nc.Block() as block:
            @block.sync
            def _(sp):
                sp.dma_start(cst[:, :], d_cst).then_inc(sem["cst_in2"], 16)
                sp.wait_ge(sem["cst_in2"], 16)

            @block.gpsimd
            def _(g):
                nc.gpsimd.memset(ones[:, :], 1.0)
                nc.gpsimd.memset(eps[:, 0:1], LN_EPS)
                nc.gpsimd.memset(eps[:, 1:2], 1e-6)
                nc.gpsimd.memset(ones_d[:, :], 1.0 / D)

            @block.vector
            def _(dve):
                for m in range(C8):
                    if m:
                        dve.wait_ge(sem["z_ready"], m)
                    sum_chunk(dve, nc, None, sem, sh, m, stat)

        nc.all_engine_barrier(sems_to_clear=sem_range)

        with nc.Fori(0, DEPTH) as layer:
            with nc.Block() as block:
                @block.sync
                def _(sp):
                    sp.dma_start(par[:, :], d_par[ds(layer, 1)].rearrange("a p n -> p (a n)")).then_inc(sem["par_in2"], 16)

                    a, w = TAB["z"]
                    sp.dma_start(emb[:, :], d_tab[:, a:a + w]).then_inc(sem["tab_in"], 16)
                    a, w = TAB["icnt"]
                    sp.dma_start(icnt[:, :, :], d_tab[:, a:a + w].rearrange("p (a n) -> p a n", a=PC)).then_inc(sem["tab_in"], 16)
                    stream_units(sp, sem, sh.ring, d_w, layer * U2 + first_unit, U2)

                @block.gpsimd
                def _(g):
                    nc.gpsimd.memset(pool[:, :, :], 0.0).then_inc(sem["pool_zero"], 1)

                    step = Count(sem["pool_step"])

                    def spectra_product():
                        G = nc.gpsimd
                        g.wait_ge(sem["spec_evac"], 2 * NF)
                        kr, vr = spec[:, 0:NF, 0:HW], spec[:, 0:NF, HW:2 * HW]
                        vs, ks = spec[:, NF:2 * NF, 0:HW], spec[:, NF:2 * NF, HW:2 * HW]
                        y = yfull[:, :, :]
                        for part, (a, b, op) in enumerate(((kr, ks, ALU.subtract), (ks, kr, ALU.add))):
                            rows = slice(part * NF, part * NF + NF)
                            step.step(g, G.tensor_tensor(y, vr, a, ALU.mult))
                            step.step(g, G.tensor_tensor(ytmp[:, :, :], vs, b, ALU.mult))
                            step.step(g, G.tensor_tensor(y, y, ytmp[:, :, :], op))
                            step.step(g, G.tensor_scalar(ys_h[:, rows, :], y, 1.0, 0.0, ALU.mult, ALU.add))
                            G.tensor_tensor(ys_l[:, rows, :], y, ys_h[:, rows, :], ALU.subtract).then_inc(sem["ys_ready"], 1)
                            g.wait_ge(sem["ys_ready"], part + 1)

                    split_units(g, nc, sem, sh, U2, interlude=(V_IDFT + SPLIT, spectra_product))

                @block.tensor
                def _(pe):
                    T = nc.tensor

                    def unit(bank, n, parity, rh=xh, rl=xl, **kw):
                        unit_products(pe, nc, sem, sh, rh, rl, bank, n, parity, **kw)

                    def flat(w, n, half):
                        return w[:, n % 2, half * 4:half * 4 + 4, :].rearrange("p a b -> p (a b)")

                    pe.sem_inc(sem["g_mm"], HEAD)
                    pe.sem_inc(sem["unit_done"], SPLIT)
                    ln_in[0](pe, nc)
                    two_units(pe, nc, sem, sh, xh, xl, (ps[:, 6, :], ps[:, 7, :]), V_POOL, 0, 0)
                    for n in range(3 * HYC):
                        pe.wait_ge(sem["proj_evac2"], n + 1)
                        unit(ps[:, n % 4, :], V_HY + n, n % 2)
                        if n == 0:
                            pe.wait_ge(sem["par_in2"], 16)
                            pe.wait_ge(sem["tab_in"], 32)
                            pe.wait_ge(sem["pool_in"], PC)
                            T.matmul(ps[0:FH, 6, :], col("fw1", 0, FH, FEMB), emb[0:FEMB, :],
                                     start=True, stop=True).then_inc(sem["f1_mm"], 1)
                            pe.wait_ge(sem["lam_prod"], 1)
                            T.matmul(ps[:, 7, 0:2], ones[:, :], lamt[:, 0:2], start=True, stop=True).then_inc(sem["lam_mm"], 1)
                    q0 = 3 * HYC

                    def rotate(n):
                        pe.wait_ge(sem["proj_evac2"], 4 + q0 + n + 1)
                        if n >= 2:
                            pe.wait_ge(sem["qk_ready"], n - 1)
                        T.matmul(ps[:, 4 + n % 2, :], con("perm"), qk[:, n, :], start=True, stop=True
                                 ).then_inc(sem["rot_mm"], 1)

                    def filters(t):
                        if t >= 2:
                            pe.wait_ge(sem["kf_win"], t - 1)
                        T.matmul(ps[:, 6 + t % 2, :], hid[0:FH, 1, t * P:t * P + P], col("fw3", 0, 2 * HW, FH),
                                 start=True, stop=True).then_inc(sem["filt_mm"], 1)

                    for n in range(2 * AC):
                        pe.wait_ge(sem["proj_evac2"], q0 + n + 1)
                        unit(ps[:, (q0 + n) % 4, :], V_QK + n, n % 2)
                        if n == 0:
                            pe.wait_ge(sem["sin1"], 1)
                            pe.wait_ge(sem["lam_exp"], 1)
                            T.matmul(ps[0:FH, 7, :], col("fw2", 0, FH, FH), hid[0:FH, 0, :], start=True, stop=True
                                     ).then_inc(sem["f2_mm"], 1)
                        else:
                            rotate(n - 1)
                        if n == 5:
                            pe.wait_ge(sem["sin2"], 1)
                        if n >= 5:
                            filters(n - 5)
                    pe.wait_ge(sem["proj_evac2"], 4 + q0 + 2 * AC - 1)
                    for q in range(AC):
                        n = V_V + q
                        if q == 1:
                            rotate(2 * AC - 1)
                            filters(3)
                        if q == 0:
                            pe.wait_ge(sem["proj_evac2"], 4 + q0 + 2 * AC)
                        if q == 3:
                            pe.wait_ge(sem["hy_v"], HYC)
                            pe.wait_ge(sem["kf_win"], 4)
                            for c in range(HYC):
                                for t in range(4):
                                    mm = T.transpose(ps[:, 6 + c, t * P:t * P + P], hy[:, 4 + c, t * P:t * P + P], ident)
                                mm.then_inc(sem["vt_mm"], 1)
                        pe.wait_ge(sem["w_split"], n + 1)
                        for kk in range(2):
                            k = 2 * q + kk
                            for t in range(4):
                                tok = slice(t * P, t * P + P)
                                mm = three(nc, ps[:, t, :], xh[:, k, tok], xl[:, k, tok], flat(sh.wh, n, kk), flat(sh.wl, n, kk),
                                           k == 0, k == 7, skip_group_check=True)
                        mm.then_inc(sem["unit_done"], 1)
                    pe.wait_ge(sem["qk_ready"], 2 * AC)
                    for n in range(PC):
                        pe.wait_ge(sem["pool_y"], n + 1)
                        T.matmul(ps[:, 4 + n, :], col("poolw", n * P, P), pacc[:, n, 0:S], start=True, stop=True
                                 ).then_inc(sem["poolm_mm"], 1)
                    def spectra(n):
                        u = V_DFT + n // 2
                        if n % 2 == 0:
                            pe.wait_ge(sem["w_split"], u + 1)
                        if n:
                            pe.wait_ge(sem["spec_evac"], n)
                        cols = slice(0, 2 * HW) if n < NF else slice(HW, 3 * HW)
                        for t in range(4):
                            b_ = (n % 2) * 4 + t
                            mm = three(nc, ps[:, 7, :], sh.wh[:, u % 2, b_, :], sh.wl[:, u % 2, b_, :],
                                       rhs3_h[:, t, cols], rhs3_l[:, t, cols], t == 0, t == 3)
                        mm.then_inc(sem["dft_mm" if n % 2 == 0 else "unit_done"], 1)

                    def scores(n):
                        h, b = n // 4, n % 4
                        if n >= 2:
                            pe.wait_ge(sem["p_ready2"], 2 * (n - 1))
                        for c in range(2):
                            lo = slice(64 * c, 64 * c + 64)
                            T.matmul(ps[:, 2 * (n % 2) + c, :], qk[lo, h, b * P:b * P + P], qk[lo, AC + h, :],
                                     start=True, stop=True).then_inc(sem["s_mm2"], 1)

                    def turn(n):
                        pe.wait_ge(sem["a_ready2"], n + 1)
                        if n >= 2:
                            pe.wait_ge(sem["at_ready"], n - 1)
                        for j in range(4):
                            mm = T.transpose(ps[:, 4 + n % 2, j * P:j * P + P], pexp[:, n % 2, 0, j * P:j * P + P], ident)
                        mm.then_inc(sem["t_mm2"], 1)

                    def weigh(n):
                        h = n // 4
                        pe.wait_ge(sem["at_ready"], n + 1)
                        pe.wait_ge(sem["o_sc"], n)
                        for j in range(4):
                            mm = T.matmul(ps[:, 6, 0:P], at[:, n % 2, j * P:j * P + P], v4[:, j, h * P:h * P + P],
                                          start=(j == 0), stop=(j == 3))
                        mm.then_inc(sem["o_mm2"], 1)

                    def turn_out(h):
                        pe.wait_ge(sem["o_nrm"], h + 1)
                        pe.wait_ge(sem["att_done"], h)
                        pe.wait_ge(sem["spec_evac"], 2 * NF if h else 2 * NF - 1)
                        for b in range(4):
                            mm = T.transpose(ps[:, 7, b * P:b * P + P], osb[:, h % 2, b, :], ident)
                        mm.then_inc(sem["ot_mm"], 1)

                    pe.wait_ge(sem["v_ready2"], 4)
                    scores(0)
                    scores(1)
                    pe.wait_ge(sem["vt_ready"], HYC)
                    pe.wait_ge(sem["sqk"], 1)
                    for c in range(HYC):
                        for t in range(4):
                            for w in range(2):
                                mm = T.matmul(ps[:, 6, c:c + 1], filt[:, t, w, c * P:c * P + P], ones[:, 0:1],
                                              start=(t + w == 0), stop=(t == 3 and w == 1), skip_group_check=True)
                    mm.then_inc(sem["norm_mm"], 1)
                    pe.wait_ge(sem["pool_done"], PC)
                    pe.wait_ge(sem["norm_raw"], 1)
                    for n in range(4 * AHEADS):
                        turn(n)
                        if n + 2 < 4 * AHEADS:
                            scores(n + 2)
                        if n == 0:
                            pe.wait_ge(sem["kf_done"], 2)
                        if n < 2 * NF - 1:
                            spectra(n)
                        if n == 2 * NF + 1:
                            pe.wait_ge(sem["att_done"], 1)
                            spectra(2 * NF - 1)
                        if n:
                            weigh(n - 1)
                        if n >= 7 and n % 4 == 3:
                            turn_out((n - 7) // 4)
                    weigh(4 * AHEADS - 1)
                    pe.wait_ge(sem["ys_ready"], 2)
                    pe.wait_ge(sem["p_ready2"], 8 * AHEADS)
                    for q in range(NF):
                        n = V_IDFT + q
                        pe.wait_ge(sem["w_split"], n + 1)
                        for kk in range(2):
                            f = 2 * q + kk
                            for c in range(HYC):
                                ch = slice(c * P, c * P + P)
                                mm = three(nc, ps[:, c, :], ys_h[:, f, ch], ys_l[:, f, ch], flat(sh.wh, n, kk),
                                           flat(sh.wl, n, kk), f == 0, f == 7, skip_group_check=True)
                        mm.then_inc(sem["unit_done"], 1)
                    turn_out(AHEADS - 1)

                    last_ones = {**{c: ("hy_done", c + 1) for c in range(HYC)}, HYC + AHEADS - 1: ("att_done", AHEADS)}
                    mix_order = [6, 7, 2, 3, 4, 0, 1, 5]
                    for m in range(C8):
                        if m >= 4:
                            pe.wait_ge(sem["z_ready"], C8 + m - 3)
                        unit(ps[:, (m + 2) % 4, :], V_OUT + m, m % 2, mix_h, mix_l,
                             ready=last_ones if m == 0 else None, order=mix_order)
                    ln1[0](pe, nc)

                    two_units(pe, nc, sem, sh, xh, xl, (ps[:, 0, :], ps[:, 1, :]), V_PLEG, V_PLEG % 2, C8)
                    pe.wait_ge(sem["router_ready"], 1)
                    for k in range(C8):
                        mm = three(nc, ps[:, 6, :], router_h[:, k, :], router_l[:, k, :], xh[:, k, :], xl[:, k, :],
                                   k == 0, k == C8 - 1)
                    mm.then_inc(sem["logit_mm"], 1)
                    for m in range(2, C8):
                        if m >= 4:
                            pe.wait_ge(sem["pg_sig"], m - 3)
                        unit(ps[:, m % 4, :], V_PLEG + m, m % 2)
                        if m == 2:
                            pe.wait_ge(sem["logits"], 1)
                            for t in range(4):
                                mm = T.transpose(ps[:, 7, t * 20:t * 20 + 20], logits[:, t * P:t * P + P],
                                                 ident[0:20, 0:20])
                            mm.then_inc(sem["route_mm"], 1)
                    pe.wait_ge(sem["pt_lo"], 1)
                    for m in range(C8):
                        n = V_PLEP + m // 4
                        if m % 4 == 0:
                            pe.wait_ge(sem["w_split"], n + 1)
                        if m < 4:
                            pe.wait_ge(sem["pg_sig"], C8)
                        else:
                            pe.wait_ge(sem["pp_done"], m - 3)
                        for k in range(2):
                            b_ = (m % 4) * 2 + k
                            mm = three(nc, ps[:, m % 4, :], sh.wh[:, n % 2, b_, :], sh.wl[:, n % 2, b_, :],
                                       pT_h[:, k, :], pT_l[:, k, :], k == 0, k == 1)
                        mm.then_inc(sem["unit_done" if m % 4 == 3 else "dft_mm"], 1)
                    pe.wait_ge(sem["gates"], 1)
                    for t in range(4):
                        mm = T.transpose(ps[0:EXPERTS, 7, t * P:t * P + P], rtr[:, 11, t, 0:16], ident)
                    mm.then_inc(sem["gt_mm"], 1)
                    pe.wait_ge(sem["pp_done"], C8)
                    for part in range(2):
                        with pe.Fori(0, HALF // 2) as i:
                            for e in range(2):
                                for f in range(EC):
                                    pe.wait_ge(sem["ex_done"], i * 4 + (part * HALF * EC + 2 * e + f + 1))
                                    for half in range(2):
                                        unit(ps[:, 2 * f + half, :], i * 8 + (V_EXP[part] + 4 * e + 2 * f + half), half)
                                    if f == 0:
                                        pe.wait_ge(sem["gm_ready"], i * 2 + (part * HALF + e + 1))
                                        T.matmul(ps[:, 4 + e, :], ones[0:EXPERTS, :], gm[:, e, :], start=True, stop=True
                                                 ).then_inc(sem["g_mm"], 1)
                        with pe.Fori(0, C8 // 2) as i:
                            for m in range(2):
                                pe.wait_ge(sem["down_evac"], i * 2 + (part * C8 + m + 1))
                                for q in range(DOWN_HALF):
                                    if m == 0:
                                        pe.wait_ge(sem["ex_done"], part * HALF * EC + 2 + (q + 1) * 8)
                                    unit(ps[:, 6 + m, :], i * 2 * DOWN_HALF + (V_DOWN[part] + m * DOWN_HALF + q), q % 2,
                                         act_h[:, q * 8:q * 8 + 8, :], act_l[:, q * 8:q * 8 + 8, :],
                                         first=q == 0, last=q == DOWN_HALF - 1)

                @block.scalar
                def _(act):
                    A = nc.scalar.activation
                    act.sem_inc(sem["proj_evac2"], 4)
                    ln_in[2](act, nc, gains=(sem["par_in2"], 16))
                    act.wait_ge(sem["x_ready"], C8)
                    a, w = TAB["trig"]
                    act.dma_start(trig[:, :, :], d_tab[:, a:a + w].rearrange("p (a n) -> p a n", a=2)).then_inc(sem["trig_in"], 16)
                    a, w = TAB["win"]
                    act.dma_start(win[:, :, :], d_tab[:, a:a + w].rearrange("p (a n) -> p a n", a=4)).then_inc(sem["trig_in"], 16)

                    def hy_tile(u):
                        act.wait_ge(sem["unit_done"], SPLIT + V_HY + u + 1)
                        A(hy[:, u, :], ps[:, u % 4, :], ACT.Identity, scale=col("hw", 3 * HYC + u), bias=col("hb", u)
                          ).then_inc(sem["hy_tap"], 1)
                        act.wait_ge(sem["hy_ready"], u + 1)
                        act.sem_inc(sem["proj_evac2"], 1)

                    def filter_sin(n):
                        act.wait_ge(sem[f"ang{n + 1}"], 1)
                        A(hid[0:FH, n, :], hid[0:FH, n, :], ACT.Sin).then_inc(sem[f"sin{n + 1}"], 1)

                    act.wait_ge(sem["pool_zero"], 1)
                    for n in range(PC):
                        act.wait_ge(sem["unit_done"], SPLIT + V_POOL + n + 1)
                        A(pool[:, n, PADW:PADW + S], ps[:, 6 + n, :], ACT.Copy).then_inc(sem["pool_in"], 1)
                    for u in range(3 * HYC):
                        hy_tile(u)
                        if u == 1:
                            filter_sin(0)
                    act.wait_ge(sem["lam_mm"], 1)
                    A(lamt[:, 2:4], ps[:, 7, 0:2], ACT.Exp).then_inc(sem["lam_exp"], 1)
                    for n in range(2 * AC):
                        u = 3 * HYC + n
                        act.wait_ge(sem["unit_done"], SPLIT + V_QK + n + 1)
                        A(qk[:, n, :], ps[:, u % 4, :], ACT.Copy).then_inc(sem["proj_evac2"], 1)
                        if n == 4:
                            filter_sin(1)
                    for c in range(HYC):
                        act.wait_ge(sem["vt_mm"], c + 1)
                        A(rhs3_h[:, :, HW + c * P:HW + c * P + P], ps[:, 6 + c, :].rearrange("p (t e) -> p t e", e=P), ACT.Copy
                          ).then_inc(sem["vt_hi"], 1)
                    act.wait_ge(sem["unit_done"], SPLIT + V_DFT)
                    for t in range(4):
                        A(v4[:, t, :], ps[:, t, :], ACT.Copy).then_inc(sem["v_ready2"], 1)
                    act.wait_ge(sem["kf_done"], 2)
                    A(filt[:, :, :, :], filt[:, :, :, :], ACT.Square).then_inc(sem["sqk"], 1)

                    def spectra_out(n):
                        if n % 2:
                            act.wait_ge(sem["unit_done"], SPLIT + V_DFT + n // 2 + 1)
                        else:
                            act.wait_ge(sem["dft_mm"], n // 2 + 1)
                        A(spec[:, n, :], ps[:, 7, :], ACT.Copy).then_inc(sem["spec_evac"], 1)

                    act.wait_ge(sem["norm_mm"], 1)
                    A(lamt[:, 6:8], ps[:, 6, 0:2], ACT.Copy).then_inc(sem["norm_raw"], 1)

                    def expo(n):
                        for c in range(2):
                            act.wait_ge(sem["nmax2"], 2 * n + c + 1)
                            if n >= 2:
                                act.wait_ge(sem["t_mm2"], n - 1)
                            A(pexp[:, n % 2, c, :], ps[:, 2 * (n % 2) + c, :], ACT.Exp, scale=0.125,
                              bias=small[:, n % 2, 2 + c:3 + c], accum_out=small[:, n % 2, 4 + c:5 + c]
                              ).then_inc(sem["p_ready2"], 1)

                    def evac_at(n):
                        act.wait_ge(sem["t_mm2"], n + 1)
                        if n >= 2:
                            act.wait_ge(sem["o_mm2"], n - 1)
                        A(at[:, n % 2, :], ps[:, 4 + n % 2, :], ACT.Copy).then_inc(sem["at_ready"], 1)

                    def squares(n):
                        h, b = n // 4, n % 4
                        act.wait_ge(sem["o_sc"], n + 1)
                        A(hid[:, 0, 0:P], osb[:, h % 2, b, :], ACT.Square, accum_out=headv[:, h % 2, b:b + 1]
                          ).then_inc(sem["o_sq"], 1)
                        act.wait_ge(sem["o_sq"], n + 1)
                        if b == 3:
                            A(headv[:, h % 2, 4:8], headv[:, h % 2, 0:4], ACT.Sqrt, scale=1.0 / P, bias=eps[:, 0:1]
                              ).then_inc(sem["o_std"], 1)
                        if n == 3:
                            act.wait_ge(sem["norm_raw"], 1)
                            A(lamt[:, 6:8], lamt[:, 6:8], ACT.Sqrt, bias=eps[:, 1:2]).then_inc(sem["norm_std"], 1)

                    expo(0)
                    expo(1)
                    for n in range(4 * AHEADS):
                        evac_at(n)
                        if n + 2 < 4 * AHEADS:
                            expo(n + 2)
                        if n < 2 * NF - 1:
                            spectra_out(n)
                        if n == 2 * NF + 1:
                            spectra_out(2 * NF - 1)
                        if n >= 3:
                            squares(n - 3)
                    for n in range(4 * AHEADS - 3, 4 * AHEADS):
                        squares(n)
                    act.wait_ge(sem["unit_done"], SPLIT + V_PLEG)
                    act.dma_start(pT[:, :, :], d_p[ds(layer, 1)].rearrange("a p k t -> p (a k) t")).then_inc(sem["p_in"], 16)
                    ln1[2](act, nc)
                    act.wait_ge(sem["p_in"], 16)
                    A(pT_h[:, :, :], pT[:, :, :], ACT.Copy).then_inc(sem["pt_hi"], 1)

                    for m in range(C8):
                        act.wait_ge(sem["unit_done"], SPLIT + V_PLEG + m + 1)
                        A(spec[:, m, :], ps[:, m % 4, :], ACT.Sigmoid, bias=col("ple_b", m)).then_inc(sem["pg_sig"], 1)
                        if m == 1:
                            act.wait_ge(sem["logit_mm"], 1)
                            A(logits[:, :], ps[0:20, 6, :], ACT.Copy).then_inc(sem["logits"], 1)
                        if m == 6:
                            act.wait_ge(sem["r_a"], 1)
                            A(rtr[:, 1, :, 0:4], rtr[:, 1, :, 0:4], ACT.Exp).then_inc(sem["r_ea"], 1)
                            act.wait_ge(sem["r_b"], 1)
                            A(rtr[:, 6, :, 0:1], rtr[:, 6, :, 0:1], ACT.Exp).then_inc(sem["r_eb"], 1)
                    act.wait_ge(sem["gt_mm"], 1)
                    A(gT[:, :], ps[0:EXPERTS, 7, :], ACT.Copy).then_inc(sem["gt_ready"], 1)
                    for part in range(2):
                        with act.Fori(0, HALF // 2) as i:
                            for n in range(4):
                                f = n % 2
                                act.wait_ge(sem["ex_done"], i * 4 + (part * HALF * EC + n + 1))
                                act.wait_ge(sem["unit_done"], SPLIT + i * 8 + (V_EXP[part] + 2 * n + 1))
                                A(hid[:, f, :], ps[:, 2 * f, :], ACT.Silu).then_inc(sem["silu"], 1)

                @block.vector
                def _(dve):
                    V = nc.vector
                    step = Count(sem["dve_step2"])

                    def do(ins):
                        step.step(dve, ins)

                    def split(v, hi, lo, done=None):
                        do(V.tensor_scalar(hi, v, 1.0, None, ALU.mult))
                        ins = V.tensor_tensor(lo, v, hi, ALU.subtract)
                        if done:
                            ins.then_inc(sem[done], 1)
                        else:
                            do(ins)

                    dve.sem_inc(sem["ex_done"], 2)
                    dve.sem_inc(sem["down_evac"], 2)
                    dve.sem_inc(sem["z_ready"], C8)
                    ln_in[1](dve, nc)
                    dve.wait_ge(sem["par_in2"], 16)
                    V.tensor_tensor(lamt[:, 0:2], col("lq1", 0, 2), col("lk1", 0, 2), ALU.mult).then_inc(sem["lam_prod"], 1)

                    def angles(n, bank):
                        dve.wait_ge(sem[f"f{n + 1}_mm"], 1)
                        r, a, k = hid[0:FH, n, :], tmp[0:FH, 0, :], tmp[0:FH, 1, :]
                        do(V.tensor_scalar(a, ps[0:FH, bank, :], col(f"fb{n + 1}", 0, 1, FH), col(f"fr{n + 1}", 0, 1, FH),
                                           ALU.add, ALU.mult))
                        reduce_angle(dve, nc, step, r, a, k)
                        dve.sem_inc(sem[f"ang{n + 1}"], 1)

                    def hy_taps(u):
                        dve.wait_ge(sem["hy_tap"], u + 1)
                        bank = ps[:, u % 4, :]
                        do(V.scalar_tensor_tensor(hy[:, u, 1:], bank[:, 0:S - 1], col("hw", u), hy[:, u, 1:], ALU.mult, ALU.add))
                        V.scalar_tensor_tensor(hy[:, u, 0:S - 1], bank[:, 1:], col("hw", 6 * HYC + u), hy[:, u, 0:S - 1],
                                               ALU.mult, ALU.add).then_inc(sem["hy_ready"], 1)

                    def pooling(n):
                        dve.wait_ge(sem["pool_in"], n + 1)
                        src = pool[:, n, :]
                        cur, width, have, k = src, S + 2 * PADW, 1, 0
                        for half in range(2):
                            window = 2 ** (2 * n + half + 1)
                            while have < window:
                                out_, width = pw[:, k % 2, :], width - have
                                do(V.tensor_tensor(out_[:, 0:width], cur[:, 0:width], cur[:, have:have + width], ALU.add))
                                cur, have, k = out_, 2 * have, k + 1
                            lo = PADW - window // 2
                            rows = slice(64 * half, 64 * half + 64)
                            do(V.tensor_tensor(pacc[rows, n, 0:S], cur[rows, lo:lo + S], icnt[rows, n, :], ALU.mult))
                        V.tensor_tensor(pacc[:, n, 0:S], pacc[:, n, 0:S], src[:, PADW:PADW + S], ALU.subtract
                                        ).then_inc(sem["pool_y"], 1)

                    dve.wait_ge(sem["tab_in"], 32)
                    dve.wait_ge(sem["trig_in"], 32)
                    for u in range(3 * HYC):
                        hy_taps(u)
                        if u == 0:
                            angles(0, 6)
                        if u in (1, 3):
                            pooling(u // 2)
                    dve.wait_ge(sem["hy_ready"], 3 * HYC)
                    for c in range(HYC):
                        V.tensor_tensor(hy[:, 4 + c, :], hy[:, 4 + c, :], hy[:, 2 + c, :], ALU.mult).then_inc(sem["hy_v"], 1)
                    dve.wait_ge(sem["lam_exp"], 1)
                    do(V.tensor_tensor(lamt[:, 4:5], lamt[:, 3:4], lamt[:, 2:3], ALU.subtract))
                    do(V.tensor_scalar(lamt[:, 4:5], lamt[:, 4:5], col("lam0"), None, ALU.subtract))
                    do(V.tensor_scalar(lamt[:, 5:6], col("sub_g"), col("lam1"), None, ALU.mult))
                    angles(1, 7)
                    def window(t):
                        dve.wait_ge(sem["filt_mm"], t + 1)
                        do(V.tensor_tensor(filt[:, t, 0, :], ps[:, 6 + t % 2, 0:HW], win[:, t, :], ALU.mult))
                        V.tensor_tensor(filt[:, t, 1, :], ps[:, 6 + t % 2, HW:2 * HW], win[:, t, :], ALU.mult
                                        ).then_inc(sem["kf_win"], 1)

                    for n in range(2 * AC):
                        dve.wait_ge(sem["rot_mm"], n + 1)
                        do(V.tensor_tensor(tmp[:, n % 2, :], ps[:, 4 + n % 2, :], trig[:, 1, :], ALU.mult))
                        do(V.tensor_tensor(qk[:, n, :], qk[:, n, :], trig[:, 0, :], ALU.mult))
                        V.tensor_tensor(qk[:, n, :], qk[:, n, :], tmp[:, n % 2, :], ALU.add).then_inc(sem["qk_ready"], 1)
                        if n >= 4:
                            window(n - 4)
                    dve.wait_ge(sem["qk_ready"], 2 * AC)
                    dve.wait_ge(sem["kf_win"], 4)
                    do(V.memset(filt[0:1, 0, 1, :], 0.0))
                    v = tmp[:, :, :].rearrange("p a (b c) -> p (a b) c", c=HW)
                    for w, op in ((0, ALU.add), (2, ALU.subtract)):
                        cols = slice(w * HW, w * HW + HW)
                        do(V.tensor_tensor(v, filt[:, :, 0, :], filt[:, :, 1, :], op))
                        split(v, rhs3_h[:, :, cols], rhs3_l[:, :, cols], "kf_done")
                        dve.wait_ge(sem["kf_done"], w // 2 + 1)
                    for c in range(HYC):
                        dve.wait_ge(sem["vt_hi"], c + 1)
                        cols = slice(HW + c * P, HW + c * P + P)
                        V.tensor_tensor(rhs3_l[:, :, cols], ps[:, 6 + c, :].rearrange("p (t e) -> p t e", e=P), rhs3_h[:, :, cols],
                                        ALU.subtract).then_inc(sem["vt_ready"], 1)

                    for n in range(PC):
                        dve.wait_ge(sem["poolm_mm"], n + 1)
                        do(V.tensor_scalar(tmp[:, n, :], ps[:, 4 + n, :], col("pool_b", n), col("pool_s", n), ALU.add, ALU.mult))
                        split(tmp[:, n, :], mix_h[:, HYC + AC + n, :], mix_l[:, HYC + AC + n, :], "pool_done")

                    def row_max(n):
                        for c in range(2):
                            dve.wait_ge(sem["s_mm2"], 2 * n + c + 1)
                            sm = small[:, n % 2, :]
                            do(V.reduce_max(sm[:, c:c + 1], ps[:, 2 * (n % 2) + c, :], AXX))
                            V.tensor_scalar(sm[:, 2 + c:3 + c], sm[:, c:c + 1], -0.125, None, ALU.mult).then_inc(sem["nmax2"], 1)

                    def difference(n):
                        dve.wait_ge(sem["p_ready2"], 2 * n + 2)
                        sm = small[:, n % 2, :]
                        do(V.reciprocal(sm[:, 6:8], sm[:, 4:6]))
                        do(V.tensor_scalar(sm[:, 8:9], sm[:, 7:8], sm[:, 4:5], lamt[:, 4:5], ALU.mult, ALU.mult))
                        do(V.tensor_copy(headv[:, n // 4 % 2, 8 + n % 4:9 + n % 4], sm[:, 6:7]))
                        V.scalar_tensor_tensor(pexp[:, n % 2, 0, :], pexp[:, n % 2, 1, :], sm[:, 8:9], pexp[:, n % 2, 0, :],
                                               ALU.mult, ALU.add).then_inc(sem["a_ready2"], 1)

                    def scale_out(n):
                        h, b = n // 4, n % 4
                        dve.wait_ge(sem["o_mm2"], n + 1)
                        V.tensor_scalar(osb[:, h % 2, b, :], ps[:, 6, 0:P], headv[:, h % 2, 8 + b:9 + b], None, ALU.mult
                                        ).then_inc(sem["o_sc"], 1)

                    def norm_out(h):
                        dve.wait_ge(sem["o_std"], h + 1)
                        do(V.reciprocal(headv[:, h % 2, 4:8], headv[:, h % 2, 4:8]))
                        V.tensor_tensor(osb[:, h % 2, :, :], osb[:, h % 2, :, :],
                                        headv[:, h % 2, 4:8].unsqueeze(2).to_broadcast([P, 4, P]), ALU.mult
                                        ).then_inc(sem["o_nrm"], 1)

                    def att_out(h):
                        dve.wait_ge(sem["ot_mm"], h + 1)
                        do(V.tensor_scalar(tmp[:, h % 2, :], ps[:, 7, :], lamt[:, 5:6], None, ALU.mult))
                        split(tmp[:, h % 2, :], mix_h[:, HYC + h, :], mix_l[:, HYC + h, :], "att_done")

                    row_max(0)
                    row_max(1)
                    difference(0)
                    for n in range(4 * AHEADS):
                        if n + 1 < 4 * AHEADS:
                            difference(n + 1)
                        if n + 2 < 4 * AHEADS:
                            row_max(n + 2)
                        if n >= 2:
                            scale_out(n - 2)
                        if n >= 6 and n % 4 == 2:
                            norm_out((n - 6) // 4)
                        if n >= 8 and n % 4 == 0:
                            att_out((n - 8) // 4)
                        if n == 15:
                            dve.wait_ge(sem["norm_std"], 1)
                            do(V.reciprocal(lamt[:, 6:8], lamt[:, 6:8]))
                    att_out(AHEADS - 2)
                    scale_out(4 * AHEADS - 2)
                    scale_out(4 * AHEADS - 1)
                    norm_out(AHEADS - 1)
                    dve.wait_ge(sem["att_done"], AHEADS - 1)
                    dve.wait_ge(sem["unit_done"], SPLIT + V_OUT)
                    for c in range(HYC):
                        do(V.tensor_scalar(tmp[:, c, :], hy[:, 4 + c, :], col("bias", c), None, ALU.mult))
                        do(V.scalar_tensor_tensor(tmp[:, c, :], ps[:, c, :], lamt[:, 6 + c:7 + c], tmp[:, c, :], ALU.mult, ALU.add))
                        do(V.tensor_tensor(tmp[:, c, :], tmp[:, c, :], hy[:, c, :], ALU.mult))
                        split(tmp[:, c, :], mix_h[:, c, :], mix_l[:, c, :], "hy_done")
                    dve.wait_ge(sem["hy_done"], HYC)
                    att_out(AHEADS - 1)
                    do(V.memset(router_h[:, :, :].bitcast(F32), 0.0))
                    do(V.memset(router_l[:, :, :].bitcast(F32), 0.0))
                    split(col("router", 0, C8 * 20).rearrange("p (k n) -> p k n", n=20), router_h[:, :, 0:20],
                          router_l[:, :, 0:20], "router_ready")

                    for m in range(C8):
                        residual_before(nc, do, sh, m)
                        dve.wait_ge(sem["unit_done"], SPLIT + V_OUT + m + 1)
                        residual_chunk(nc, do, sh, m, ps[:, (m + 2) % 4, :])
                        if m:
                            dve.wait_ge(sem["z_ready"], C8 + m)
                        sum_chunk(dve, nc, do, sem, sh, m, stat)
                    dve.wait_ge(sem["z_ready"], 2 * C8)
                    ln1[1](dve, nc)

                    dve.wait_ge(sem["pt_hi"], 1)
                    V.tensor_tensor(pT_l[:, :, :], pT[:, :, :], pT_h[:, :, :], ALU.subtract).then_inc(sem["pt_lo"], 1)
                    R = [rtr[:, n, :, :] for n in range(12)]

                    def bc(a, n):
                        return a.to_broadcast([P, 4, n])

                    def first_max(src, n, mx, oh):
                        do(V.reduce_max(mx, src, AXX))
                        do(V.tensor_tensor(oh, src, bc(mx, n), ALU.is_equal))
                        for j in range(n):
                            if j:
                                do(V.tensor_tensor(oh[:, :, j:j + 1], oh[:, :, j:j + 1], R[10][:, :, 4:5], ALU.is_gt))
                                do(V.tensor_tensor(R[10][:, :, 4:5], R[10][:, :, 4:5], oh[:, :, j:j + 1], ALU.add))
                            else:
                                do(V.tensor_copy(R[10][:, :, 4:5], oh[:, :, 0:1]))

                    dve.wait_ge(sem["route_mm"], 1)
                    rb = col("rbias", 0, 20).unsqueeze(1).to_broadcast([P, 4, 20])
                    do(V.tensor_tensor(R[0], ps[:, 7, 0:80].rearrange("p (t n) -> p t n", n=20), rb, ALU.add))
                    gl, fl = R[0][:, :, 0:4], R[0][:, :, 4:20]
                    ohg = R[2][:, :, 0:4]
                    first_max(gl, 4, R[2][:, :, 4:5], ohg)
                    V.tensor_tensor(R[1][:, :, 0:4], gl, bc(R[2][:, :, 4:5], 4), ALU.subtract).then_inc(sem["r_a"], 1)
                    for gidx in range(GROUPS):
                        do(V.tensor_tensor(R[3][:, :, 4 * gidx:4 * gidx + 4], fl[:, :, 4 * gidx:4 * gidx + 4],
                                           bc(ohg[:, :, gidx:gidx + 1], 4), ALU.mult))
                    fs = R[4][:, :, 0:4]
                    do(V.tensor_tensor(fs, R[3][:, :, 0:4], R[3][:, :, 4:8], ALU.add))
                    do(V.tensor_tensor(fs, fs, R[3][:, :, 8:12], ALU.add))
                    do(V.tensor_tensor(fs, fs, R[3][:, :, 12:16], ALU.add))
                    m1, oh1 = R[4][:, :, 8:9], R[5][:, :, 0:4]
                    first_max(fs, 4, m1, oh1)
                    fs2 = R[5][:, :, 4:8]
                    do(V.scalar_tensor_tensor(fs2, oh1, -1e30, fs, ALU.mult, ALU.add))
                    m2_, oh2 = R[5][:, :, 12:13], R[5][:, :, 8:12]
                    first_max(fs2, 4, m2_, oh2)
                    V.tensor_tensor(R[6][:, :, 0:1], m2_, m1, ALU.subtract).then_inc(sem["r_b"], 1)
                    dve.wait_ge(sem["r_ea"], 1)
                    do(V.reduce_sum(R[7][:, :, 0:1], R[1][:, :, 0:4], AXX))
                    dve.wait_ge(sem["r_eb"], 1)
                    do(V.tensor_scalar(R[7][:, :, 1:2], R[6][:, :, 0:1], 1.0, None, ALU.add))
                    do(V.tensor_tensor(R[7][:, :, 2:3], R[7][:, :, 1:2], R[7][:, :, 0:1], ALU.mult))
                    do(V.reciprocal(R[7][:, :, 3:4], R[7][:, :, 2:3]))
                    do(V.tensor_tensor(R[7][:, :, 4:5], R[7][:, :, 3:4], R[6][:, :, 0:1], ALU.mult))
                    do(V.tensor_tensor(oh1, oh1, bc(R[7][:, :, 3:4], 4), ALU.mult))
                    do(V.tensor_tensor(oh2, oh2, bc(R[7][:, :, 4:5], 4), ALU.mult))
                    do(V.tensor_tensor(oh1, oh1, oh2, ALU.add))
                    for gidx in range(GROUPS):
                        ins = V.tensor_tensor(R[11][:, :, 4 * gidx:4 * gidx + 4], oh1, bc(ohg[:, :, gidx:gidx + 1], 4), ALU.mult)
                        if gidx < GROUPS - 1:
                            do(ins)
                        else:
                            ins.then_inc(sem["gates"], 1)
                    for m in range(C8):
                        if m % 4 == 3:
                            dve.wait_ge(sem["unit_done"], SPLIT + V_PLEP + m // 4 + 1)
                        else:
                            dve.wait_ge(sem["dft_mm"], NF + m // 4 * 3 + m % 4 + 1)
                        V.tensor_tensor(spec[:, m, :], spec[:, m, :], ps[:, m % 4, :], ALU.mult).then_inc(sem["pp_done"], 1)
                    dve.wait_ge(sem["gt_ready"], 1)

                    def mask_gate(e, slot):
                        one = cst[0:EXPERTS, e:e + 1] if isinstance(e, int) else cst[0:EXPERTS, ds(e, 1)]
                        V.tensor_scalar(gm[:, slot, :], gT[:, :], one, None, ALU.mult).then_inc(sem["gm_ready"], 1)

                    for part in range(2):
                        e0 = part * HALF
                        with dve.Fori(0, HALF // 2) as i:
                            step.enter(i, 4 * 3)
                            for n in range(4):
                                e, f = n // 2, n % 2
                                if n == 0:
                                    dve.wait_ge(sem["g_mm"], HEAD + i * 2 + e0)
                                    mask_gate(i * 2 + e0, 0)
                                    mask_gate(i * 2 + (e0 + 1), 1)
                                dve.wait_ge(sem["silu"], i * 4 + (e0 * EC + n + 1))
                                dve.wait_ge(sem["unit_done"], SPLIT + i * 8 + (V_EXP[part] + 2 * n + 2))
                                h = hid[:, f, :]
                                do(V.tensor_tensor(h, h, ps[:, 2 * f + 1, :], ALU.mult))
                                dve.wait_ge(sem["g_mm"], HEAD + i * 2 + (e0 + e + 1))
                                do(V.tensor_tensor(h, h, ps[:, 4 + e, :], ALU.mult))
                                do(V.tensor_scalar(act_h[:, ds(i * 4 + n, 1), :], hid[:, f:f + 1, :], 1.0, None, ALU.mult))
                                V.tensor_tensor(act_l[:, ds(i * 4 + n, 1), :], hid[:, f:f + 1, :], act_h[:, ds(i * 4 + n, 1), :],
                                                ALU.subtract).then_inc(sem["ex_done"], 1)
                            step.leave(HALF // 2)
                        for m in range(C8):
                            dve.wait_ge(sem["unit_done"], SPLIT + V_DOWN[part] + DOWN_HALF * (m + 1))
                            zm, bank = z[:, m, :], ps[:, 6 + m % 2, :]
                            if part == 0:
                                V.scalar_tensor_tensor(zm, zm, ALPHA, bank, ALU.mult, ALU.add).then_inc(sem["down_evac"], 1)
                                dve.wait_ge(sem["down_evac"], 2 + m + 1)
                                do(V.tensor_tensor(zm, zm, spec[:, m, :], ALU.add))
                            else:
                                V.tensor_tensor(zm, zm, bank, ALU.add).then_inc(sem["down_evac"], 1)
                                dve.wait_ge(sem["down_evac"], 2 + C8 + m + 1)
                                if m:
                                    dve.wait_ge(sem["z_ready"], 2 * C8 + m)
                                sum_chunk(dve, nc, do, sem, sh, m, stat)

            nc.all_engine_barrier(sems_to_clear=sem_range)

        with nc.Block() as block:
            @block.sync
            def _(sp):
                for k in range(C8):
                    sp.wait_ge(sem["xa_ready"], k + 1)
                    sp.dma_start(out[:, k, :], z[:, k, :]).then_inc(sem["stored"], 16)
                sp.wait_ge(sem["stored"], 16 * C8)

            @block.tensor
            def _(pe):
                ln_out[0](pe, nc)

            @block.scalar
            def _(act):
                ln_out[2](act, nc)

            @block.vector
            def _(dve):
                dve.sem_inc(sem["z_ready"], C8)
                ln_out[1](dve, nc)


def build(nc, d, out):
    with ExitStack() as ctx:
        ps = ctx.enter_context(nc.psum_tensor("ps", [P, 8, S], F32))
        mem = Memory(nc)
        sh = Shared(nc, mem, ps)
        first_block(nc, mem, sh, d["x"], d["pos"], d["cst"], d["w"], d["gw"], d["par1"])
        second_block(nc, mem, sh, d["cst2"], d["tab"], d["w"], DEPTH * U1, d["par2"], d["p"], out)


def _blocks(w):
    k, m = w.shape
    return w.reshape(k // P, P, m // P, P).transpose(2, 1, 0, 3)


def _units(w):
    b = _blocks(w)
    m, p, k, n = b.shape
    return b.reshape(m, p, k // 8, 8 * n).transpose(0, 2, 1, 3).reshape(m * (k // 8), p, 8 * n)


def _cols(v):
    return np.asarray(v).reshape(-1, P).T


def _swap(w):
    h = w.shape[-1] // 2
    return np.concatenate([w[..., h:], w[..., :h]], -1)


def _first_layout(a):
    out = {}
    w1, gw, par = [], [], []
    for l in range(DEPTH):
        w_in = a["w_in"][l]
        q0 = 2 * D
        kv0 = q0 + QC * P
        r0 = kv0 + KVC * P
        ga0 = r0 + ROPE
        gb0 = ga0 + D
        wr = w_in[:, r0:ga0]
        tile = np.concatenate([np.zeros((D, 64), np.float32), wr, _swap(wr)], 1)
        order = [w_in[:, kv0:r0], tile, w_in[:, q0:kv0], w_in[:, 0:D], w_in[:, D:2 * D]]
        gate_a, gate_b = _units(w_in[:, ga0:gb0]), _units(w_in[:, gb0:])
        w1.append(_units(np.concatenate(order, 1)))
        uq = a["w_uq"][l].reshape(QC, P, HEADS, NOPE + ROPE)
        uq = np.concatenate([uq, _swap(uq[..., NOPE:])], -1)
        ukv = a["w_ukv"][l].reshape(KVC, P, HEADS, NOPE + VH)
        w1.append(ukv[..., NOPE:].reshape(KVC, P, HEADS * VH))
        for p in range(PAIRS):
            bl = [uq[c, :, 2 * p + h] for h in range(2) for c in range(QC)]
            bl += [ukv[c, :, 2 * p:2 * p + 2, :NOPE].reshape(P, P) for c in range(KVC)]
            w1 += [gate_b[p:p + 1], np.concatenate(bl, 1)[None], gate_a[p:p + 1]]
            tile = np.zeros((P, 2, P), np.float32)
            for n, g in enumerate(("gx_w", "ga_w")):
                tile[:64, n, :64], tile[64:, n, 64:] = a[g][l][2 * p], a[g][l][2 * p + 1]
            gw.append(tile.reshape(P, 2 * P))
        w1.append(_units(a["w_out"][l]))
        up = _units(a["w_up"][l]).reshape(2, FC, P, 1024).transpose(1, 0, 2, 3).reshape(2 * FC, P, 1024)
        w1 += [up, _units(a["w_down"][l])]
        par.append(np.concatenate([_cols(a[n][l]) for n in (
            "conv_w", "conv_b", "gx_b", "ga_b", "lru_lambda", "q_norm_g", "kv_norm_g", "ln1_g", "ln1_b", "ln2_g",
            "ln2_b", "ffn_conv_w", "ffn_conv_b")], 1))
    out["w"] = w1
    out["gw"] = np.stack(gw)
    out["par1"] = np.stack(par)
    out["x"] = np.asarray(a["x"])[0].T.reshape(C8, P, S).transpose(1, 0, 2)
    out["pos"] = np.repeat(np.asarray(a["positions"]).reshape(1, S), P, 0)
    cst = np.zeros((P, NCST), np.float32)
    cst[:, :P] = np.eye(P)
    cst[:, P:2 * P] = np.where(np.arange(P)[None, :] > np.arange(P)[:, None], -1e30, 0.0)
    half = ROPE // 2
    cst[:, 2 * P] = 10000.0 ** (-np.arange(P) % half * 0.0 - (np.arange(P) % half) * 2.0 / ROPE)
    cst[:, 2 * P + 1] = np.where((np.arange(P) >= 96) & (np.arange(P) < 96 + half), -1.0, 1.0)
    out["cst"] = cst
    return out


def _rows(v, rows=P):
    v = np.asarray(v, np.float32)
    v = v.reshape(v.shape[0], -1)
    return np.concatenate([v, np.zeros((P - v.shape[0], v.shape[1]), np.float32)], 0)


def _wide_units(w):
    return w.reshape(-1, 2, P, S).transpose(0, 2, 1, 3).reshape(-1, P, 2 * S)


def _tables():
    t = np.arange(S)
    f = np.arange(S) + 0.5
    ang = 2 * np.pi * np.outer(t, f) / (2 * S)
    fwd = np.concatenate([np.cos(ang), np.sin(ang)], 1)
    b = fwd.reshape(4, P, 2 * NF, P).transpose(2, 1, 0, 3)
    dft = b.reshape(NF, 2, P, 4 * P).transpose(0, 2, 1, 3).reshape(NF, P, 8 * P)
    idft = _wide_units(np.concatenate([np.cos(ang).T, np.sin(ang).T], 0) / S)
    cst = {}
    cst["ident"] = np.eye(P)
    perm = np.zeros((P, P))
    rd = 64 // 4
    cos, sin = np.ones((P, S)), np.zeros((P, S))
    inv = (500000.0 ** (-np.arange(0, rd, 2) / rd)).astype(np.float32)
    a = (t.astype(np.float32)[None, :] * inv[:, None]).astype(np.float64)
    for c in (0, 64):
        for i in range(rd // 2):
            perm[c + i + rd // 2, c + i] = -1.0
            perm[c + i, c + i + rd // 2] = 1.0
            for r in (c + i, c + i + rd // 2):
                cos[r], sin[r] = np.cos(a[i]), np.sin(a[i])
    cst["perm"], cst["trig"] = perm, np.concatenate([cos, sin], 1)
    tt = np.linspace(0.0, 1.0, S, dtype=np.float32)
    wp = (np.float32(2 * np.pi) * t.astype(np.float32) / np.float32(S)).astype(np.float32)
    bands = np.linspace(1e-4, (FEMB - 1) // 2 - 1, (FEMB - 1) // 2, dtype=np.float32)
    za = (wp[:, None] * bands[None, :]).astype(np.float64)
    cst["z"] = _rows(np.concatenate([tt[:, None], np.cos(za), -np.sin(za)], 1).T)
    deltas = np.linspace(np.log(1e-2) / 1.5, np.log(1e-2) / 0.3, HW)
    win = np.exp(-tt.astype(np.float64)[:, None] * np.abs(deltas)[None, :])
    cst["win"] = win.reshape(4, P, HW).transpose(1, 0, 2).reshape(P, 4 * HW)
    icnt = np.zeros((P, PC, S))
    for g, w in enumerate((2, 4, 8, 16)):
        lo, hi = np.clip(t - w // 2, 0, S - 1), np.clip(t + w // 2 - 1, 0, S - 1)
        icnt[64 * (g % 2):64 * (g % 2) + 64, g // 2] = 1.0 / (hi - lo + 1)
    cst["icnt"] = icnt.reshape(P, PC * S)
    return dft, idft, cst


def _second_layout(a):
    out = {}
    dft, idft, cst = _tables()
    cst["out_g"], cst["out_b"] = _cols(a["ln2_g_2"][DEPTH - 1]), _cols(a["ln2_b_2"][DEPTH - 1])
    out["tab"] = np.concatenate([cst[n] for n in TAB], 1).astype(np.float32)
    out["cst2"] = np.concatenate([cst[n] for n in CST2], 1).astype(np.float32)
    w2, par = [], []
    for l in range(DEPTH):
        w_in = a["w_in_2"][l]
        q0 = 3 * HW
        v0 = q0 + 2 * AW
        p0 = v0 + AW
        w2 += [_units(w_in[:, p0:]), _units(w_in[:, :v0]), _wide_units(w_in[:, v0:p0]),
               dft.astype(np.float32), idft.astype(np.float32), _units(a["w_out_2"][l]), _units(a["ple_wg_2"][l])]
        b = _blocks(a["ple_wp_2"][l])
        w2.append(b.reshape(2, 4, P, 2 * P).transpose(0, 2, 1, 3).reshape(2, P, 8 * P))
        ex = [np.stack([_units(a[n][l][e]) for n in ("moe_w1_2", "moe_w3_2")], 1).reshape(2 * EC, P, 8 * P)
              for e in range(EXPERTS)]
        for e in (0, HALF):
            w2 += ex[e:e + HALF] + [_units(a["moe_w2_2"][l][e:e + HALF].reshape(HALF * DE, D))]
        lam0 = 0.8 - 0.6 * np.exp(-0.3 * l)
        full = lambda v: np.full((P, 1), v, np.float32)
        pw = []
        for n in range(PC):
            m = np.zeros((P, P), np.float32)
            m[:64, :64], m[64:, 64:] = a["pool_w_2"][l][2 * n], a["pool_w_2"][l][2 * n + 1]
            pw.append(m)
        router = np.concatenate([a["moe_wgc_2"][l], a["moe_wgf_2"][l]], 1)
        parts = {
            "hw": _cols(a["hy_conv_w_2"][l]), "hb": _cols(a["hy_conv_b_2"][l]),
            "fb1": _rows(a["hy_fb1_2"][l]), "fr1": _rows(a["hy_freq1_2"][l]),
            "fb2": _rows(a["hy_fb2_2"][l]), "fr2": _rows(a["hy_freq2_2"][l]),
            "bias": _cols(a["hy_bias_2"][l]),
            "lq1": _rows(a["att_lq1_2"][l]), "lq2": _rows(a["att_lq2_2"][l]),
            "lk1": _rows(a["att_lk1_2"][l]), "lk2": _rows(a["att_lk2_2"][l]),
            "lam0": full(lam0), "lam1": full(1.0 - lam0), "sub_g": _cols(a["att_subln_g_2"][l]),
            "pool_b": _cols(a["pool_b_2"][l]), "pool_s": _cols(a["pool_scale_2"][l]),
            "ln1_g": _cols(a["ln1_g_2"][l]), "ln1_b": _cols(a["ln1_b_2"][l]),
            "in_g": _cols(a["ln2_g_2"][l - 1] if l else a["ln0_g_2"]),
            "in_b": _cols(a["ln2_b_2"][l - 1] if l else a["ln0_b_2"]), "ple_b": _cols(a["ple_bg_2"][l]),
            "rbias": np.repeat(np.concatenate([a["moe_bgc_2"][l], a["moe_bgf_2"][l]])[None], P, 0),
            "fw1": _rows(a["hy_fw1_2"][l]), "fw2": _rows(a["hy_fw2_2"][l]), "fw3": _rows(a["hy_fw3_2"][l]),
            "poolw": np.concatenate(pw, 1),
            "router": router.reshape(C8, P, 20).transpose(1, 0, 2).reshape(P, C8 * 20),
        }
        par.append(np.concatenate([parts[n] for n in PAR2], 1))
    out["w"] = w2
    out["par2"] = np.stack(par)
    out["p"] = a["p_2"][:, 0].transpose(0, 2, 1).reshape(DEPTH, 2, P, S).transpose(0, 2, 1, 3)
    return out


def _layout(inputs):
    a = {k: np.asarray(v) for k, v in inputs.items()}
    first, second = _first_layout(a), _second_layout(a)
    out = {**first, **second}
    out["w"] = np.concatenate(first["w"] + second["w"] + [np.zeros((RAW, P, 8 * P), np.float32)], 0)
    return {k: np.ascontiguousarray(v) for k, v in out.items()}


def kernel(**inputs):
    import concourse.bacc as bacc
    from concourse.bass_utils import run_bass_kernel_spmd

    nc = bacc.Bacc("TRN2", target_bir_lowering=False, num_devices=1)
    arrays = _layout(inputs)
    d = {k: nc.dram_tensor("in_" + k, v.shape, mybir.dt.from_np(v.dtype), kind="ExternalInput").ap()
         for k, v in arrays.items()}
    out = nc.dram_tensor("out", (P, C8, S), F32, kind="ExternalOutput").ap()
    build(nc, d, out)
    r = run_bass_kernel_spmd(nc, [{"in_" + k: v for k, v in arrays.items()}], core_ids=[0])
    y = r.results[0]["out"]
    return np.ascontiguousarray(y.transpose(1, 0, 2).reshape(D, S).T).reshape(1, S, D)
```
